# Optimizing a Trainium2 kernel written in Bass

```python
import jax
import jax.numpy as jnp
from jax import lax
import numpy as np

D_MODEL = 1024
BATCH = 1
SEQ = 256
DEPTH = 2

BRANCH_W = D_MODEL // 2
N_BRANCH = 3
SB_HDIM = 64
SB_HEADS = BRANCH_W // SB_HDIM
SB_QBLOCK = 128
MB_HDIM = 64
MB_HEADS = BRANCH_W // MB_HDIM
MB_BLOCK = 256
MB_TOPK = 3
MB_QCHUNK = 16
ROPE_THETA = 500000.0
ROPE_DIM = MB_HDIM // 4
ML_HEADS = 4
ML_HDIM = BRANCH_W // ML_HEADS
ML_CHUNK = 64
CONV_W = 4
N_GROUPS = 4
EXPERTS_PER_GROUP = 8
N_EXPERTS = N_GROUPS * EXPERTS_PER_GROUP
EXPERT_TOPK = 2
D_EXPERT = D_MODEL // 4
RMS_EPS = 1e-6
P_IN = 10 * BRANCH_W + 2 * ML_HEADS + N_BRANCH * D_MODEL

kernel_name = "hybrid_sb_moba_mlstm_hmoe"

def rms_norm(x, g):
    xf = x.astype(jnp.float32)
    y = xf * lax.rsqrt(jnp.mean(xf * xf, axis=-1, keepdims=True) + RMS_EPS)
    return (y * g.astype(jnp.float32)).astype(x.dtype)

def split_heads(t, n_heads):
    b, s, _ = t.shape
    return t.reshape(b, s, n_heads, -1).transpose(0, 2, 1, 3)

def merge_heads(t):
    b, h, s, d = t.shape
    return t.transpose(0, 2, 1, 3).reshape(b, s, h * d)

def rotary_partial(x, positions):
    half = ROPE_DIM // 2
    inv_freq = jnp.power(jnp.float32(ROPE_THETA), -jnp.arange(half, dtype=jnp.float32) / half)
    ang = positions.astype(jnp.float32)[:, None, :, None] * inv_freq
    cos, sin = jnp.cos(ang), jnp.sin(ang)
    xr = x[..., :ROPE_DIM].astype(jnp.float32)
    x1, x2 = xr[..., :half], xr[..., half:]
    rot = jnp.concatenate([x1 * cos - x2 * sin, x1 * sin + x2 * cos], axis=-1).astype(x.dtype)
    return jnp.concatenate([rot, x[..., ROPE_DIM:]], axis=-1)

def causal_depthwise_conv(u, w):
    c = u.shape[-1]
    return lax.conv_general_dilated(
        u, w[:, None, :].astype(u.dtype), window_strides=(1,),
        padding=[(CONV_W - 1, 0)], dimension_numbers=("NWC", "WIO", "NWC"),
        feature_group_count=c)

def stick_breaking_attention(q, k, v):
    b, h, s, d = q.shape
    nq = s // SB_QBLOCK
    scale = d ** -0.5
    kpos = jnp.arange(s)
    qb = q.reshape(b, h, nq, SB_QBLOCK, d).transpose(2, 0, 1, 3, 4)

    def block(args):
        qi, iblk = args
        qpos = iblk * SB_QBLOCK + jnp.arange(SB_QBLOCK)
        z = jnp.einsum("bhqd,bhkd->bhqk", qi, k).astype(jnp.float32) * scale
        past = kpos[None, :] < qpos[:, None]
        log_rem = jnp.where(past, jax.nn.log_sigmoid(-z), 0.0)
        after = lax.cumsum(log_rem, axis=3, reverse=True) - log_rem
        w = jnp.where(past, jnp.exp(jax.nn.log_sigmoid(z) + after), 0.0)
        return jnp.einsum("bhqk,bhkd->bhqd", w.astype(v.dtype), v)

    out = lax.map(block, (qb, jnp.arange(nq)))
    return out.transpose(1, 2, 0, 3, 4).reshape(b, h, s, d)

def moba_attention(q, k, v):
    b, h, s, d = q.shape
    nb = -(-s // MB_BLOCK)
    sp = nb * MB_BLOCK
    pad = ((0, 0), (0, 0), (0, sp - s), (0, 0))
    kb = jnp.pad(k, pad).reshape(b, h, nb, MB_BLOCK, d)
    vb = jnp.pad(v, pad).reshape(b, h, nb, MB_BLOCK, d)
    kmean = jnp.mean(kb.astype(jnp.float32), axis=3)
    topk = min(MB_TOPK, nb - 1)
    scale = d ** -0.5
    nc = s // MB_QCHUNK
    qc = q.reshape(b, h, nc, MB_QCHUNK, d).transpose(2, 0, 1, 3, 4)
    bi = jnp.arange(b)[:, None, None, None]
    hi = jnp.arange(h)[None, :, None, None]
    blk_ids = jnp.arange(nb)

    def chunk(args):
        qi, ci = args
        qpos = ci * MB_QCHUNK + jnp.arange(MB_QCHUNK)
        own = (ci * MB_QCHUNK) // MB_BLOCK
        k_own = lax.dynamic_index_in_dim(kb, own, axis=2, keepdims=False)
        v_own = lax.dynamic_index_in_dim(vb, own, axis=2, keepdims=False)
        kpos_own = own * MB_BLOCK + jnp.arange(MB_BLOCK)
        s_own = jnp.einsum("bhqd,bhkd->bhqk", qi, k_own).astype(jnp.float32) * scale
        s_own = jnp.where(kpos_own[None, :] <= qpos[:, None], s_own, -jnp.inf)
        if topk == 0:
            p = jax.nn.softmax(s_own, axis=-1).astype(v.dtype)
            return jnp.einsum("bhqk,bhkd->bhqd", p, v_own)
        gate = jnp.einsum("bhqd,bhnd->bhqn", qi.astype(jnp.float32), kmean)
        gate = jnp.where(blk_ids < own, gate, -jnp.inf)
        _, idx = lax.top_k(gate, topk)
        valid = idx < own
        k_sel = kb[bi, hi, idx]
        v_sel = vb[bi, hi, idx]
        s_sel = jnp.einsum("bhqd,bhqnkd->bhqnk", qi, k_sel).astype(jnp.float32) * scale
        s_sel = jnp.where(valid[..., None], s_sel, -jnp.inf)
        s_all = jnp.concatenate([s_own, s_sel.reshape(b, h, MB_QCHUNK, topk * MB_BLOCK)], axis=-1)
        p = jax.nn.softmax(s_all, axis=-1).astype(v.dtype)
        p_own = p[..., :MB_BLOCK]
        p_sel = p[..., MB_BLOCK:].reshape(b, h, MB_QCHUNK, topk, MB_BLOCK)
        return (jnp.einsum("bhqk,bhkd->bhqd", p_own, v_own)
                + jnp.einsum("bhqnk,bhqnkd->bhqd", p_sel, v_sel))

    out = lax.map(chunk, (qc, jnp.arange(nc)))
    return out.transpose(1, 2, 0, 3, 4).reshape(b, h, s, d)

def mlstm_chunkwise(q, k, v, log_i, log_f):
    b, h, s, d = q.shape
    L = ML_CHUNK
    nc = s // L
    k = k * d ** -0.5

    def to_chunks(a):
        return jnp.moveaxis(a.reshape(b, h, nc, L, *a.shape[3:]), 2, 0)

    causal = jnp.tril(jnp.ones((L, L), dtype=bool))

    def step(carry, inp):
        C, n, m = carry
        qc, kc, vc, li, lf = inp
        qf, kf, vf = qc.astype(jnp.float32), kc.astype(jnp.float32), vc.astype(jnp.float32)
        bcum = jnp.cumsum(lf, axis=-1)
        dmat = bcum[..., :, None] - bcum[..., None, :] + li[..., None, :]
        dmat = jnp.where(causal, dmat, -jnp.inf)
        inter = bcum + m[..., None]
        m_t = jnp.maximum(inter, jnp.max(dmat, axis=-1))
        w_intra = jnp.exp(dmat - m_t[..., None])
        w_inter = jnp.exp(inter - m_t)
        sc = jnp.einsum("bhtd,bhsd->bhts", qf, kf) * w_intra
        num = (jnp.einsum("bhts,bhse->bhte", sc, vf)
               + w_inter[..., None] * jnp.einsum("bhed,bhtd->bhte", C, qf))
        den = jnp.sum(sc, axis=-1) + w_inter * jnp.einsum("bhd,bhtd->bht", n, qf)
        out = num / jnp.maximum(jnp.abs(den), jnp.exp(-m_t))[..., None]
        m_new = m_t[..., -1]
        decay = jnp.exp(bcum[..., -1] + m - m_new)
        w_k = jnp.exp(bcum[..., -1:] - bcum + li - m_new[..., None])
        C_new = decay[..., None, None] * C + jnp.einsum("bhs,bhse,bhsd->bhed", w_k, vf, kf)
        n_new = decay[..., None] * n + jnp.einsum("bhs,bhsd->bhd", w_k, kf)
        return (C_new, n_new, m_new), out

    init = (jnp.zeros((b, h, d, d), jnp.float32), jnp.zeros((b, h, d), jnp.float32),
            jnp.zeros((b, h), jnp.float32))
    _, hs = lax.scan(step, init, (to_chunks(q), to_chunks(k), to_chunks(v),
                                  to_chunks(log_i), to_chunks(log_f)))
    return jnp.moveaxis(hs, 0, 2).reshape(b, h, s, d).astype(v.dtype)

def mixer_block(x, positions, norm_g, w_in, qn_g, kn_g, conv_w, ml_gate_b, w_branch, w_out):
    W = BRANCH_W
    bsz, s, _ = x.shape
    xn = rms_norm(x, norm_g)
    proj = xn @ w_in
    sb = proj[..., 0:3 * W]
    mb = proj[..., 3 * W:6 * W]
    ml_qk = proj[..., 6 * W:8 * W]
    ml_v = proj[..., 8 * W:9 * W]
    ml_o = proj[..., 9 * W:10 * W]
    ml_if = proj[..., 10 * W:10 * W + 2 * ML_HEADS]
    gate_logits = proj[..., 10 * W + 2 * ML_HEADS:]

    q, k, v = (split_heads(t, SB_HEADS) for t in jnp.split(sb, 3, axis=-1))
    y_sb = merge_heads(stick_breaking_attention(q, k, v))

    q, k, v = (split_heads(t, MB_HEADS) for t in jnp.split(mb, 3, axis=-1))
    q = rotary_partial(rms_norm(q, qn_g), positions)
    k = rotary_partial(rms_norm(k, kn_g), positions)
    y_mb = merge_heads(moba_attention(q, k, v))

    qk = jax.nn.silu(causal_depthwise_conv(ml_qk, conv_w))
    q = split_heads(qk[..., :W], ML_HEADS)
    k = split_heads(qk[..., W:], ML_HEADS)
    v = split_heads(ml_v, ML_HEADS)
    if_pre = ml_if.astype(jnp.float32) + ml_gate_b.astype(jnp.float32)
    log_i = if_pre[..., :ML_HEADS].transpose(0, 2, 1)
    log_f = jax.nn.log_sigmoid(if_pre[..., ML_HEADS:]).transpose(0, 2, 1)
    y_ml = merge_heads(mlstm_chunkwise(q, k, v, log_i, log_f)) * jax.nn.sigmoid(ml_o)

    branches = jnp.stack([y_sb, y_mb, y_ml], axis=0)
    y = jnp.einsum("nbsw,nwd->nbsd", branches, w_branch)
    gates = jax.nn.sigmoid(gate_logits.reshape(bsz, s, N_BRANCH, D_MODEL))
    merged = jnp.einsum("bsnd,nbsd->bsd", gates, y)
    return x + merged @ w_out

def hier_moe_block(x, norm_g, w_rg, b_rg, w_re, b_re, w1, w3, w2):
    bsz, s, d = x.shape
    n_tok = bsz * s
    xn = rms_norm(x, norm_g).reshape(n_tok, d)
    g_prob = jax.nn.softmax((xn @ w_rg).astype(jnp.float32) + b_rg, axis=-1)
    g_w, g_idx = lax.top_k(g_prob, 1)
    e_logits = ((xn @ w_re).astype(jnp.float32) + b_re).reshape(n_tok, N_GROUPS, EXPERTS_PER_GROUP)
    e_in = jnp.take_along_axis(e_logits, g_idx[:, :, None], axis=1)[:, 0]
    e_w, e_idx = lax.top_k(jax.nn.softmax(e_in, axis=-1), EXPERT_TOPK)
    e_w = e_w / jnp.sum(e_w, axis=-1, keepdims=True) * g_w
    flat_idx = g_idx * EXPERTS_PER_GROUP + e_idx
    combine = jnp.zeros((n_tok, N_EXPERTS), jnp.float32).at[
        jnp.arange(n_tok)[:, None], flat_idx].add(e_w)
    hid = jax.nn.silu(jnp.einsum("nd,edf->nef", xn, w1)) * jnp.einsum("nd,edf->nef", xn, w3)
    hid = hid * combine.astype(hid.dtype)[:, :, None]
    y = jnp.einsum("nef,efd->nd", hid, w2)
    return x + y.reshape(bsz, s, d)

def setup_inputs(seed: int = 0) -> dict:
    key = jax.random.key(seed)
    ks = jax.random.split(key, 20)

    def nrm(k, shape, scale):
        return jax.random.normal(k, shape, jnp.float32) * scale

    x = nrm(ks[0], (BATCH, SEQ, D_MODEL), 1.0)
    start = jax.random.randint(ks[1], (BATCH,), 0, 4096, dtype=jnp.int32)
    positions = (start[:, None] + jnp.arange(SEQ, dtype=jnp.int32)[None, :]).astype(jnp.int32)
    norm1_g = 1.0 + nrm(ks[2], (DEPTH, D_MODEL), 0.02)
    w_in = nrm(ks[3], (DEPTH, D_MODEL, P_IN), D_MODEL ** -0.5)
    qn_g = 1.0 + nrm(ks[4], (DEPTH, MB_HDIM), 0.02)
    kn_g = 1.0 + nrm(ks[5], (DEPTH, MB_HDIM), 0.02)
    conv_w = nrm(ks[6], (DEPTH, CONV_W, 2 * BRANCH_W), CONV_W ** -0.5)
    i_bias = nrm(ks[7], (DEPTH, ML_HEADS), 0.1)
    f_bias = jnp.linspace(3.0, 6.0, ML_HEADS, dtype=jnp.float32)[None, :] + nrm(ks[8], (DEPTH, ML_HEADS), 0.1)
    ml_gate_b = jnp.concatenate([i_bias, f_bias], axis=-1)
    w_branch = nrm(ks[9], (DEPTH, N_BRANCH, BRANCH_W, D_MODEL), BRANCH_W ** -0.5)
    w_out = nrm(ks[10], (DEPTH, D_MODEL, D_MODEL), D_MODEL ** -0.5)
    norm2_g = 1.0 + nrm(ks[11], (DEPTH, D_MODEL), 0.02)
    w_rg = nrm(ks[12], (DEPTH, D_MODEL, N_GROUPS), D_MODEL ** -0.5)
    b_rg = nrm(ks[13], (DEPTH, N_GROUPS), 0.01)
    w_re = nrm(ks[14], (DEPTH, D_MODEL, N_EXPERTS), D_MODEL ** -0.5)
    b_re = nrm(ks[15], (DEPTH, N_EXPERTS), 0.01)
    w1 = nrm(ks[16], (DEPTH, N_EXPERTS, D_MODEL, D_EXPERT), D_MODEL ** -0.5)
    w3 = nrm(ks[17], (DEPTH, N_EXPERTS, D_MODEL, D_EXPERT), D_MODEL ** -0.5)
    w2 = nrm(ks[18], (DEPTH, N_EXPERTS, D_EXPERT, D_MODEL), D_EXPERT ** -0.5)
    return {"x": x, "positions": positions, "norm1_g": norm1_g, "w_in": w_in,
            "qn_g": qn_g, "kn_g": kn_g, "conv_w": conv_w, "ml_gate_b": ml_gate_b,
            "w_branch": w_branch, "w_out": w_out, "norm2_g": norm2_g,
            "w_rg": w_rg, "b_rg": b_rg, "w_re": w_re, "b_re": b_re,
            "w1": w1, "w3": w3, "w2": w2}

def reference(x, positions, norm1_g, w_in, qn_g, kn_g, conv_w, ml_gate_b, w_branch, w_out,
              norm2_g, w_rg, b_rg, w_re, b_re, w1, w3, w2):
    for l in range(DEPTH):
        x = mixer_block(x, positions, norm1_g[l], w_in[l], qn_g[l], kn_g[l], conv_w[l],
                        ml_gate_b[l], w_branch[l], w_out[l])
        x = hier_moe_block(x, norm2_g[l], w_rg[l], b_rg[l], w_re[l], b_re[l],
                           w1[l], w3[l], w2[l])
    return x


_drawn_inputs = setup_inputs


def setup_inputs(seed=0):
    import zlib

    import numpy as np

    out = dict(_drawn_inputs(seed))
    spreads = {}
    factors = {'qn_g': 3.537, 'kn_g': 6.375, 'b_rg': 8.0, 'b_re': 6.714}
    for name, (base, spread) in spreads.items():
        noise = np.random.default_rng([zlib.crc32(name.encode()), seed]).standard_normal(out[name].shape)
        drawn = base * np.exp(spread * noise) if base else spread * noise
        out[name] = jnp.asarray(drawn.astype(out[name].dtype))
    for name, factor in factors.items():
        out[name] = (out[name] * factor).astype(out[name].dtype)
    return out
```

```python
from contextlib import ExitStack

import numpy as np
import concourse.bass as bass
from concourse import mybir

ALU = mybir.AluOpType
ACT = mybir.ActivationFunctionType
AX = mybir.AxisListType
F32 = mybir.dt.float32
F32R = mybir.dt.float32r
I32 = mybir.dt.int32

P = 128
SEQ, D = 256, 1024
DEPTH = 2
NT = SEQ // P
NK = D // P
W = D // 2
NC = W // P
HD = 64
HEADS = W // HD
ML_HEADS = 4
ML_HD = W // ML_HEADS
ROT = HD // 8
THETA = 500000.0
EPS = 1e-6
NEG = -1e30
NG, NE, FE = 4, 32, D // 4
EPG = NE // NG
CHUNK = 512
RING = 4
COL_IF = 10 * W
COL_GATE = COL_IF + 2 * ML_HEADS

SLOTS = 64
BATCH = 8
UNIT = 2048
URING = RING * NK * CHUNK // UNIT
SPLITS = 3


def bc(ap, axis, count):
    shape = list(ap.shape)
    shape.insert(axis, count)
    return ap.unsqueeze(axis).broadcast_to(shape)


class Chain:

    def __init__(self, eng, sem):
        self.eng, self.sem, self.n = eng, sem, 0

    def after(self, ins):
        self.n += 1
        ins.then_inc(self.sem, 1)
        self.eng.wait_ge(self.sem, self.n)


class Phase:

    def __init__(self, nc, tag):
        self.nc, self.tag, self.sems, self.ctx = nc, tag, [], ExitStack()

    def sem(self, name):
        s = self.ctx.enter_context(self.nc.semaphore(f"{self.tag}_{name}"))
        self.sems.append(s)
        return s

    def end(self):
        for s in self.sems:
            self.nc.sync.sem_clear(s)
        self.nc.all_engine_barrier()
        self.ctx.close()


def setup_constants(nc, t, d):
    ph = Phase(nc, "setup")
    loaded, raw, made, chain = ph.sem("x_loaded"), ph.sem("filled"), ph.sem("masks_made"), ph.sem("dve_chain")
    slot_ints, trig_ready, ang_ready = ph.sem("slot_ints"), ph.sem("trig_ready"), ph.sem("angles_ready")
    pos_in = ph.sem("positions_loaded")
    with nc.Block() as block:
        @block.sync
        def _(sp):
            sp.dma_start(t.x[:, :, :], d.x[0].rearrange("(t p) n -> p t n", p=P)).then_inc(loaded, 16)
            sp.dma_start(t.pos_i[:, :], d.positions[0].rearrange("(t p) -> p t", p=P), allow_slow_non_contiguous=True).then_inc(pos_in, 16)
            sp.wait_ge(loaded, 16)

        @block.gpsimd
        def _(pool):
            fills = [(t.ident, 0.0), (t.trineg, -1.0), (t.tri, 1.0), (t.tri_strict, 1.0), (t.neg_mask, 0.0),
                     (t.ones, 1.0), (t.negones, -1.0), (t.eps, EPS)]
            for buf, v in fills:
                nc.gpsimd.memset(buf[:, :], v).then_inc(raw, 1)
            nc.gpsimd.iota(t.slot_i[:, :], pattern=[[1, SLOTS]], base=0, channel_multiplier=0).then_inc(slot_ints, 1)
            pool.wait_ge(raw, len(fills))
            for buf, cmp, row, part, fill in [
                    (t.ident, ALU.not_equal, -1, 1, 1.0),
                    (t.trineg, ALU.is_ge, -1, 1, 0.0),
                    (t.tri, ALU.is_ge, 1, -1, 0.0),
                    (t.tri_strict, ALU.is_gt, 1, -1, 0.0),
                    (t.neg_mask, ALU.is_ge, -1, 1, NEG)]:
                nc.gpsimd.affine_select(out=buf[:, :], in_=buf[:, :], compare_op=cmp, fill=fill, base=0,
                                        pattern=[[row, P]], channel_multiplier=part).then_inc(made, 1)

        @block.vector
        def _(dve):
            ch = Chain(dve, chain)
            v = nc.vector
            dve.wait_ge(slot_ints, 1)
            v.tensor_copy(t.slot[:, :], t.slot_i[:, :])
            dve.wait_ge(made, 5)
            v.tensor_tensor(t.fold[:, :], t.ident[:, 0:SLOTS], t.ident[:, SLOTS:2 * SLOTS], ALU.add)
            for i in range(ROT):
                f = float(np.power(np.float32(THETA), np.float32(-i) / np.float32(ROT)))
                v.memset(t.freq[:, i:i + 1], f)
            dve.wait_ge(pos_in, 16)
            ch.after(v.tensor_copy(t.pos[:, :], t.pos_i[:, :]))
            ch.after(v.tensor_tensor(t.ang[:, :, :], bc(t.pos[:, :], 2, ROT), bc(t.freq[:, :], 1, NT), ALU.mult))
            two_pi = 2.0 * np.pi
            c1 = 6.28125
            c2 = float(np.float32(np.round((two_pi - c1) * 2.0 ** 20) / 2.0 ** 20))
            c3 = float(np.float32(two_pi - c1 - c2))
            big = float(1.5 * 2 ** 23)
            ch.after(v.tensor_scalar(t.turn[:, :, :], t.ang[:, :, :], 1.0 / two_pi, big, ALU.mult, ALU.add))
            ch.after(v.tensor_scalar(t.turn[:, :, :], t.turn[:, :, :], -big, None, ALU.add))
            for c in (c1, c2, c3):
                ch.after(v.scalar_tensor_tensor(out=t.ang[:, :, :], in0=t.turn[:, :, :], scalar=-c,
                                                in1=t.ang[:, :, :], op0=ALU.mult, op1=ALU.add))
            ch.after(v.tensor_scalar(t.turn[:, :, :], t.ang[:, :, :], np.pi / 2, -two_pi, ALU.is_gt, ALU.mult))
            ch.after(v.scalar_tensor_tensor(out=t.turn[:, :, :], in0=t.ang[:, :, :], scalar=np.pi / 2,
                                            in1=t.turn[:, :, :], op0=ALU.add, op1=ALU.add))
            lim = 3.1415925
            for buf in (t.ang, t.turn):
                v.tensor_scalar(buf[:, :, :], buf[:, :, :], lim, -lim, ALU.min, ALU.max).then_inc(ang_ready, 1)
            dve.wait_ge(ang_ready, 2)

        @block.scalar
        def _(act):
            act.wait_ge(ang_ready, 2)
            nc.scalar.activation(t.sin[:, :, :], t.ang[:, :, :], ACT.Sin).then_inc(trig_ready, 1)
            nc.scalar.activation(t.cos[:, :, :], t.turn[:, :, :], ACT.Sin).then_inc(trig_ready, 1)
            act.wait_ge(trig_ready, 2)
    ph.end()



def mixer(nc, t, d, l):
    ph = Phase(nc, "mix")
    mem = ExitStack()
    S = ph.sem

    def sb(name, shape, dt=F32):
        return mem.enter_context(nc.sbuf_tensor(name, shape, dt))

    xs = sb("mix_scaled_x", [P, NT, D])
    xnT = sb("mix_xnT", [P, NK, SEQ])
    sbq, sbk, sbv = sb("sb_qT", [P, NC, SEQ]), sb("sb_kT", [P, NC, SEQ]), sb("sb_v", [P, NT, W])
    mbqk = sb("mb_qk", [P, 2, NT, W])
    mbqkT, mbv = sb("mb_qkT", [P, 2, NC, SEQ]), sb("mb_v", [P, NT, W])
    mlpre = sb("ml_pre", [P, 2 * NC, SEQ + 3])
    mlqk, mlv = sb("ml_qk", [P, 2 * NC, SEQ]), sb("ml_v", [P, NT, W])
    gates = sb("gates", [P, NC + 3 * NK, SEQ])
    brT = sb("branchT", [P, 3, NC, SEQ])
    ta, tb, tw = sb("attn_a", [P, 4, 384]), sb("attn_b", [P, 4, 384]), sb("attn_w", [P, 4, 384])
    gain, convw, convr = sb("gain1", [P, NK]), sb("conv_w", [P, 4 * 2 * NC]), sb("conv_rows", [4 * 2 * NC, P])
    qkg, mlb, wif = sb("qk_gain", [P, 2, HD]), sb("ml_bias", [P, 2 * ML_HEADS]), sb("w_if", [P, NK, 2 * ML_HEADS])
    ms, rs = sb("mean_sq", [P, NT]), sb("rstd", [P, NT])
    hss, hrs = sb("head_sq", [P, 2, NT * HEADS]), sb("head_rstd", [P, 2, NT * HEADS])
    r4 = sb("rot_tmp", [P, 4, NT, HEADS, ROT])
    mxb, nmx, sums, rsum = (sb(n, [P, 4, 2]) for n in ("row_max", "neg_max", "row_sum", "inv_sum"))
    iff, lf, lft, Fc, av = (sb(n, [P, NT, ML_HEADS * k]) for n, k in
                            (("if_pre", 2), ("log_f", 1), ("log_f_tmp", 1), ("F_cum", 1), ("a_row", 1)))
    flo, den, dneg = (sb(n, [P, 4, 2]) for n in ("floor", "den", "den_neg"))
    ring = t.ring

    smalls, xs_ready, xT_done, xnT_ready = S("small_loads"), S("xs_ready"), S("xT_done"), S("xnT_ready")
    slot_in = [S(f"weights_in{i}") for i in range(RING)]
    weights_used, proj_done, proj_copied = S("weights_used"), S("proj_done"), S("proj_copied")
    sq_done, rstd_ready = S("sum_sq_done"), S("rstd_ready")
    cw_t, cw_ready = S("convw_transposed"), S("convw_ready")
    conv_done, silu_done, pads = S("conv_done"), S("silu_done"), S("pads_zeroed")
    sb_z, sb_ln, sb_sp, sb_spm, sb_c, sb_w, sb_wm, sb_o, sb_e = (S(n) for n in (
        "sb_scores", "sb_log1p", "sb_softplus", "sb_softplus_masked", "sb_exponent", "sb_w",
        "sb_w_masked", "sb_out", "sb_out_copied"))
    mb_sq, mb_ss, mb_rs, mb_rot, mb_t, mb_tc = (S(n) for n in (
        "mb_squares", "mb_sums", "mb_rstd", "mb_rotated", "mb_transposed", "mb_T_copied"))
    mb_s, mb_m, mb_exp, mb_p, mb_pt, mb_w, mb_o, mb_e = (S(n) for n in (
        "mb_scores", "mb_max", "mb_exp", "mb_probs", "mb_probsT", "mb_probsT_copied", "mb_out", "mb_out_copied"))
    if_b, if_sp, lf_r, f_done, f_ready, abc, abc_used, d_ready, w_ready, fl_in, fl_ready = (S(n) for n in (
        "if_biased", "if_softplus", "log_f_ready", "F_done", "a_diag_ready", "a_rows", "a_rows_used", "d_ready",
        "w_ready", "floor_in", "floor_ready"))
    ml_s, ml_p, ml_pt, ml_w, ml_o, ml_e, sig = (S(n) for n in (
        "ml_scores", "ml_probs", "ml_probsT", "ml_probsT_copied", "ml_out", "ml_out_ready", "gates_ready"))
    merged, out_done, x_added = S("merged"), S("out_done"), S("x_added")
    dch, ach = S("dve_chain"), S("act_chain")

    psP, psA = t.ps_a, t.ps_b

    chunks = [("sbq", 0), ("sbk", W), ("sbv", 2 * W), ("if", COL_IF), ("mlq", 6 * W), ("mlk", 7 * W),
              ("mbq", 3 * W), ("mbk", 4 * W), ("mlv", 8 * W), ("mbv", 5 * W), ("mlo", 9 * W)]
    chunks += [(f"g{i}", COL_GATE + i * CHUNK) for i in range(3 * D // CHUNK)]
    index = {name: i for i, (name, _) in enumerate(chunks)}
    big = [(n, c) for n, c in chunks if n != "if"]
    stream = [("in", c) for _, c in big] + [("branch", b) for b in range(3)] + [("out", n) for n in range(2)]
    place = {n: i for i, (n, _) in enumerate(big)}
    first_branch, first_out = len(big), len(big) + 3
    token_major = {"sbv", "mlv", "mbv", "mbq", "mbk", "if"}
    w_in_l = d.w_in[bass.ds(l, 1)].rearrange("l (p k) n -> p (l k) n", p=P)
    w_br_l = d.w_branch[bass.ds(l, 1)].rearrange("l b (c p) n -> p (l b) c n", p=P)
    w_out_l = d.w_out[bass.ds(l, 1)].rearrange("l (j p) n -> p (l j) n", p=P)

    def slot_view(i, kind="in"):
        v = ring[:, i % RING, :]
        return v.rearrange("p (k n) -> p k n", k=NC if kind == "branch" else NK)

    def arrived(eng, i):
        eng.wait_ge(slot_in[i % RING], 16 * (i // RING + 1))

    SMALL = 7

    with nc.Block() as block:
        @block.sync
        def _(sp):
            for i, (kind, c) in enumerate(stream):
                if i >= RING:
                    sp.wait_ge(weights_used, i - RING + 1)
                src = {"in": lambda: w_in_l[:, :, c:c + CHUNK], "branch": lambda: w_br_l[:, c],
                       "out": lambda: w_out_l[:, :, c * CHUNK:(c + 1) * CHUNK]}[kind]()
                sp.dma_start(slot_view(i, kind), src).then_inc(slot_in[i % RING], 16)

        @block.gpsimd
        def _(pool):
            nc.gpsimd.memset(mlpre[:, :, 0:3], 0.0).then_inc(pads, 1)
            for g in range(2):
                diag = [b[:, :, :].rearrange("p h (b q) -> p h b q", q=P)[:, :, 0:3:2, :] for b in (tb, tw)]
                for buf, before, after in ((diag[0], sb_sp, sb_spm), (diag[1], sb_w, sb_wm)):
                    pool.wait_ge(before, g + 1)
                    for half in range(2):
                        nc.gpsimd.affine_select(out=buf[:, :, half, :], in_=buf[:, :, half, :], compare_op=ALU.is_gt,
                                                fill=0.0, base=0, pattern=[[0, 4], [1, P]],
                                                channel_multiplier=-1).then_inc(after, 1)

        @block.tensor
        def _(pe):
            mm, tr = nc.tensor.matmul, nc.tensor.transpose

            pe.wait_ge(smalls, 16 * 9)
            tr(psA[:, 0, 0:32], convr[:, :], t.ident[0:32, 0:32]).then_inc(cw_t, 1)
            pe.wait_ge(xs_ready, 1)
            for b in range(4):
                for k in (2 * b, 2 * b + 1):
                    for tt in range(NT):
                        o = (k % 2) * SEQ + tt * P
                        last = tr(psP[:, b, o:o + P], xs[:, tt, k::NK], t.ident[:, :])
                last.then_inc(xT_done, 1)
            pe.wait_ge(xnT_ready, 4)

            def project(name):
                i = index[name]
                pair = psP[:, 2 * (i % 2):2 * (i % 2) + 2, :]
                if i >= 2:
                    pe.wait_ge(proj_copied, i - 1)
                if name == "if":
                    w = wif[:, :, :]
                else:
                    arrived(pe, place[name])
                    w = slot_view(place[name])
                if name in token_major:
                    n = w.shape[2]
                    for tt in range(NT):
                        for k in range(NK):
                            last = mm(pair[:, tt, 0:n], xnT[:, k, tt * P:(tt + 1) * P], w[:, k, :],
                                      start=k == 0, stop=k == NK - 1)
                else:
                    for s in range(4):
                        for k in range(NK):
                            last = mm(pair[:, s // 2, (s % 2) * SEQ:(s % 2 + 1) * SEQ], w[:, k, s * P:(s + 1) * P],
                                      xnT[:, k, :], start=k == 0, stop=k == NK - 1)
                last.then_inc(proj_done, 1)
                if name != "if":
                    pe.wait_ge(proj_done, i + 1)
                    pe.sem_inc(weights_used, 1)

            def head(h):
                return 64 * (h % 2), h // 2

            def sb_scores(g):
                pe.wait_ge(proj_copied, index["sbk"] + 1)
                if g == 0:
                    pe.wait_ge(cw_ready, 1)
                else:
                    pe.wait_ge(sb_e, g)
                for hh in range(4):
                    o, c = head(4 * g + hh)
                    mm(psA[:, hh, 0:256], sbk[o:o + HD, c, 0:P], sbq[o:o + HD, c, :], start=True, stop=True)
                    last = mm(psA[:, hh, 256:384], sbk[o:o + HD, c, P:], sbq[o:o + HD, c, P:], start=False, stop=True,
                              skip_group_check=True)
                last.then_inc(sb_z, 1)

            def sb_cumsum(g):
                pe.wait_ge(sb_spm, 2 * (g + 1))
                for hh in range(4):
                    mm(psA[:, hh, 0:256], t.trineg[:, :], tb[:, hh, 0:256], start=False, stop=True,
                       skip_group_check=True)
                    mm(psA[:, hh, P:256], t.negones[:, :], tb[:, hh, 256:384], start=False, stop=True,
                       skip_group_check=True)
                    last = mm(psA[:, hh, 256:384], t.trineg[:, :], tb[:, hh, 256:384], start=False, stop=True,
                              skip_group_check=True)
                last.then_inc(sb_c, 1)

            def weigh_values(g, v, done):
                for hh in range(4):
                    h = 4 * g + hh
                    o, _ = head(h)
                    dst = psA[o:o + HD, hh - hh % 2, :]
                    mm(dst[:, 0:256], v[:, 0, h * HD:(h + 1) * HD], tw[:, hh, 0:256], start=True, stop=True,
                       skip_group_check=True)
                    last = mm(dst[:, P:256], v[:, 1, h * HD:(h + 1) * HD], tw[:, hh, 256:384], start=False, stop=True,
                              skip_group_check=True)
                last.then_inc(done, 1)

            def sb_out(g):
                pe.wait_ge(sb_wm, 2 * (g + 1))
                pe.wait_ge(proj_copied, index["sbv"] + 1)
                weigh_values(g, sbv, sb_o)

            def mb_transposes():
                pe.wait_ge(mb_rot, 2)
                pe.wait_ge(abc_used, 1)
                for q in range(2):
                    for c in range(NC):
                        for tt in range(NT):
                            o = (c % 2) * SEQ + tt * P
                            last = tr(psA[:, 2 * q + c // 2, o:o + P], mbqk[:, q, tt, c * P:(c + 1) * P], t.ident[:, :])
                last.then_inc(mb_t, 1)

            def mb_scores(g):
                pe.wait_ge(mb_tc, 2)
                if g:
                    pe.wait_ge(mb_e, g)
                for hh in range(4):
                    o, c = head(4 * g + hh)
                    q, k = mbqkT[o:o + HD, 0, c, :], mbqkT[o:o + HD, 1, c, :]
                    mm(psA[:, hh, 0:P], q[:, 0:P], k[:, 0:P], start=True, stop=True)
                    last = mm(psA[:, hh, P:384], q[:, P:], k, start=True, stop=True)
                last.then_inc(mb_s, 1)

            def probs_T(ready, count, done):
                pe.wait_ge(ready, count)
                for hh in range(4):
                    for b in range(3):
                        last = tr(psA[:, hh, b * P:(b + 1) * P], ta[:, hh, b * P:(b + 1) * P], t.ident[:, :])
                last.then_inc(done, 1)

            def mb_out(g):
                pe.wait_ge(mb_w, g + 1)
                pe.wait_ge(proj_copied, index["mbv"] + 1)
                weigh_values(g, mbv, mb_o)

            def ml_cumsum():
                pe.wait_ge(lf_r, 1)
                pe.wait_ge(sb_e, 2)
                mm(psA[:, 0, 0:4], t.tri[:, :], lf[:, 0, :], start=True, stop=True, skip_group_check=True)
                mm(psA[:, 0, 4:8], t.tri[:, :], lf[:, 1, :], start=False, stop=True, skip_group_check=True)
                mm(psA[:, 0, 4:8], t.ones[:, :], lf[:, 0, :], start=False, stop=True,
                   skip_group_check=True).then_inc(f_done, 1)

            def ml_rows():
                pe.wait_ge(f_ready, 1)
                for tt in range(NT):
                    dg = mbqkT[:, 0, :, :].rearrange("p c n -> p (c n)")[:, tt * 512:(tt + 1) * 512]
                    last = mm(psA[:, tt, :], t.ones[:, :], dg, start=True, stop=True)
                last.then_inc(abc, 1)

            def ml_scores():
                pe.wait_ge(silu_done, 2)
                pe.wait_ge(mb_e, 2)
                for c in range(NC):
                    mm(psA[:, c, 0:P], mlqk[:, c, 0:P], mlqk[:, NC + c, 0:P], start=True, stop=True)
                    last = mm(psA[:, c, P:384], mlqk[:, c, P:], mlqk[:, NC + c, :], start=True, stop=True)
                last.then_inc(ml_s, 1)

            def ml_out():
                pe.wait_ge(ml_w, 1)
                pe.wait_ge(proj_copied, index["mlv"] + 1)
                for c in range(NC):
                    mm(psA[:, c, 0:256], mlv[:, 0, c * P:(c + 1) * P], tw[:, c, 0:256], start=True, stop=False,
                       skip_group_check=True)
                    last = mm(psA[:, c, P:256], mlv[:, 1, c * P:(c + 1) * P], tw[:, c, 256:384], start=False,
                              stop=True, skip_group_check=True)
                last.then_inc(ml_o, 1)

            npj = [len(chunks)]

            def take_pair():
                n = npj[0]
                npj[0] += 1
                if n - 2 < len(chunks):
                    pe.wait_ge(proj_copied, n - 1)
                else:
                    k = n - 2 - len(chunks)
                    if k < 6:
                        pe.wait_ge(merged, k + 1)
                    else:
                        pe.wait_ge(x_added, k - 6 + 1)
                return psP[:, 2 * (n % 2):2 * (n % 2) + 2, :]

            def branch(b):
                i = first_branch + b
                arrived(pe, i)
                w = slot_view(i, "branch")
                pe.wait_ge(*((sb_e, 2), (mb_e, 2), (ml_e, 1))[b])
                for half in range(2):
                    pair = take_pair()
                    for s in range(4):
                        j = 4 * half + s
                        for c in range(NC):
                            last = mm(pair[:, s // 2, (s % 2) * SEQ:(s % 2 + 1) * SEQ], w[:, c, j * P:(j + 1) * P],
                                      brT[:, b, c, :], start=c == 0, stop=c == NC - 1)
                    last.then_inc(proj_done, 1)
                pe.wait_ge(proj_done, npj[0])
                pe.sem_inc(weights_used, 1)

            def out_proj(n):
                i = first_out + n
                arrived(pe, i)
                w = slot_view(i)
                if n == 0:
                    pe.wait_ge(merged, 6)
                pair = take_pair()
                for tt in range(NT):
                    for j in range(NK):
                        last = mm(pair[:, tt, :], gates[:, NC + j, tt * P:(tt + 1) * P], w[:, j, :],
                                  start=j == 0, stop=j == NK - 1)
                last.then_inc(out_done, 1)

            project("sbq"); project("sbk"); project("sbv"); project("if")
            sb_scores(0); project("mlq"); sb_cumsum(0); project("mlk"); sb_out(0); project("mbq")
            sb_scores(1); project("mbk"); sb_cumsum(1); project("mlv"); sb_out(1); project("mbv")
            ml_cumsum(); project("mlo"); ml_rows(); project("g0"); mb_transposes(); project("g1")
            mb_scores(0); project("g2"); probs_T(mb_p, 1, mb_pt); project("g3"); mb_out(0)
            mb_scores(1); project("g4"); probs_T(mb_p, 2, mb_pt); project("g5"); mb_out(1)
            branch(0)
            ml_scores(); branch(1); probs_T(ml_p, 1, ml_pt)
            ml_out(); branch(2)
            out_proj(0); out_proj(1)

        @block.scalar
        def _(act):
            ch = Chain(act, ach)
            A = nc.scalar.activation

            for src, dst in [
                    (d.norm1_g[bass.ds(l, 1)].rearrange("l (p k) -> p (l k)", k=NK), gain[:, :]),
                    (d.qn_g[bass.ds(l, 1)].partition_broadcast(P).rearrange("p l n -> p (l n)"), qkg[:, 0, :]),
                    (d.kn_g[bass.ds(l, 1)].partition_broadcast(P).rearrange("p l n -> p (l n)"), qkg[:, 1, :]),
                    (d.ml_gate_b[bass.ds(l, 1)].partition_broadcast(P).rearrange("p l n -> p (l n)"), mlb[:, :]),
                    (w_in_l[:, :, COL_IF:COL_IF + 2 * ML_HEADS], wif[:, :, :])]:
                act.dma_start(dst, src).then_inc(smalls, 16)
            for j in range(4):
                act.dma_start(convr[8 * j:8 * j + 8, :],
                               d.conv_w[bass.ds(l, 1), j, :].rearrange("l (c p) -> (l c) p", p=P)).then_inc(smalls, 16)
            for tt in range(NT):
                A(xs[:, tt, :], t.x[:, tt, :], ACT.Square, accum_out=ms[:, tt:tt + 1]).then_inc(sq_done, 1)
            act.wait_ge(sq_done, NT)
            ch.after(A(rs[:, :], ms[:, :], ACT.Ln, bias=t.eps[:, :], scale=1.0 / D))
            A(rs[:, :], rs[:, :], ACT.Exp, scale=-0.5).then_inc(rstd_ready, 1)
            act.wait_ge(cw_t, 1)
            A(convw[:, :], psA[:, 0, 0:32], ACT.Copy).then_inc(cw_ready, 1)

            dest = {"sbq": (sbq, 1.0 / 8), "sbk": (sbk, 1.0), "sbv": (sbv, 1.0), "mbv": (mbv, 1.0), "mlv": (mlv, 1.0)}

            def copy(name):
                i = index[name]
                act.wait_ge(proj_done, i + 1)
                src = psP[:, 2 * (i % 2):2 * (i % 2) + 2, :]
                scale = 1.0
                if name == "if":
                    src, dst = src[:, :, 0:2 * ML_HEADS], iff[:, :, :]
                elif name in dest:
                    buf, scale = dest[name]
                    dst = buf[:, :, :]
                    src = src.rearrange("p b (c n) -> p (b c) n", n=dst.shape[2])
                elif name in ("mbq", "mbk"):
                    dst = mbqk[:, int(name == "mbk"), :, :]
                elif name in ("mlq", "mlk"):
                    o = NC * int(name == "mlk")
                    dst = mlpre[:, o:o + NC, 3:]
                    src = src.rearrange("p b (c n) -> p (b c) n", n=SEQ)
                else:
                    o = 0 if name == "mlo" else NC + 4 * int(name[1:])
                    dst = gates[:, o:o + 4, :]
                    src = src.rearrange("p b (c n) -> p (b c) n", n=SEQ)
                A(dst, src, ACT.Copy, scale=scale).then_inc(proj_copied, 1)

            def sb_softplus(g):
                act.wait_ge(sb_z, g + 1)
                ch.after(A(ta[:, :, :], psA[:, :, 0:384], ACT.Abs))
                ch.after(A(ta[:, :, :], ta[:, :, :], ACT.Exp, scale=-1.0))
                A(ta[:, :, :], ta[:, :, :], ACT.Ln, bias=1.0).then_inc(sb_ln, 1)

            def sb_exp(g):
                act.wait_ge(sb_c, g + 1)
                if g:
                    act.wait_ge(sb_o, g)
                A(tw[:, :, :], psA[:, :, 0:384], ACT.Exp).then_inc(sb_w, 1)

            def mb_squares(q):
                act.wait_ge(proj_copied, index["mbk" if q else "mbq"] + 1)
                if q == 0:
                    act.wait_ge(xT_done, 4)
                A(xs[:, q, :], mbqk[:, q, :, :].rearrange("p t n -> p (t n)"), ACT.Square).then_inc(mb_sq, 1)

            def mb_rstd():
                act.wait_ge(mb_ss, 2)
                ch.after(A(hrs[:, :, :], hss[:, :, :], ACT.Ln, bias=t.eps[:, :], scale=1.0 / HD))
                A(hrs[:, :, :], hrs[:, :, :], ACT.Exp, scale=-0.5).then_inc(mb_rs, 1)

            def mb_copyT():
                act.wait_ge(mb_t, 1)
                for q, s in ((0, 1.0 / 8), (1, 1.0)):
                    A(mbqkT[:, q, :, :], psA[:, 2 * q:2 * q + 2, :].rearrange("p b (c n) -> p (b c) n", n=SEQ),
                      ACT.Copy, scale=s).then_inc(mb_tc, 1)

            def rows_exp(ready, count, sink, done):
                act.wait_ge(ready, count)
                for hh in range(4):
                    for r, (a, b) in enumerate(((0, P), (P, 384))):
                        acc = {"accum_out": sums[:, hh, r:r + 1]} if sink else {}
                        A(ta[:, hh, a:b], ta[:, hh, a:b], ACT.Exp, bias=nmx[:, hh, r:r + 1], **acc).then_inc(done, 1)

            def copy_w(src_done, count, done):
                act.wait_ge(src_done, count)
                A(tw[:, :, :], psA[:, :, 0:384], ACT.Copy).then_inc(done, 1)

            def if_softplus():
                act.wait_ge(if_b, 1)
                ch.after(A(lft[:, :, :], iff[:, :, 4:8], ACT.Abs))
                ch.after(A(lft[:, :, :], lft[:, :, :], ACT.Exp, scale=-1.0))
                A(lft[:, :, :], lft[:, :, :], ACT.Ln, bias=1.0).then_inc(if_sp, 1)

            copy("sbq"); copy("sbk"); copy("sbv"); copy("if")
            sb_softplus(0); copy("mlq")
            sb_exp(0); copy("mlk")
            if_softplus()
            copy("mbq"); mb_squares(0); sb_softplus(1); copy("mbk"); mb_squares(1)
            sb_exp(1); mb_rstd(); copy("mlv"); copy("mbv")
            copy("mlo"); copy("g0"); mb_copyT(); copy("g1")
            copy("g2"); rows_exp(mb_m, 1, True, mb_exp); copy_w(mb_pt, 1, mb_w); copy("g3")
            copy("g4"); rows_exp(mb_m, 2, True, mb_exp)
            copy_w(mb_pt, 2, mb_w); copy("g5")
            act.wait_ge(proj_copied, len(chunks))
            A(gates[:, :, :], gates[:, :, :], ACT.Sigmoid).then_inc(sig, 1)
            for q in range(2):
                act.wait_ge(conv_done, q + 1)
                o = q * NC
                A(mlqk[:, o:o + NC, :], mlqk[:, o:o + NC, :], ACT.Silu).then_inc(silu_done, 1)
            act.wait_ge(fl_in, 1)
            A(flo[:, :, :], flo[:, :, :], ACT.Exp, scale=-1.0).then_inc(fl_ready, 1)
            rows_exp(d_ready, 1, False, w_ready)
            copy_w(ml_pt, 1, ml_w)

        @block.vector
        def _(dve):
            ch = Chain(dve, dch)
            v = nc.vector
            dve.wait_ge(rstd_ready, 1)
            dve.wait_ge(sq_done, NT)
            for tt in range(NT):
                last = v.tensor_scalar(xs[:, tt, :], t.x[:, tt, :], rs[:, tt:tt + 1], None, ALU.mult)
                ch.after(last)
            v.tensor_copy(t.junk[:, 0:1], rs[:, 0:1]).then_inc(xs_ready, 1)
            dve.wait_ge(smalls, 16 * 9)
            for b in range(4):
                dve.wait_ge(xT_done, b + 1)
                v.tensor_tensor(xnT[:, 2 * b:2 * b + 2, :], psP[:, b, :].rearrange("p (k n) -> p k n", k=2),
                                bc(gain[:, 2 * b:2 * b + 2], 2, SEQ), ALU.mult).then_inc(xnT_ready, 1)

            def sb_softplus(g):
                dve.wait_ge(sb_ln, g + 1)
                if g:
                    dve.wait_ge(sb_c, g)
                v.scalar_tensor_tensor(out=tb[:, :, :], in0=psA[:, :, 0:384], scalar=0.0, in1=ta[:, :, :],
                                       op0=ALU.max, op1=ALU.add).then_inc(sb_sp, 1)

            def copy_out(g, b, ready, done):
                dve.wait_ge(ready, g + 1)
                v.tensor_copy(brT[:, b, 2 * g:2 * g + 2, :], psA[:, 0:3:2, 0:256]).then_inc(done, 1)

            def conv(q):
                dve.wait_ge(proj_copied, index["mlk" if q else "mlq"] + 1)
                dve.wait_ge(cw_ready, 1)
                dve.wait_ge(pads, 1)
                for j in range(4):
                    for c in range(q * NC, q * NC + NC):
                        w = convw[:, 8 * j + c:8 * j + c + 1]
                        src = mlpre[:, c, j:j + SEQ]
                        if j == 0:
                            last = v.tensor_scalar(mlqk[:, c, :], src, w, None, ALU.mult)
                        else:
                            last = v.scalar_tensor_tensor(out=mlqk[:, c, :], in0=src, scalar=w, in1=mlqk[:, c, :],
                                                          op0=ALU.mult, op1=ALU.add)
                    if j < 3:
                        ch.after(last)
                last.then_inc(conv_done, 1)

            def mb_norm(q):
                x = mbqk[:, q, :, :].rearrange("p t (h n) -> p (t h) n", n=HD)
                ch.after(v.tensor_tensor(x, x, bc(hrs[:, q, :], 2, HD), ALU.mult))
                ch.after(v.tensor_tensor(x, x, bc(qkg[:, q, :], 1, NT * HEADS), ALU.mult))
                x = mbqk[:, q, :, :].rearrange("p t (h n) -> p t h n", n=HD)
                x1, x2 = x[:, :, :, 0:ROT], x[:, :, :, ROT:2 * ROT]
                cos, sin = bc(t.cos[:, :, :], 2, HEADS), bc(t.sin[:, :, :], 2, HEADS)
                v.tensor_tensor(r4[:, 0], x1, cos, ALU.mult)
                v.tensor_tensor(r4[:, 1], x2, sin, ALU.mult)
                v.tensor_tensor(r4[:, 2], x1, sin, ALU.mult)
                ch.after(v.tensor_tensor(r4[:, 3], x2, cos, ALU.mult))
                v.tensor_tensor(x1, r4[:, 0], r4[:, 1], ALU.subtract)
                ch.after(v.tensor_tensor(x2, r4[:, 2], r4[:, 3], ALU.add))
                v.tensor_copy(t.junk[:, 0:1], rs[:, 0:1]).then_inc(mb_rot, 1)

            def row_max(floor):
                ch.after(v.tensor_reduce(mxb[:, :, 0], ta[:, :, 0:P], AX.X, ALU.max))
                ch.after(v.tensor_reduce(mxb[:, :, 1], ta[:, :, P:384], AX.X, ALU.max))
                if floor:
                    ch.after(v.tensor_scalar(mxb[:, :, :], mxb[:, :, :], 0.0, None, ALU.max))
                return v.tensor_scalar(nmx[:, :, :], mxb[:, :, :], -1.0, None, ALU.mult)

            def mb_softmax_in(g):
                dve.wait_ge(mb_s, g + 1)
                if g:
                    dve.wait_ge(mb_pt, g)
                nm = bc(t.neg_mask[:, :], 1, 4)
                v.tensor_tensor(ta[:, :, 0:P], psA[:, :, 0:P], nm, ALU.add)
                v.tensor_copy(ta[:, :, P:2 * P], psA[:, :, P:2 * P])
                ch.after(v.tensor_tensor(ta[:, :, 2 * P:], psA[:, :, 2 * P:384], nm, ALU.add))
                row_max(False).then_inc(mb_m, 1)

            def scale_rows(r, done):
                v.tensor_tensor(ta[:, :, 0:P], ta[:, :, 0:P], bc(r[:, :, 0], 2, P), ALU.mult)
                ch.after(v.tensor_tensor(ta[:, :, P:], ta[:, :, P:], bc(r[:, :, 1], 2, 2 * P), ALU.mult))
                v.tensor_copy(t.junk[:, 0:1], rs[:, 0:1]).then_inc(done, 1)

            def mb_normalise(g):
                dve.wait_ge(mb_exp, 8 * (g + 1))
                ch.after(v.reciprocal(rsum[:, :, :], sums[:, :, :]))
                scale_rows(rsum, mb_p)

            def if_bias():
                dve.wait_ge(proj_copied, index["if"] + 1)
                v.tensor_tensor(iff[:, :, :], iff[:, :, :], bc(mlb[:, :], 1, NT), ALU.add).then_inc(if_b, 1)

            def log_f():
                dve.wait_ge(if_sp, 1)
                v.scalar_tensor_tensor(out=lf[:, :, :], in0=iff[:, :, 4:8], scalar=0.0, in1=lft[:, :, :],
                                       op0=ALU.min, op1=ALU.subtract).then_inc(lf_r, 1)

            def a_diag():
                dve.wait_ge(f_done, 1)
                ch.after(v.tensor_copy(Fc[:, :, :], psA[:, 0, 0:8].rearrange("p (t h) -> p t h", t=NT)))
                ch.after(v.tensor_tensor(av[:, :, :], iff[:, :, 0:4], Fc[:, :, :], ALU.subtract))
                dst = mbqkT[:, 0, :, :].rearrange("p c (a n) -> p (c a) n", n=P)
                v.tensor_tensor(dst, bc(t.ident[:, :], 1, NT * ML_HEADS),
                                bc(av[:, :, :].rearrange("p t h -> p (t h)"), 2, P), ALU.mult).then_inc(f_ready, 1)

            def a_rows_copy():
                dve.wait_ge(abc, 1)
                v.tensor_copy(mbqkT[:, 1, :, :].rearrange("p c n -> p (c n)"),
                              psA[:, 0:2, :].rearrange("p b n -> p (b n)")).then_inc(abc_used, 1)

            if_bias()
            sb_softplus(0)
            conv(0)
            log_f()
            copy_out(0, 0, sb_o, sb_e)
            sb_softplus(1)
            conv(1)
            for q in range(2):
                dve.wait_ge(mb_sq, q + 1)
                v.tensor_reduce(hss[:, q, :], xs[:, q, :].rearrange("p (h n) -> p h n", n=HD), AX.X,
                                ALU.add).then_inc(mb_ss, 1)
            copy_out(1, 0, sb_o, sb_e)
            dve.wait_ge(mb_rs, 1)
            mb_norm(0)
            a_diag()
            mb_norm(1)
            dve.wait_ge(abc, 1)
            ml_d = xs[:, :, :].rearrange("p t n -> p (t n)")[:, 0:1536].rearrange("p (h n) -> p h n", n=384)
            row = [psA[:, tt, :].rearrange("p (h n) -> p h n", n=P) for tt in range(NT)]
            nm = bc(t.neg_mask[:, :], 1, 4)
            v.tensor_tensor(ml_d[:, :, 0:P], row[0], nm, ALU.add)
            v.tensor_copy(ml_d[:, :, P:2 * P], row[0])
            v.tensor_tensor(ml_d[:, :, 2 * P:], row[1], nm, ALU.add).then_inc(abc_used, 1)
            for g in range(2):
                mb_softmax_in(g)
                mb_normalise(g)
                copy_out(g, 1, mb_o, mb_e)
            dve.wait_ge(mb_pt, 2)
            dve.wait_ge(mb_exp, 16)
            ch.after(v.tensor_copy(ta[:, :, :], ml_d))
            row_max(True).then_inc(d_ready, 1)
            v.tensor_tensor(flo[:, :, :], mxb[:, :, :], Fc[:, :, :].rearrange("p t h -> p h t"),
                            ALU.add).then_inc(fl_in, 1)

            def merge(b):
                for half in range(2):
                    n = 2 * b + half
                    i = len(chunks) + n
                    dve.wait_ge(proj_done, i + 1)
                    ps = psP[:, 2 * (i % 2):2 * (i % 2) + 2, :].rearrange("p b (c n) -> p (b c) n", n=SEQ)
                    o = NC + b * NK + 4 * half
                    gb, g0 = gates[:, o:o + 4, :], gates[:, NC + 4 * half:NC + 4 * half + 4, :]
                    ins = v.tensor_tensor(gb, ps, gb, ALU.mult)
                    if b:
                        ch.after(ins)
                        ins = v.tensor_tensor(g0, g0, gb, ALU.add)
                    ins.then_inc(merged, 1)
                    dve.wait_ge(merged, n + 1)

            dve.wait_ge(sig, 1)
            merge(0)
            dve.wait_ge(ml_s, 1)
            dve.wait_ge(w_ready, 8)
            ch.after(v.scalar_tensor_tensor(out=ta[:, :, :], in0=psA[:, :, 0:384], scalar=float(ML_HD) ** -0.5,
                                            in1=ta[:, :, :], op0=ALU.mult, op1=ALU.mult))
            v.tensor_reduce(den[:, :, 0], ta[:, :, 0:P], AX.X, ALU.add)
            ch.after(v.tensor_reduce(den[:, :, 1], ta[:, :, P:384], AX.X, ALU.add))
            ch.after(v.tensor_scalar(dneg[:, :, :], den[:, :, :], -1.0, None, ALU.mult))
            ch.after(v.tensor_tensor(den[:, :, :], den[:, :, :], dneg[:, :, :], ALU.max))
            dve.wait_ge(fl_ready, 1)
            ch.after(v.tensor_tensor(den[:, :, :], den[:, :, :], flo[:, :, :], ALU.max))
            ch.after(v.reciprocal(den[:, :, :], den[:, :, :]))
            scale_rows(den, ml_p)
            merge(1)
            dve.wait_ge(ml_o, 1)
            v.tensor_tensor(brT[:, 2, :, :], psA[:, :, 0:256], gates[:, 0:NC, :], ALU.mult).then_inc(ml_e, 1)
            merge(2)
            for n in range(2):
                i = len(chunks) + 6 + n
                dve.wait_ge(out_done, n + 1)
                xh = t.x[:, :, n * CHUNK:(n + 1) * CHUNK]
                v.tensor_tensor(xh, psP[:, 2 * (i % 2):2 * (i % 2) + 2, :], xh, ALU.add).then_inc(x_added, 1)
            dve.wait_ge(x_added, 2)
    ph.end()
    mem.close()


def tensors(nc, ctx):
    class T:
        pass
    t = T()

    def sb(name, shape, dt=F32):
        return ctx.enter_context(nc.sbuf_tensor(name, shape, dt))
    t.x = sb("x_res", [P, NT, D])
    t.ring = sb("weight_ring", [P, RING, NK * CHUNK])
    t.ident, t.trineg, t.tri, t.tri_strict = (sb(n, [P, P]) for n in ("ident", "trineg", "tri", "tri_strict"))
    t.neg_mask, t.ones, t.negones = (sb(n, [P, P]) for n in ("neg_mask", "ones", "negones"))
    t.eps, t.junk = sb("eps", [P, 1]), sb("junk", [P, 1])
    t.fold, t.slot, t.slot_i = sb("fold", [P, SLOTS]), sb("slot", [P, SLOTS]), sb("slot_i", [P, SLOTS], I32)
    t.pos_i, t.pos, t.freq = sb("pos_i", [P, NT], I32), sb("pos", [P, NT]), sb("freq", [P, ROT])
    t.ang, t.turn, t.sin, t.cos = (sb(n, [P, NT, ROT]) for n in ("ang", "turn", "sin", "cos"))
    t.ps_a = ctx.enter_context(nc.psum_tensor("ps_a", [P, 4, 512], F32))
    t.ps_b = ctx.enter_context(nc.psum_tensor("ps_b", [P, 4, 512], F32))
    return t



def route(nc, t, d, l, m, prefetch):
    ph = Phase(nc, "route")
    mem = ExitStack()
    S = ph.sem

    def sb(name, shape, dt=F32):
        return mem.enter_context(nc.sbuf_tensor(name, shape, dt))

    NR = NG + NE
    gain, xn, xnT = sb("gain2", [P, D]), sb("xn2", [P, NT, D]), sb("xn2T", [P, NK, SEQ])
    wr, br, lg = sb("w_router", [P, NK, NR]), sb("b_router", [P, NR]), sb("logits", [P, NT, NR])
    ms, rs = sb("mean_sq2", [P, NT]), sb("rstd2", [P, NT])
    gmax, gsum, kmin, m1, m2, w1, w2, er = (sb(n, [P, NT]) for n in (
        "group_max", "group_sum", "key_min", "first_max", "second_max", "first_w", "second_w", "max_ratio"))
    gexp, ohg, keyg = (sb(n, [P, NT, NG]) for n in ("group_exp", "group_pick", "group_key"))
    em, key, oh1, oh2, A = (sb(n, [P, NT, NE]) for n in (
        "group_logits", "expert_key", "first_pick", "second_pick", "assigned"))
    nmax, cmp = sb("most_tokens", [P, 1]), sb("over", [P, 3])

    smalls, sq_done, rstd_ready, xn_ready, hi_done, xnT_ps, xnT_ready = (S(n) for n in (
        "small_loads", "sum_sq_done", "rstd_ready", "xn_ready", "xn_high_done", "xT_done", "xnT_ready"))
    logits_done, gexp_in, gexp_done, er_in, er_done, picked, counted, dch, ach = (S(n) for n in (
        "logits_done", "group_exp_in", "group_exp_done", "ratio_in", "ratio_done", "picked", "counted",
        "dve_chain", "act_chain"))

    with nc.Block() as block:
        @block.sync
        def _(sp):
            prefetch(sp)

        @block.scalar
        def _(act):
            ch = Chain(act, ach)
            A_ = nc.scalar.activation
            L = bass.ds(l, 1)
            for src, dst in [
                    (d.norm2_g[L].partition_broadcast(P).rearrange("p l n -> p (l n)"), gain[:, :]),
                    (d.w_rg[L].rearrange("l (p k) n -> p (l k) n", p=P), wr[:, :, 0:NG]),
                    (d.w_re[L].rearrange("l (p k) n -> p (l k) n", p=P), wr[:, :, NG:]),
                    (d.b_rg[L].partition_broadcast(P).rearrange("p l n -> p (l n)"), br[:, 0:NG]),
                    (d.b_re[L].partition_broadcast(P).rearrange("p l n -> p (l n)"), br[:, NG:])]:
                act.dma_start(dst, src).then_inc(smalls, 16)
            for tt in range(NT):
                A_(xn[:, tt, :], t.x[:, tt, :], ACT.Square, accum_out=ms[:, tt:tt + 1]).then_inc(sq_done, 1)
            act.wait_ge(sq_done, NT)
            ch.after(A_(rs[:, :], ms[:, :], ACT.Ln, bias=t.eps[:, :], scale=1.0 / D))
            A_(rs[:, :], rs[:, :], ACT.Exp, scale=-0.5).then_inc(rstd_ready, 1)
            for b in range(4):
                act.wait_ge(xnT_ps, b + 1)
                A_(xnT[:, 2 * b:2 * b + 2, :], t.ps_a[:, b, :].rearrange("p (k n) -> p k n", k=2),
                   ACT.Copy).then_inc(xnT_ready, 1)
            for tt in range(NT):
                act.wait_ge(xn_ready, tt + 1)
                A_(m.xn_hi[:, tt, :], xn[:, tt, :], ACT.Copy).then_inc(hi_done, 1)
            act.wait_ge(gexp_in, 1)
            A_(gexp[:, :, :], gexp[:, :, :], ACT.Exp).then_inc(gexp_done, 1)
            act.wait_ge(er_in, 1)
            A_(er[:, :], er[:, :], ACT.Exp).then_inc(er_done, 1)

        @block.tensor
        def _(pe):
            mm = nc.tensor.matmul
            pe.wait_ge(xn_ready, NT)
            for b in range(4):
                for k in (2 * b, 2 * b + 1):
                    for tt in range(NT):
                        o = (k % 2) * SEQ + tt * P
                        last = nc.tensor.transpose(t.ps_a[:, b, o:o + P], xn[:, tt, k::NK], t.ident[:, :])
                last.then_inc(xnT_ps, 1)
            pe.wait_ge(smalls, 16 * 5)
            pe.wait_ge(xnT_ready, 4)
            for tt in range(NT):
                for k in range(NK):
                    last = mm(t.ps_b[:, tt, 0:NR], xnT[:, k, tt * P:(tt + 1) * P], wr[:, k, :],
                              start=k == 0, stop=k == NK - 1)
            last.then_inc(logits_done, 1)
            pe.wait_ge(picked, 1)
            o = t.ps_b[:, 2, :]
            mm(o[:, 0:NE], t.tri_strict[:, :], A[:, 0, :], start=True, stop=True, skip_group_check=True)
            mm(o[:, NE:2 * NE], t.tri_strict[:, :], A[:, 1, :], start=False, stop=True, skip_group_check=True)
            mm(o[:, NE:2 * NE], t.ones[:, :], A[:, 0, :], start=False, stop=True, skip_group_check=True)
            mm(o[:, 2 * NE:3 * NE], t.ones[:, :], A[:, 0, :], start=False, stop=True, skip_group_check=True)
            mm(o[:, 2 * NE:3 * NE], t.ones[:, :], A[:, 1, :], start=False, stop=True,
               skip_group_check=True).then_inc(counted, 1)

        @block.vector
        def _(dve):
            ch = Chain(dve, dch)
            v = nc.vector
            dve.wait_ge(rstd_ready, 1)
            dve.wait_ge(smalls, 16 * 5)
            for tt in range(NT):
                v.scalar_tensor_tensor(out=xn[:, tt, :], in0=t.x[:, tt, :], scalar=rs[:, tt:tt + 1], in1=gain[:, :],
                                       op0=ALU.mult, op1=ALU.mult).then_inc(xn_ready, 1)
            for tt in range(NT):
                dve.wait_ge(hi_done, tt + 1)
                ch.after(v.tensor_tensor(m.xn_lo[:, tt, :], xn[:, tt, :], m.xn_hi[:, tt, :].bitcast(F32),
                                         ALU.subtract))
            dve.wait_ge(logits_done, 1)
            ch.after(v.tensor_tensor(lg[:, :, :], t.ps_b[:, 0:NT, 0:NR], bc(br[:, :], 1, NT), ALU.add))

            def first_max(vals, mx, k, out, n):
                ch.after(v.tensor_reduce(mx[:, :], vals, AX.X, ALU.max))
                ch.after(v.tensor_tensor(k[:, :, :], vals, bc(mx[:, :], 2, n), ALU.is_equal))
                ch.after(v.scalar_tensor_tensor(out=k[:, :, :], in0=k[:, :, :], scalar=-64.0,
                                                in1=bc(t.slot[:, 0:n], 1, NT), op0=ALU.mult, op1=ALU.add))
                ch.after(v.tensor_reduce(kmin[:, :], k[:, :, :], AX.X, ALU.min))
                ch.after(v.tensor_tensor(out[:, :, :], k[:, :, :], bc(kmin[:, :], 2, n), ALU.is_equal))

            groups = lg[:, :, 0:NG]
            first_max(groups, gmax, keyg, ohg, NG)
            v.tensor_tensor(gexp[:, :, :], groups, bc(gmax[:, :], 2, NG), ALU.subtract).then_inc(gexp_in, 1)
            ch.after(v.tensor_scalar(keyg[:, :, :], ohg[:, :, :], -NEG, NEG, ALU.mult, ALU.add))
            for tt in range(NT):
                last = v.tensor_tensor(em[:, tt, :].rearrange("p (g e) -> p g e", g=NG),
                                       lg[:, tt, NG:].rearrange("p (g e) -> p g e", g=NG),
                                       bc(keyg[:, tt, :], 2, EPG), ALU.add)
                ch.after(last)
            first_max(em[:, :, :], m1, key, oh1, NE)
            ch.after(v.scalar_tensor_tensor(out=em[:, :, :], in0=oh1[:, :, :], scalar=NEG, in1=em[:, :, :],
                                            op0=ALU.mult, op1=ALU.add))
            first_max(em[:, :, :], m2, key, oh2, NE)
            v.tensor_tensor(er[:, :], m2[:, :], m1[:, :], ALU.subtract).then_inc(er_in, 1)
            v.tensor_tensor(A[:, :, :], oh1[:, :, :], oh2[:, :, :], ALU.add).then_inc(picked, 1)
            dve.wait_ge(gexp_done, 1)
            ch.after(v.tensor_reduce(gsum[:, :], gexp[:, :, :], AX.X, ALU.add))
            dve.wait_ge(er_done, 1)
            ch.after(v.tensor_scalar(w1[:, :], er[:, :], 1.0, None, ALU.add))
            ch.after(v.tensor_tensor(w1[:, :], w1[:, :], gsum[:, :], ALU.mult))
            ch.after(v.reciprocal(w1[:, :], w1[:, :]))
            ch.after(v.tensor_tensor(w2[:, :], w1[:, :], er[:, :], ALU.mult))
            v.tensor_tensor(oh1[:, :, :], oh1[:, :, :], bc(w1[:, :], 2, NE), ALU.mult)
            ch.after(v.tensor_tensor(oh2[:, :, :], oh2[:, :, :], bc(w2[:, :], 2, NE), ALU.mult))
            ch.after(v.tensor_tensor(m.comb[:, :, :], oh1[:, :, :], oh2[:, :, :], ALU.add))
            dve.wait_ge(counted, 1)
            ch.after(v.scalar_tensor_tensor(out=m.place[:, :, :],
                                            in0=t.ps_b[:, 2, 0:2 * NE].rearrange("p (t e) -> p t e", t=NT), scalar=1.0,
                                            in1=A[:, :, :], op0=ALU.add, op1=ALU.mult))
            ch.after(v.tensor_scalar(m.place[:, :, :], m.place[:, :, :], -1.0, None, ALU.add))
            ch.after(v.tensor_reduce(nmax[:, :], t.ps_b[:, 2, 2 * NE:3 * NE], AX.X, ALU.max))
            for i in range(3):
                last = v.tensor_scalar(cmp[:, i:i + 1], nmax[:, :], float(SLOTS * (i + 1)), None, ALU.is_gt)
            ch.after(last)
            ch.after(v.tensor_reduce(nmax[:, :], cmp[:, :], AX.X, ALU.add))
            ch.after(v.tensor_scalar(m.rounds[:, :], nmax[0:1, :], 1.0, None, ALU.add))
            ch.after(v.tensor_copy(m.slot[:, :], t.slot[:, :]))
    ph.end()
    mem.close()



def moe(nc, t, d, l):
    mem = ExitStack()

    class M:
        pass
    m = M()

    def sb(name, shape, dt=F32):
        return mem.enter_context(nc.sbuf_tensor(name, shape, dt))

    m.xn_hi, m.xn_lo = sb("xn_hi", [P, NT, D], F32R), sb("xn_lo", [P, NT, D], F32R)
    m.comb, m.place, m.slot = sb("combine", [P, NT, NE]), sb("place", [P, NT, NE]), sb("slot_round", [P, SLOTS])
    m.rounds = sb("rounds", [1, 1], I32)
    pre = [mem.enter_context(nc.semaphore(f"units_ahead{i}")) for i in range(URING)]

    order = [("A", 0), ("B", 0)]
    for e in range(1, BATCH + 1):
        order += [("A", e), ("B", e)] if e < BATCH else []
        order += [("C", e - 1)]
    number = {u: i for i, u in enumerate(order)}

    def load(sp, n, first, sem):
        kind, e = order[n]
        dst = t.ring[:, :, :].rearrange("p a b -> p (a b)")[:, (n % URING) * UNIT:(n % URING + 1) * UNIT]
        L, X = bass.ds(l, 1), bass.ds(first + e, 1)
        if kind == "C":
            src = d.w2[L, X].rearrange("l e (p j) n -> p (l e j) n", p=P)
            dst = dst.rearrange("p (j n) -> p j n", j=2)
            for j in range(2):
                sp.dma_start(dst[:, j, :], src[:, j, :]).then_inc(sem, 16)
        else:
            k0 = 0 if kind == "A" else 4
            dst = dst.rearrange("p (k n) -> p k n", k=4)
            for j, w in enumerate((d.w1, d.w3)):
                src = w[L, X].rearrange("l e (p k) n -> p (l e k) n", p=P)
                sp.dma_start(dst[:, :, j * FE:(j + 1) * FE], src[:, k0:k0 + 4, :]).then_inc(sem, 16)

    def prefetch(sp):
        for n in range(URING):
            load(sp, n, 0, pre[n])

    route(nc, t, d, l, m, prefetch)

    hi, lo = sb("w_hi", [P, SPLITS, UNIT], F32R), sb("w_lo", [P, SPLITS, UNIT], F32R)
    XT = sb("XT", [P, NK, BATCH, 2 * SLOTS], F32R)
    sel, selw0 = sb("select", [P, NT, BATCH, 2 * SLOTS], F32R), sb("select_weighted", [P, 2 * FE])
    selT, cw = sb("selectT", [P, BATCH, SEQ], F32R), sb("slot_weight", [P, BATCH, SLOTS])
    h, act1, u = sb("h", [P, 2 * FE]), sb("silu_h1", [P, 2, SLOTS]), sb("h3_weighted", [P, 2, SLOTS])
    selw = [selw0, h]
    hid = sb("hid", [P, 2, 2, 2 * SLOTS], F32R)
    yhi, ylo = sb("y_hi", [P, D], F32R), sb("y_lo", [P, D], F32R)

    rounds = nc.values_load(m.rounds[0:1, 0:1], min_val=1, max_val=SEQ // SLOTS)
    with nc.Fori(0, rounds) as r:
        with nc.Fori(0, NE // BATCH) as b:
            experts(nc, t, l, m, b, r, rounds, pre, order, number, load, hi, lo, XT, sel, selw, selT, cw, h, act1, u,
                    hid, yhi, ylo)
        ph = Phase(nc, "next_round")
        moved = ph.sem("slots_moved")
        with nc.Block() as block:
            @block.vector
            def _(dve):
                nc.vector.tensor_scalar(m.slot[:, :], m.slot[:, :], float(SLOTS), None, ALU.add).then_inc(moved, 1)
                dve.wait_ge(moved, 1)
        ph.end()
    for s in pre:
        nc.sync.sem_clear(s)
    nc.all_engine_barrier()
    mem.close()


def experts(nc, t, l, m, b, r, rounds, pre, order, number, load, hi, lo, XT, sel, selw, selT, cw, h, act1, u, hid,
            yhi, ylo):
    ph = Phase(nc, "exp")
    S = ph.sem
    later = [S(f"units_in{i}") for i in range(URING)]
    hi_ready, lo_ready, unit_used = S("high_ready"), S("low_ready"), S("unit_used")
    sel_ready, selw_ready, selT_ps, selT_ready, cw_ps, cw_ready = (S(n) for n in (
        "select_ready", "weighted_ready", "selectT_ps", "selectT_ready", "slot_weight_ps", "slot_weight_ready"))
    xt_ps, xt_hi, xt_lo = S("gathered_ps"), S("gathered_high"), S("gathered_low")
    h_done, h_copied, ht_done, silu_done, u_done, hid_ready = (S(n) for n in (
        "h_done", "h_copied", "hT_done", "silu_done", "h3_weighted_done", "hid_ready"))
    y_done, yhi_done, ylo_done, s_done, x_added, dch = (S(n) for n in (
        "y_done", "y_high_done", "y_low_done", "scattered", "x_added", "dve_chain"))
    acc, ps_h, ps_ht, ps_y = t.ps_a, t.ps_b[:, 0, :], t.ps_b[:, 1, 0:4 * SLOTS], t.ps_b[:, 2:4, :]
    raw = t.ring[:, :, :].rearrange("p a b -> p (a b)").rearrange("p (u n) -> p u n", n=UNIT)
    NU = len(order)
    ready_batch = bass.ds(b * BATCH, BATCH)

    def arrived(eng, n):
        if n < URING:
            eng.wait_ge(pre[n], 32)
        else:
            eng.wait_ge(later[n % URING], 32 * (n // URING))

    with nc.Block() as block:
        @block.sync
        def _(sp):
            for n in range(URING, NU):
                sp.wait_ge(lo_ready, n - URING + 1)
                load(sp, n, b * BATCH, later[n % URING])
            with sp.If(r * (NE // BATCH) + b + 1 < rounds * (NE // BATCH)):
                for n in range(URING):
                    sp.wait_ge(lo_ready, NU - URING + n + 1)
                    sp.sem_clear(pre[n])
                    load(sp, n, ((b + 1) % (NE // BATCH)) * BATCH, pre[n])

        @block.tensor
        def _(pe):
            mm, tr = nc.tensor.matmul, nc.tensor.transpose
            pe.wait_ge(sel_ready, 2 * NT)
            for q in range(BATCH // 2):
                if q >= 2:
                    pe.wait_ge(selT_ready, q - 1)
                for e in (2 * q, 2 * q + 1):
                    for tt in range(NT):
                        o = (e % 2) * SEQ + tt * P
                        last = tr(ps_y[:, q % 2, o:o + P], sel[:, tt, e, :].bitcast(F32), t.ident[:, :])
                last.then_inc(selT_ps, 1)
            pe.wait_ge(selw_ready, NT)
            for tt in range(NT):
                last = mm(t.ps_b[:, 1, :], t.ones[:, :], selw[tt][:, :],
                          start=tt == 0, stop=tt == NT - 1)
            last.then_inc(cw_ps, 1)
            for k in range(NK):
                if k >= 2:
                    pe.wait_ge(xt_hi, k - 1)
                    pe.wait_ge(xt_lo, k - 1)
                for part, xn in enumerate((m.xn_hi, m.xn_lo)):
                    for tt in range(NT):
                        last = mm(acc[:, 2 * (k % 2) + part, :], xn[:, tt, k::NK],
                                  sel[:, tt, :, 0:SLOTS], start=tt == 0, stop=tt == NT - 1)
                last.then_inc(xt_ps, 1)
            pe.wait_ge(xt_hi, NK)
            pe.wait_ge(xt_lo, NK)

            def split_ready(n):
                pe.wait_ge(hi_ready, n + 1)
                pe.wait_ge(lo_ready, n + 1)

            for e in range(BATCH + 2):
                if e < BATCH:
                    if e:
                        pe.wait_ge(h_copied, e)
                    for half, kind in enumerate("AB"):
                        n = number[kind, e]
                        split_ready(n)
                        for k in range(4):
                            for part in (hi, lo):
                                last = mm(ps_h, XT[:, 4 * half + k, e, :], part[:, n % SPLITS, k * 512:(k + 1) * 512],
                                          start=half == 0 and k == 0 and part is hi,
                                          stop=half == 1 and k == 3 and part is lo)
                        last.then_inc(unit_used, 1)
                    pe.wait_ge(unit_used, n + 1)
                    pe.sem_inc(h_done, 1)
                if e >= 2:
                    pe.wait_ge(ylo_done, e - 1)
                    pe.wait_ge(yhi_done, e - 1)
                    if e == 2:
                        pe.wait_ge(selT_ready, BATCH // 2)
                    for tt in range(NT):
                        for n2 in range(2):
                            for part in (yhi, ylo):
                                last = mm(acc[:, 2 * tt + n2, :], selT[:, e - 2, tt * P:(tt + 1) * P],
                                          part[:, n2 * 512:(n2 + 1) * 512], start=e == 2 and part is yhi,
                                          stop=e == BATCH + 1 and part is ylo)
                    last.then_inc(s_done, 1)
                if e < BATCH:
                    pe.wait_ge(h_copied, e + 1)
                    if e:
                        pe.wait_ge(hid_ready, e)
                    else:
                        pe.wait_ge(cw_ready, 1)
                    for w in range(2):
                        for j in range(2):
                            o = (2 * w + j) * SLOTS
                            last = mm(ps_ht[:, o:o + SLOTS], h[:, w * FE + j:(w + 1) * FE:2], t.fold[:, :],
                                      start=True, stop=True)
                    last.then_inc(ht_done, 1)
                if 1 <= e <= BATCH:
                    n = number["C", e - 1]
                    split_ready(n)
                    pe.wait_ge(hid_ready, e)
                    if e >= 2:
                        pe.wait_ge(ylo_done, e - 1)
                    for n2 in range(2):
                        for j in range(2):
                            for part in (hi, lo):
                                last = mm(ps_y[:, n2, :], hid[:, (e - 1) % 2, j, :],
                                          part[:, n % SPLITS, j * D + n2 * 512:j * D + n2 * 512 + 512],
                                          start=j == 0 and part is hi, stop=j == 1 and part is lo)
                    last.then_inc(unit_used, 1)
                    pe.wait_ge(unit_used, n + 1)
                    pe.sem_inc(y_done, 1)

        @block.scalar
        def _(act):
            A = nc.scalar.activation

            def split_high(kind, e):
                n = number[kind, e]
                arrived(act, n)
                if n >= SPLITS:
                    act.wait_ge(unit_used, n - SPLITS + 1)
                A(hi[:, n % SPLITS, :], raw[:, n % URING, :], ACT.Copy).then_inc(hi_ready, 1)

            for q in range(BATCH // 2):
                act.wait_ge(selT_ps, q + 1)
                A(selT[:, 2 * q:2 * q + 2, :], ps_y[:, q % 2, :].rearrange("p (e n) -> p e n", e=2),
                  ACT.Copy).then_inc(selT_ready, 1)
            act.wait_ge(cw_ps, 1)
            A(cw[:, :, :], t.ps_b[:, 1, :].rearrange("p (e s) -> p e s", s=SLOTS), ACT.Copy).then_inc(cw_ready, 1)
            for k in range(NK):
                act.wait_ge(xt_ps, k + 1)
                A(XT[:, k, :, 0:SLOTS], acc[:, 2 * (k % 2), :].rearrange("p (e s) -> p e s", s=SLOTS),
                  ACT.Copy).then_inc(xt_hi, 1)
                if k in (2, 5):
                    split_high("A" if k == 2 else "B", 0)
            for e in range(BATCH + 2):
                if e >= 2:
                    act.wait_ge(y_done, e - 1)
                    if e >= 3:
                        act.wait_ge(s_done, e - 2)
                    A(yhi[:, :], ps_y.rearrange("p b n -> p (b n)"), ACT.Copy).then_inc(yhi_done, 1)
                if 1 <= e <= BATCH:
                    split_high("C", e - 1)
                if e < BATCH:
                    act.wait_ge(h_done, e + 1)
                    if e:
                        act.wait_ge(ht_done, e)
                    A(h[:, :], ps_h, ACT.Copy).then_inc(h_copied, 1)
                if e + 1 < BATCH:
                    split_high("A", e + 1)
                if e < BATCH:
                    act.wait_ge(ht_done, e + 1)
                    if e:
                        act.wait_ge(hid_ready, e)
                    A(act1[:, :, :], ps_ht[:, 0:2 * SLOTS].rearrange("p (j s) -> p j s", s=SLOTS),
                      ACT.Silu).then_inc(silu_done, 1)
                if e + 1 < BATCH:
                    split_high("B", e + 1)

        @block.vector
        def _(dve):
            ch = Chain(dve, dch)
            v = nc.vector

            def split_low(kind, e):
                n = number[kind, e]
                dve.wait_ge(hi_ready, n + 1)
                v.tensor_tensor(lo[:, n % SPLITS, :], raw[:, n % URING, :], hi[:, n % SPLITS, :].bitcast(F32),
                                ALU.subtract).then_inc(lo_ready, 1)

            for tt in range(NT):
                for o in (0, SLOTS):
                    v.tensor_tensor(sel[:, tt, :, o:o + SLOTS], bc(m.slot[:, :], 1, BATCH),
                                    bc(m.place[:, tt, ready_batch], 2, SLOTS), ALU.is_equal).then_inc(sel_ready, 1)
            dve.wait_ge(sel_ready, 2 * NT)
            for tt in range(NT):
                v.tensor_tensor(selw[tt][:, :].rearrange("p (e s) -> p e s", s=SLOTS), sel[:, tt, :, 0:SLOTS].bitcast(F32), bc(m.comb[:, tt, ready_batch], 2, SLOTS),
                                ALU.mult).then_inc(selw_ready, 1)
            for k in range(NK):
                dve.wait_ge(xt_ps, k + 1)
                v.tensor_copy(XT[:, k, :, SLOTS:], acc[:, 2 * (k % 2) + 1, :].rearrange("p (e s) -> p e s", s=SLOTS)
                              ).then_inc(xt_lo, 1)
                if k in (3, 6):
                    split_low("A" if k == 3 else "B", 0)
            for e in range(BATCH + 2):
                if e >= 2:
                    dve.wait_ge(yhi_done, e - 1)
                    v.tensor_tensor(ylo[:, :], ps_y.rearrange("p b n -> p (b n)"), yhi[:, :].bitcast(F32),
                                    ALU.subtract).then_inc(ylo_done, 1)
                if 1 <= e <= BATCH:
                    split_low("C", e - 1)
                if e + 1 < BATCH:
                    split_low("A", e + 1)
                if e < BATCH:
                    dve.wait_ge(ht_done, e + 1)
                    if e == 0:
                        dve.wait_ge(cw_ready, 1)
                    dve.wait_ge(silu_done, e + 1)
                    ch.after(v.tensor_tensor(u[:, :, :], ps_ht[:, 2 * SLOTS:].rearrange("p (j s) -> p j s", s=SLOTS),
                                             bc(cw[:, e, :], 1, 2), ALU.mult))
                    ch.after(v.tensor_tensor(u[:, :, :], u[:, :, :], act1[:, :, :], ALU.mult))
                    if e >= 2:
                        dve.wait_ge(y_done, e - 1)
                    ch.after(v.tensor_copy(hid[:, e % 2, :, 0:SLOTS], u[:, :, :]))
                    v.tensor_tensor(hid[:, e % 2, :, SLOTS:], u[:, :, :], hid[:, e % 2, :, 0:SLOTS].bitcast(F32),
                                    ALU.subtract).then_inc(hid_ready, 1)
                if e + 1 < BATCH:
                    split_low("B", e + 1)
            dve.wait_ge(s_done, BATCH)
            v.tensor_tensor(t.x[:, :, :].rearrange("p t n -> p (t n)"), acc[:, :, :].rearrange("p b n -> p (b n)"),
                            t.x[:, :, :].rearrange("p t n -> p (t n)"), ALU.add).then_inc(x_added, 1)
            dve.wait_ge(x_added, 1)
    ph.end()


def build_program(nc, d):
    with ExitStack() as ctx:
        t = tensors(nc, ctx)
        setup_constants(nc, t, d)
        with nc.Fori(0, DEPTH) as l:
            mixer(nc, t, d, l)
            if True:
                moe(nc, t, d, l)
        ph = Phase(nc, "store")
        stored = ph.sem("stored")
        with nc.Block() as block:
            @block.sync
            def _(sp):
                sp.dma_start(d.out[0].rearrange("(t p) n -> p t n", p=P), t.x[:, :, :]).then_inc(stored, 16)
                sp.wait_ge(stored, 16)
        ph.end()


_INS = ["x", "positions", "norm1_g", "w_in", "qn_g", "kn_g", "conv_w", "ml_gate_b", "w_branch", "w_out",
        "norm2_g", "w_rg", "b_rg", "w_re", "b_re", "w1", "w3", "w2"]


def kernel(**inputs):
    import numpy as _np
    import concourse.bacc as _bacc
    from concourse import mybir as _mybir
    from concourse.bass_utils import run_bass_kernel_spmd as _run

    nc = _bacc.Bacc("TRN2", target_bir_lowering=False, num_devices=1)
    arrays = {}

    class Dram:
        pass
    d = Dram()
    for name in _INS:
        a = _np.ascontiguousarray(inputs[name])
        arrays[f"in_{name}_dram"] = a
        d.__dict__[name] = nc.dram_tensor(f"in_{name}_dram", a.shape, _mybir.dt.from_np(a.dtype),
                                          kind="ExternalInput").ap()
    d.out = nc.dram_tensor("out_0_dram", (1, SEQ, D), _mybir.dt.float32, kind="ExternalOutput").ap()
    build_program(nc, d)
    r = _run(nc, [arrays], core_ids=[0])
    return r.results[0]["out_0_dram"]
```

```python
from contextlib import ExitStack

import numpy as np
import concourse.bass as bass
from concourse import mybir

ALU = mybir.AluOpType
ACT = mybir.ActivationFunctionType
AX = mybir.AxisListType
F32 = mybir.dt.float32
F32R = mybir.dt.float32r
I32 = mybir.dt.int32

P = 128
SEQ, D = 256, 1024
DEPTH = 2
NT = SEQ // P
NK = D // P
W = D // 2
NC = W // P
HD = 64
HEADS = W // HD
ML_HEADS = 4
ML_HD = W // ML_HEADS
ROT = HD // 8
THETA = 500000.0
EPS = 1e-6
NEG = -1e30
NG, NE, FE = 4, 32, D // 4
EPG = NE // NG
CHUNK = 512
RING = 4
COL_IF = 10 * W
COL_GATE = COL_IF + 2 * ML_HEADS

SLOTS = 32
MAX_ROUNDS = SEQ // SLOTS
BATCH = 8
BATCHES = NE // BATCH
PAIRS = NE // 2
UNIT = 2048
URING = RING * NK * CHUNK // UNIT
PART = UNIT // 2
SPLITS = 6


def bc(ap, axis, count):
    shape = list(ap.shape)
    shape.insert(axis, count)
    return ap.unsqueeze(axis).broadcast_to(shape)


class Chain:

    def __init__(self, eng, sem):
        self.eng, self.sem, self.n = eng, sem, 0

    def after(self, ins):
        self.n += 1
        ins.then_inc(self.sem, 1)
        self.eng.wait_ge(self.sem, self.n)


class Phase:

    def __init__(self, nc, tag):
        self.nc, self.tag, self.sems, self.ctx = nc, tag, [], ExitStack()

    def sem(self, name):
        s = self.ctx.enter_context(self.nc.semaphore(f"{self.tag}_{name}"))
        self.sems.append(s)
        return s

    def end(self):
        for s in self.sems:
            self.nc.sync.sem_clear(s)
        self.nc.all_engine_barrier()
        self.ctx.close()


def setup_constants(nc, t, d):
    ph = Phase(nc, "setup")
    loaded, raw, made, chain = ph.sem("x_loaded"), ph.sem("filled"), ph.sem("masks_made"), ph.sem("dve_chain")
    slot_ints, trig_ready, ang_ready = ph.sem("slot_ints"), ph.sem("trig_ready"), ph.sem("angles_ready")
    pos_in = ph.sem("positions_loaded")
    with nc.Block() as block:
        @block.sync
        def _(sp):
            sp.dma_start(t.x[:, :, :], d.x[0].rearrange("(t p) n -> p t n", p=P)).then_inc(loaded, 16)
            sp.dma_start(t.pos_i[:, :], d.positions[0].rearrange("(t p) -> p t", p=P), allow_slow_non_contiguous=True).then_inc(pos_in, 16)
            sp.wait_ge(loaded, 16)

        @block.gpsimd
        def _(pool):
            fills = [(t.ident, 0.0), (t.trineg, -1.0), (t.tri, 1.0), (t.tri_strict, 1.0), (t.neg_mask, 0.0),
                     (t.ones, 1.0), (t.negones, -1.0), (t.eps, EPS)]
            for buf, v in fills:
                nc.gpsimd.memset(buf[:, :], v).then_inc(raw, 1)
            nc.gpsimd.iota(t.index_i[:, :], pattern=[[1, NE]], base=0, channel_multiplier=0).then_inc(slot_ints, 1)
            pool.wait_ge(raw, len(fills))
            for buf, cmp, row, part, fill in [
                    (t.ident, ALU.not_equal, -1, 1, 1.0),
                    (t.trineg, ALU.is_ge, -1, 1, 0.0),
                    (t.tri, ALU.is_ge, 1, -1, 0.0),
                    (t.tri_strict, ALU.is_gt, 1, -1, 0.0),
                    (t.neg_mask, ALU.is_ge, -1, 1, NEG)]:
                nc.gpsimd.affine_select(out=buf[:, :], in_=buf[:, :], compare_op=cmp, fill=fill, base=0,
                                        pattern=[[row, P]], channel_multiplier=part).then_inc(made, 1)

        @block.vector
        def _(dve):
            ch = Chain(dve, chain)
            v = nc.vector
            dve.wait_ge(slot_ints, 1)
            v.tensor_copy(t.index[:, :], t.index_i[:, :])
            dve.wait_ge(made, 5)
            halves = t.ident[:, :].rearrange("p (e d s) -> p e d s", e=2, s=SLOTS)
            v.tensor_tensor(t.fold[:, :].rearrange("p (e s) -> p e s", e=2), halves[:, :, 0, :], halves[:, :, 1, :],
                            ALU.add)
            for i in range(ROT):
                f = float(np.power(np.float32(THETA), np.float32(-i) / np.float32(ROT)))
                v.memset(t.freq[:, i:i + 1], f)
            dve.wait_ge(pos_in, 16)
            ch.after(v.tensor_copy(t.pos[:, :], t.pos_i[:, :]))
            ch.after(v.tensor_tensor(t.ang[:, :, :], bc(t.pos[:, :], 2, ROT), bc(t.freq[:, :], 1, NT), ALU.mult))
            two_pi = 2.0 * np.pi
            c1 = 6.28125
            c2 = float(np.float32(np.round((two_pi - c1) * 2.0 ** 20) / 2.0 ** 20))
            c3 = float(np.float32(two_pi - c1 - c2))
            big = float(1.5 * 2 ** 23)
            ch.after(v.tensor_scalar(t.turn[:, :, :], t.ang[:, :, :], 1.0 / two_pi, big, ALU.mult, ALU.add))
            ch.after(v.tensor_scalar(t.turn[:, :, :], t.turn[:, :, :], -big, None, ALU.add))
            for c in (c1, c2, c3):
                ch.after(v.scalar_tensor_tensor(out=t.ang[:, :, :], in0=t.turn[:, :, :], scalar=-c,
                                                in1=t.ang[:, :, :], op0=ALU.mult, op1=ALU.add))
            ch.after(v.tensor_scalar(t.turn[:, :, :], t.ang[:, :, :], np.pi / 2, -two_pi, ALU.is_gt, ALU.mult))
            ch.after(v.scalar_tensor_tensor(out=t.turn[:, :, :], in0=t.ang[:, :, :], scalar=np.pi / 2,
                                            in1=t.turn[:, :, :], op0=ALU.add, op1=ALU.add))
            lim = 3.1415925
            for buf in (t.ang, t.turn):
                v.tensor_scalar(buf[:, :, :], buf[:, :, :], lim, -lim, ALU.min, ALU.max).then_inc(ang_ready, 1)
            dve.wait_ge(ang_ready, 2)

        @block.scalar
        def _(act):
            act.wait_ge(ang_ready, 2)
            nc.scalar.activation(t.sin[:, :, :], t.ang[:, :, :], ACT.Sin).then_inc(trig_ready, 1)
            nc.scalar.activation(t.cos[:, :, :], t.turn[:, :, :], ACT.Sin).then_inc(trig_ready, 1)
            act.wait_ge(trig_ready, 2)
    ph.end()



def mixer(nc, t, d, l):
    ph = Phase(nc, "mix")
    mem = ExitStack()
    S = ph.sem

    def sb(name, shape, dt=F32):
        return mem.enter_context(nc.sbuf_tensor(name, shape, dt))

    xs = sb("mix_scaled_x", [P, NT, D])
    xnT = sb("mix_xnT", [P, NK, SEQ])
    sbq, sbk, sbv = sb("sb_qT", [P, NC, SEQ]), sb("sb_kT", [P, NC, SEQ]), sb("sb_v", [P, NT, W])
    mbqk = sb("mb_qk", [P, 2, NT, W])
    mbqkT, mbv = sb("mb_qkT", [P, 2, NC, SEQ]), sb("mb_v", [P, NT, W])
    mlpre = sb("ml_pre", [P, 2 * NC, SEQ + 3])
    mlqk, mlv = sb("ml_qk", [P, 2 * NC, SEQ]), sb("ml_v", [P, NT, W])
    gates = sb("gates", [P, NC + 3 * NK, SEQ])
    brT = sb("branchT", [P, 3, NC, SEQ])
    ta, tb, tw = sb("attn_a", [P, 4, 384]), sb("attn_b", [P, 4, 384]), sb("attn_w", [P, 4, 384])
    gain, convw, convr = sb("gain1", [P, NK]), sb("conv_w", [P, 4 * 2 * NC]), sb("conv_rows", [4 * 2 * NC, P])
    qkg, mlb, wif = sb("qk_gain", [P, 2, HD]), sb("ml_bias", [P, 2 * ML_HEADS]), sb("w_if", [P, NK, 2 * ML_HEADS])
    ms, rs = sb("mean_sq", [P, NT]), sb("rstd", [P, NT])
    hss, hrs = sb("head_sq", [P, 2, NT * HEADS]), sb("head_rstd", [P, 2, NT * HEADS])
    r4 = sb("rot_tmp", [P, 4, NT, HEADS, ROT])
    mxb, nmx, sums, rsum = (sb(n, [P, 4, 2]) for n in ("row_max", "neg_max", "row_sum", "inv_sum"))
    iff, lf, lft, Fc, av = (sb(n, [P, NT, ML_HEADS * k]) for n, k in
                            (("if_pre", 2), ("log_f", 1), ("log_f_tmp", 1), ("F_cum", 1), ("a_row", 1)))
    flo, den, dneg = (sb(n, [P, 4, 2]) for n in ("floor", "den", "den_neg"))
    ring = t.ring

    smalls, gain_in = S("small_loads"), S("gain_in")
    xs_ready, xT_done, xnT_ready = S("xs_ready"), S("xT_done"), S("xnT_ready")
    slot_in = [S(f"weights_in{i}") for i in range(RING)]
    weights_used, proj_done, proj_copied = S("weights_used"), S("proj_done"), S("proj_copied")
    sq_done, rstd_ready = S("sum_sq_done"), S("rstd_ready")
    cw_t, cw_ready = S("convw_transposed"), S("convw_ready")
    conv_done, silu_done, pads = S("conv_done"), S("silu_done"), S("pads_zeroed")
    sb_z, sb_ln, sb_sp, sb_spm, sb_c, sb_w, sb_wm, sb_o, sb_e = (S(n) for n in (
        "sb_scores", "sb_log1p", "sb_softplus", "sb_softplus_masked", "sb_exponent", "sb_w",
        "sb_w_masked", "sb_out", "sb_out_copied"))
    mb_sq, mb_ss, mb_rs, mb_rot, mb_t, mb_tc = (S(n) for n in (
        "mb_squares", "mb_sums", "mb_rstd", "mb_rotated", "mb_transposed", "mb_T_copied"))
    mb_s, mb_m, mb_exp, mb_p, mb_pt, mb_w, mb_o, mb_e = (S(n) for n in (
        "mb_scores", "mb_max", "mb_exp", "mb_probs", "mb_probsT", "mb_probsT_copied", "mb_out", "mb_out_copied"))
    if_b, if_sp, lf_r, f_done, f_ready, abc, abc_used, d_ready, w_ready, fl_in, fl_ready = (S(n) for n in (
        "if_biased", "if_softplus", "log_f_ready", "F_done", "a_diag_ready", "a_rows", "a_rows_used", "d_ready",
        "w_ready", "floor_in", "floor_ready"))
    ml_s, ml_p, ml_pt, ml_w, ml_o, ml_e, sig = (S(n) for n in (
        "ml_scores", "ml_probs", "ml_probsT", "ml_probsT_copied", "ml_out", "ml_out_ready", "gates_ready"))
    merged, out_done, x_added = S("merged"), S("out_done"), S("x_added")
    dch, ach = S("dve_chain"), S("act_chain")

    psP, psA = t.ps_a, t.ps_b

    chunks = [("sbq", 0), ("sbk", W), ("sbv", 2 * W), ("if", COL_IF), ("mlq", 6 * W), ("mlk", 7 * W),
              ("mbq", 3 * W), ("mbk", 4 * W), ("mlv", 8 * W), ("mbv", 5 * W), ("mlo", 9 * W)]
    chunks += [(f"g{i}", COL_GATE + i * CHUNK) for i in range(3 * D // CHUNK)]
    index = {name: i for i, (name, _) in enumerate(chunks)}
    big = [(n, c) for n, c in chunks if n != "if"]
    stream = [("in", c) for _, c in big] + [("branch", b) for b in range(3)] + [("out", n) for n in range(2)]
    place = {n: i for i, (n, _) in enumerate(big)}
    first_branch, first_out = len(big), len(big) + 3
    token_major = {"sbv", "mlv", "mbv", "mbq", "mbk", "if"}
    w_in_l = d.w_in[bass.ds(l, 1)].rearrange("l (p k) n -> p (l k) n", p=P)
    w_br_l = d.w_branch[bass.ds(l, 1)].rearrange("l b (c p) n -> p (l b) c n", p=P)
    w_out_l = d.w_out[bass.ds(l, 1)].rearrange("l (j p) n -> p (l j) n", p=P)

    def slot_view(i, kind="in"):
        v = ring[:, i % RING, :]
        return v.rearrange("p (k n) -> p k n", k=NC if kind == "branch" else NK)

    def arrived(eng, i):
        eng.wait_ge(slot_in[i % RING], 16 * (i // RING + 1))

    SMALLS = 8
    with nc.Block() as block:
        @block.sync
        def _(sp):
            sp.dma_start(gain[:, :], d.norm1_g[bass.ds(l, 1)].rearrange("l (p k) -> p (l k)", k=NK)).then_inc(
                gain_in, 16)
            for i, (kind, c) in enumerate(stream):
                if i == 1:
                    for src, dst in [
                            (d.qn_g[bass.ds(l, 1)].partition_broadcast(P).rearrange("p l n -> p (l n)"), qkg[:, 0, :]),
                            (d.kn_g[bass.ds(l, 1)].partition_broadcast(P).rearrange("p l n -> p (l n)"), qkg[:, 1, :]),
                            (d.ml_gate_b[bass.ds(l, 1)].partition_broadcast(P).rearrange("p l n -> p (l n)"),
                             mlb[:, :]),
                            (w_in_l[:, :, COL_IF:COL_IF + 2 * ML_HEADS], wif[:, :, :])]:
                        sp.dma_start(dst, src).then_inc(smalls, 16)
                    for j in range(4):
                        sp.dma_start(convr[8 * j:8 * j + 8, :], d.conv_w[bass.ds(l, 1), j, :].rearrange(
                            "l (c p) -> (l c) p", p=P)).then_inc(smalls, 16)
                if i >= RING:
                    sp.wait_ge(weights_used, i - RING + 1)
                src = {"in": lambda: w_in_l[:, :, c:c + CHUNK], "branch": lambda: w_br_l[:, c],
                       "out": lambda: w_out_l[:, :, c * CHUNK:(c + 1) * CHUNK]}[kind]()
                sp.dma_start(slot_view(i, kind), src).then_inc(slot_in[i % RING], 16)

        @block.gpsimd
        def _(pool):
            nc.gpsimd.memset(mlpre[:, :, 0:3], 0.0).then_inc(pads, 1)
            for g in range(2):
                diag = [b[:, :, :].rearrange("p h (b q) -> p h b q", q=P)[:, :, 0:3:2, :] for b in (tb, tw)]
                for buf, before, after in ((diag[0], sb_sp, sb_spm), (diag[1], sb_w, sb_wm)):
                    pool.wait_ge(before, g + 1)
                    for half in range(2):
                        nc.gpsimd.affine_select(out=buf[:, :, half, :], in_=buf[:, :, half, :], compare_op=ALU.is_gt,
                                                fill=0.0, base=0, pattern=[[0, 4], [1, P]],
                                                channel_multiplier=-1).then_inc(after, 1)

        @block.tensor
        def _(pe):
            mm, tr = nc.tensor.matmul, nc.tensor.transpose

            pe.wait_ge(xs_ready, 1)
            for b in range(4):
                for k in (2 * b, 2 * b + 1):
                    for tt in range(NT):
                        o = (k % 2) * SEQ + tt * P
                        last = tr(psP[:, b, o:o + P], xs[:, tt, k::NK], t.ident[:, :])
                last.then_inc(xT_done, 1)
            pe.wait_ge(xnT_ready, 4)

            def project(name):
                i = index[name]
                pair = psP[:, 2 * (i % 2):2 * (i % 2) + 2, :]
                if i >= 2:
                    pe.wait_ge(proj_copied, i - 1)
                if name == "if":
                    w = wif[:, :, :]
                else:
                    arrived(pe, place[name])
                    w = slot_view(place[name])
                if name in token_major:
                    n = w.shape[2]
                    for tt in range(NT):
                        for k in range(NK):
                            last = mm(pair[:, tt, 0:n], xnT[:, k, tt * P:(tt + 1) * P], w[:, k, :],
                                      start=k == 0, stop=k == NK - 1)
                else:
                    for s in range(4):
                        for k in range(NK):
                            last = mm(pair[:, s // 2, (s % 2) * SEQ:(s % 2 + 1) * SEQ], w[:, k, s * P:(s + 1) * P],
                                      xnT[:, k, :], start=k == 0, stop=k == NK - 1)
                last.then_inc(proj_done, 1)
                if name != "if":
                    pe.wait_ge(proj_done, i + 1)
                    pe.sem_inc(weights_used, 1)

            def head(h):
                return 64 * (h % 2), h // 2

            def sb_scores(g):
                pe.wait_ge(proj_copied, index["sbk"] + 1)
                if g == 0:
                    pe.wait_ge(cw_ready, 1)
                else:
                    pe.wait_ge(sb_e, g)
                for hh in range(4):
                    o, c = head(4 * g + hh)
                    mm(psA[:, hh, 0:256], sbk[o:o + HD, c, 0:P], sbq[o:o + HD, c, :], start=True, stop=True)
                    last = mm(psA[:, hh, 256:384], sbk[o:o + HD, c, P:], sbq[o:o + HD, c, P:], start=False, stop=True,
                              skip_group_check=True)
                last.then_inc(sb_z, 1)

            def sb_cumsum(g):
                pe.wait_ge(sb_spm, 2 * (g + 1))
                for hh in range(4):
                    mm(psA[:, hh, 0:256], t.trineg[:, :], tb[:, hh, 0:256], start=False, stop=True,
                       skip_group_check=True)
                    mm(psA[:, hh, P:256], t.negones[:, :], tb[:, hh, 256:384], start=False, stop=True,
                       skip_group_check=True)
                    last = mm(psA[:, hh, 256:384], t.trineg[:, :], tb[:, hh, 256:384], start=False, stop=True,
                              skip_group_check=True)
                last.then_inc(sb_c, 1)

            def weigh_values(g, v, done):
                for hh in range(4):
                    h = 4 * g + hh
                    o, _ = head(h)
                    dst = psA[o:o + HD, hh - hh % 2, :]
                    mm(dst[:, 0:256], v[:, 0, h * HD:(h + 1) * HD], tw[:, hh, 0:256], start=True, stop=True,
                       skip_group_check=True)
                    last = mm(dst[:, P:256], v[:, 1, h * HD:(h + 1) * HD], tw[:, hh, 256:384], start=False, stop=True,
                              skip_group_check=True)
                last.then_inc(done, 1)

            def sb_out(g):
                pe.wait_ge(sb_wm, 2 * (g + 1))
                pe.wait_ge(proj_copied, index["sbv"] + 1)
                weigh_values(g, sbv, sb_o)

            def mb_transposes():
                pe.wait_ge(mb_rot, 2)
                pe.wait_ge(abc_used, 1)
                for q in range(2):
                    for c in range(NC):
                        for tt in range(NT):
                            o = (c % 2) * SEQ + tt * P
                            last = tr(psA[:, 2 * q + c // 2, o:o + P], mbqk[:, q, tt, c * P:(c + 1) * P], t.ident[:, :])
                last.then_inc(mb_t, 1)

            def mb_scores(g):
                pe.wait_ge(mb_tc, 2)
                if g:
                    pe.wait_ge(mb_e, g)
                for hh in range(4):
                    o, c = head(4 * g + hh)
                    q, k = mbqkT[o:o + HD, 0, c, :], mbqkT[o:o + HD, 1, c, :]
                    mm(psA[:, hh, 0:P], q[:, 0:P], k[:, 0:P], start=True, stop=True)
                    last = mm(psA[:, hh, P:384], q[:, P:], k, start=True, stop=True)
                last.then_inc(mb_s, 1)

            def probs_T(ready, count, done):
                pe.wait_ge(ready, count)
                for hh in range(4):
                    for b in range(3):
                        last = tr(psA[:, hh, b * P:(b + 1) * P], ta[:, hh, b * P:(b + 1) * P], t.ident[:, :])
                last.then_inc(done, 1)

            def mb_out(g):
                pe.wait_ge(mb_w, g + 1)
                pe.wait_ge(proj_copied, index["mbv"] + 1)
                weigh_values(g, mbv, mb_o)

            def ml_cumsum():
                pe.wait_ge(lf_r, 1)
                pe.wait_ge(sb_e, 2)
                mm(psA[:, 0, 0:4], t.tri[:, :], lf[:, 0, :], start=True, stop=True, skip_group_check=True)
                mm(psA[:, 0, 4:8], t.tri[:, :], lf[:, 1, :], start=False, stop=True, skip_group_check=True)
                mm(psA[:, 0, 4:8], t.ones[:, :], lf[:, 0, :], start=False, stop=True,
                   skip_group_check=True).then_inc(f_done, 1)

            def ml_rows():
                pe.wait_ge(f_ready, 1)
                for tt in range(NT):
                    dg = mbqkT[:, 0, :, :].rearrange("p c n -> p (c n)")[:, tt * 512:(tt + 1) * 512]
                    last = mm(psA[:, tt, :], t.ones[:, :], dg, start=True, stop=True)
                last.then_inc(abc, 1)

            def ml_scores():
                pe.wait_ge(silu_done, 2)
                pe.wait_ge(mb_e, 2)
                for c in range(NC):
                    mm(psA[:, c, 0:P], mlqk[:, c, 0:P], mlqk[:, NC + c, 0:P], start=True, stop=True)
                    last = mm(psA[:, c, P:384], mlqk[:, c, P:], mlqk[:, NC + c, :], start=True, stop=True)
                last.then_inc(ml_s, 1)

            def ml_out():
                pe.wait_ge(ml_w, 1)
                pe.wait_ge(proj_copied, index["mlv"] + 1)
                for c in range(NC):
                    mm(psA[:, c, 0:256], mlv[:, 0, c * P:(c + 1) * P], tw[:, c, 0:256], start=True, stop=False,
                       skip_group_check=True)
                    last = mm(psA[:, c, P:256], mlv[:, 1, c * P:(c + 1) * P], tw[:, c, 256:384], start=False,
                              stop=True, skip_group_check=True)
                last.then_inc(ml_o, 1)

            npj = [len(chunks)]

            def take_pair():
                n = npj[0]
                npj[0] += 1
                if n - 2 < len(chunks):
                    pe.wait_ge(proj_copied, n - 1)
                else:
                    k = n - 2 - len(chunks)
                    if k < 6:
                        pe.wait_ge(merged, k + 1)
                    else:
                        pe.wait_ge(x_added, k - 6 + 1)
                return psP[:, 2 * (n % 2):2 * (n % 2) + 2, :]

            def branch(b):
                i = first_branch + b
                arrived(pe, i)
                w = slot_view(i, "branch")
                pe.wait_ge(*((sb_e, 2), (mb_e, 2), (ml_e, 1))[b])
                for half in range(2):
                    pair = take_pair()
                    for s in range(4):
                        j = 4 * half + s
                        for c in range(NC):
                            last = mm(pair[:, s // 2, (s % 2) * SEQ:(s % 2 + 1) * SEQ], w[:, c, j * P:(j + 1) * P],
                                      brT[:, b, c, :], start=c == 0, stop=c == NC - 1)
                    last.then_inc(proj_done, 1)
                pe.wait_ge(proj_done, npj[0])
                pe.sem_inc(weights_used, 1)

            def out_proj(n):
                i = first_out + n
                arrived(pe, i)
                w = slot_view(i)
                if n == 0:
                    pe.wait_ge(merged, 6)
                pair = take_pair()
                for tt in range(NT):
                    for j in range(NK):
                        last = mm(pair[:, tt, :], gates[:, NC + j, tt * P:(tt + 1) * P], w[:, j, :],
                                  start=j == 0, stop=j == NK - 1)
                last.then_inc(out_done, 1)

            project("sbq"); project("sbk"); project("sbv")
            pe.wait_ge(smalls, 16 * SMALLS)
            tr(psA[:, 0, 0:32], convr[:, :], t.ident[0:32, 0:32]).then_inc(cw_t, 1)
            project("if")
            sb_scores(0); project("mlq"); sb_cumsum(0); project("mlk"); sb_out(0); project("mbq")
            sb_scores(1); project("mbk"); sb_cumsum(1); project("mlv"); sb_out(1); project("mbv")
            ml_cumsum(); project("mlo"); ml_rows(); project("g0"); mb_transposes(); project("g1")
            mb_scores(0); project("g2"); probs_T(mb_p, 1, mb_pt); project("g3"); mb_out(0)
            mb_scores(1); project("g4"); probs_T(mb_p, 2, mb_pt); project("g5"); mb_out(1)
            branch(0)
            ml_scores(); branch(1); probs_T(ml_p, 1, ml_pt)
            ml_out(); branch(2)
            out_proj(0); out_proj(1)

        @block.scalar
        def _(act):
            ch = Chain(act, ach)
            A = nc.scalar.activation

            for tt in range(NT):
                A(xs[:, tt, :], t.x[:, tt, :], ACT.Square, accum_out=ms[:, tt:tt + 1]).then_inc(sq_done, 1)
            act.wait_ge(sq_done, NT)
            ch.after(A(rs[:, :], ms[:, :], ACT.Ln, bias=t.eps[:, :], scale=1.0 / D))
            A(rs[:, :], rs[:, :], ACT.Exp, scale=-0.5).then_inc(rstd_ready, 1)

            dest = {"sbq": (sbq, 1.0 / 8), "sbk": (sbk, 1.0), "sbv": (sbv, 1.0), "mbv": (mbv, 1.0), "mlv": (mlv, 1.0)}

            def copy(name):
                i = index[name]
                act.wait_ge(proj_done, i + 1)
                src = psP[:, 2 * (i % 2):2 * (i % 2) + 2, :]
                scale = 1.0
                if name == "if":
                    src, dst = src[:, :, 0:2 * ML_HEADS], iff[:, :, :]
                elif name in dest:
                    buf, scale = dest[name]
                    dst = buf[:, :, :]
                    src = src.rearrange("p b (c n) -> p (b c) n", n=dst.shape[2])
                elif name in ("mbq", "mbk"):
                    dst = mbqk[:, int(name == "mbk"), :, :]
                elif name in ("mlq", "mlk"):
                    o = NC * int(name == "mlk")
                    dst = mlpre[:, o:o + NC, 3:]
                    src = src.rearrange("p b (c n) -> p (b c) n", n=SEQ)
                else:
                    o = 0 if name == "mlo" else NC + 4 * int(name[1:])
                    dst = gates[:, o:o + 4, :]
                    src = src.rearrange("p b (c n) -> p (b c) n", n=SEQ)
                A(dst, src, ACT.Copy, scale=scale).then_inc(proj_copied, 1)

            def sb_softplus(g):
                act.wait_ge(sb_z, g + 1)
                ch.after(A(ta[:, :, :], psA[:, :, 0:384], ACT.Abs))
                ch.after(A(ta[:, :, :], ta[:, :, :], ACT.Exp, scale=-1.0))
                A(ta[:, :, :], ta[:, :, :], ACT.Ln, bias=1.0).then_inc(sb_ln, 1)

            def sb_exp(g):
                act.wait_ge(sb_c, g + 1)
                if g:
                    act.wait_ge(sb_o, g)
                A(tw[:, :, :], psA[:, :, 0:384], ACT.Exp).then_inc(sb_w, 1)

            def mb_squares(q):
                act.wait_ge(proj_copied, index["mbk" if q else "mbq"] + 1)
                if q == 0:
                    act.wait_ge(xT_done, 4)
                A(xs[:, q, :], mbqk[:, q, :, :].rearrange("p t n -> p (t n)"), ACT.Square).then_inc(mb_sq, 1)

            def mb_rstd():
                act.wait_ge(mb_ss, 2)
                ch.after(A(hrs[:, :, :], hss[:, :, :], ACT.Ln, bias=t.eps[:, :], scale=1.0 / HD))
                A(hrs[:, :, :], hrs[:, :, :], ACT.Exp, scale=-0.5).then_inc(mb_rs, 1)

            def mb_copyT():
                act.wait_ge(mb_t, 1)
                for q, s in ((0, 1.0 / 8), (1, 1.0)):
                    A(mbqkT[:, q, :, :], psA[:, 2 * q:2 * q + 2, :].rearrange("p b (c n) -> p (b c) n", n=SEQ),
                      ACT.Copy, scale=s).then_inc(mb_tc, 1)

            def rows_exp(ready, count, sink, done):
                act.wait_ge(ready, count)
                for hh in range(4):
                    for r, (a, b) in enumerate(((0, P), (P, 384))):
                        acc = {"accum_out": sums[:, hh, r:r + 1]} if sink else {}
                        A(ta[:, hh, a:b], ta[:, hh, a:b], ACT.Exp, bias=nmx[:, hh, r:r + 1], **acc).then_inc(done, 1)

            def copy_w(src_done, count, done):
                act.wait_ge(src_done, count)
                A(tw[:, :, :], psA[:, :, 0:384], ACT.Copy).then_inc(done, 1)

            def if_softplus():
                act.wait_ge(if_b, 1)
                ch.after(A(lft[:, :, :], iff[:, :, 4:8], ACT.Abs))
                ch.after(A(lft[:, :, :], lft[:, :, :], ACT.Exp, scale=-1.0))
                A(lft[:, :, :], lft[:, :, :], ACT.Ln, bias=1.0).then_inc(if_sp, 1)

            copy("sbq"); copy("sbk"); copy("sbv")
            act.wait_ge(cw_t, 1)
            A(convw[:, :], psA[:, 0, 0:32], ACT.Copy).then_inc(cw_ready, 1)
            copy("if")
            sb_softplus(0); copy("mlq")
            sb_exp(0); copy("mlk")
            if_softplus()
            copy("mbq"); mb_squares(0); sb_softplus(1); copy("mbk"); mb_squares(1)
            sb_exp(1); mb_rstd(); copy("mlv"); copy("mbv")
            copy("mlo"); copy("g0"); mb_copyT(); copy("g1")
            copy("g2"); rows_exp(mb_m, 1, True, mb_exp); copy_w(mb_pt, 1, mb_w); copy("g3")
            copy("g4"); rows_exp(mb_m, 2, True, mb_exp)
            copy_w(mb_pt, 2, mb_w); copy("g5")
            act.wait_ge(proj_copied, len(chunks))
            A(gates[:, :, :], gates[:, :, :], ACT.Sigmoid).then_inc(sig, 1)
            for q in range(2):
                act.wait_ge(conv_done, q + 1)
                o = q * NC
                A(mlqk[:, o:o + NC, :], mlqk[:, o:o + NC, :], ACT.Silu).then_inc(silu_done, 1)
            act.wait_ge(fl_in, 1)
            A(flo[:, :, :], flo[:, :, :], ACT.Exp, scale=-1.0).then_inc(fl_ready, 1)
            rows_exp(d_ready, 1, False, w_ready)
            copy_w(ml_pt, 1, ml_w)

        @block.vector
        def _(dve):
            ch = Chain(dve, dch)
            v = nc.vector
            dve.wait_ge(rstd_ready, 1)
            dve.wait_ge(sq_done, NT)
            for tt in range(NT):
                last = v.tensor_scalar(xs[:, tt, :], t.x[:, tt, :], rs[:, tt:tt + 1], None, ALU.mult)
                ch.after(last)
            v.tensor_copy(t.junk[:, 0:1], rs[:, 0:1]).then_inc(xs_ready, 1)
            dve.wait_ge(gain_in, 16)
            for b in range(4):
                dve.wait_ge(xT_done, b + 1)
                v.tensor_tensor(xnT[:, 2 * b:2 * b + 2, :], psP[:, b, :].rearrange("p (k n) -> p k n", k=2),
                                bc(gain[:, 2 * b:2 * b + 2], 2, SEQ), ALU.mult).then_inc(xnT_ready, 1)

            def sb_softplus(g):
                dve.wait_ge(sb_ln, g + 1)
                if g:
                    dve.wait_ge(sb_c, g)
                v.scalar_tensor_tensor(out=tb[:, :, :], in0=psA[:, :, 0:384], scalar=0.0, in1=ta[:, :, :],
                                       op0=ALU.max, op1=ALU.add).then_inc(sb_sp, 1)

            def copy_out(g, b, ready, done):
                dve.wait_ge(ready, g + 1)
                v.tensor_copy(brT[:, b, 2 * g:2 * g + 2, :], psA[:, 0:3:2, 0:256]).then_inc(done, 1)

            def conv(q):
                dve.wait_ge(proj_copied, index["mlk" if q else "mlq"] + 1)
                dve.wait_ge(cw_ready, 1)
                dve.wait_ge(pads, 1)
                for j in range(4):
                    for c in range(q * NC, q * NC + NC):
                        w = convw[:, 8 * j + c:8 * j + c + 1]
                        src = mlpre[:, c, j:j + SEQ]
                        if j == 0:
                            last = v.tensor_scalar(mlqk[:, c, :], src, w, None, ALU.mult)
                        else:
                            last = v.scalar_tensor_tensor(out=mlqk[:, c, :], in0=src, scalar=w, in1=mlqk[:, c, :],
                                                          op0=ALU.mult, op1=ALU.add)
                    if j < 3:
                        ch.after(last)
                last.then_inc(conv_done, 1)

            def mb_norm(q):
                x = mbqk[:, q, :, :].rearrange("p t (h n) -> p (t h) n", n=HD)
                ch.after(v.tensor_tensor(x, x, bc(hrs[:, q, :], 2, HD), ALU.mult))
                ch.after(v.tensor_tensor(x, x, bc(qkg[:, q, :], 1, NT * HEADS), ALU.mult))
                x = mbqk[:, q, :, :].rearrange("p t (h n) -> p t h n", n=HD)
                x1, x2 = x[:, :, :, 0:ROT], x[:, :, :, ROT:2 * ROT]
                cos, sin = bc(t.cos[:, :, :], 2, HEADS), bc(t.sin[:, :, :], 2, HEADS)
                v.tensor_tensor(r4[:, 0], x1, cos, ALU.mult)
                v.tensor_tensor(r4[:, 1], x2, sin, ALU.mult)
                v.tensor_tensor(r4[:, 2], x1, sin, ALU.mult)
                ch.after(v.tensor_tensor(r4[:, 3], x2, cos, ALU.mult))
                v.tensor_tensor(x1, r4[:, 0], r4[:, 1], ALU.subtract)
                ch.after(v.tensor_tensor(x2, r4[:, 2], r4[:, 3], ALU.add))
                v.tensor_copy(t.junk[:, 0:1], rs[:, 0:1]).then_inc(mb_rot, 1)

            def row_max(floor):
                ch.after(v.tensor_reduce(mxb[:, :, 0], ta[:, :, 0:P], AX.X, ALU.max))
                ch.after(v.tensor_reduce(mxb[:, :, 1], ta[:, :, P:384], AX.X, ALU.max))
                if floor:
                    ch.after(v.tensor_scalar(mxb[:, :, :], mxb[:, :, :], 0.0, None, ALU.max))
                return v.tensor_scalar(nmx[:, :, :], mxb[:, :, :], -1.0, None, ALU.mult)

            def mb_softmax_in(g):
                dve.wait_ge(mb_s, g + 1)
                if g:
                    dve.wait_ge(mb_pt, g)
                nm = bc(t.neg_mask[:, :], 1, 4)
                v.tensor_tensor(ta[:, :, 0:P], psA[:, :, 0:P], nm, ALU.add)
                v.tensor_copy(ta[:, :, P:2 * P], psA[:, :, P:2 * P])
                ch.after(v.tensor_tensor(ta[:, :, 2 * P:], psA[:, :, 2 * P:384], nm, ALU.add))
                row_max(False).then_inc(mb_m, 1)

            def scale_rows(r, done):
                v.tensor_tensor(ta[:, :, 0:P], ta[:, :, 0:P], bc(r[:, :, 0], 2, P), ALU.mult)
                ch.after(v.tensor_tensor(ta[:, :, P:], ta[:, :, P:], bc(r[:, :, 1], 2, 2 * P), ALU.mult))
                v.tensor_copy(t.junk[:, 0:1], rs[:, 0:1]).then_inc(done, 1)

            def mb_normalise(g):
                dve.wait_ge(mb_exp, 8 * (g + 1))
                ch.after(v.reciprocal(rsum[:, :, :], sums[:, :, :]))
                scale_rows(rsum, mb_p)

            def if_bias():
                dve.wait_ge(proj_copied, index["if"] + 1)
                v.tensor_tensor(iff[:, :, :], iff[:, :, :], bc(mlb[:, :], 1, NT), ALU.add).then_inc(if_b, 1)

            def log_f():
                dve.wait_ge(if_sp, 1)
                v.scalar_tensor_tensor(out=lf[:, :, :], in0=iff[:, :, 4:8], scalar=0.0, in1=lft[:, :, :],
                                       op0=ALU.min, op1=ALU.subtract).then_inc(lf_r, 1)

            def a_diag():
                dve.wait_ge(f_done, 1)
                ch.after(v.tensor_copy(Fc[:, :, :], psA[:, 0, 0:8].rearrange("p (t h) -> p t h", t=NT)))
                ch.after(v.tensor_tensor(av[:, :, :], iff[:, :, 0:4], Fc[:, :, :], ALU.subtract))
                dst = mbqkT[:, 0, :, :].rearrange("p c (a n) -> p (c a) n", n=P)
                v.tensor_tensor(dst, bc(t.ident[:, :], 1, NT * ML_HEADS),
                                bc(av[:, :, :].rearrange("p t h -> p (t h)"), 2, P), ALU.mult).then_inc(f_ready, 1)

            def a_rows_copy():
                dve.wait_ge(abc, 1)
                v.tensor_copy(mbqkT[:, 1, :, :].rearrange("p c n -> p (c n)"),
                              psA[:, 0:2, :].rearrange("p b n -> p (b n)")).then_inc(abc_used, 1)

            if_bias()
            sb_softplus(0)
            conv(0)
            log_f()
            copy_out(0, 0, sb_o, sb_e)
            sb_softplus(1)
            conv(1)
            for q in range(2):
                dve.wait_ge(mb_sq, q + 1)
                v.tensor_reduce(hss[:, q, :], xs[:, q, :].rearrange("p (h n) -> p h n", n=HD), AX.X,
                                ALU.add).then_inc(mb_ss, 1)
            copy_out(1, 0, sb_o, sb_e)
            dve.wait_ge(mb_rs, 1)
            mb_norm(0)
            a_diag()
            mb_norm(1)
            dve.wait_ge(abc, 1)
            ml_d = xs[:, :, :].rearrange("p t n -> p (t n)")[:, 0:1536].rearrange("p (h n) -> p h n", n=384)
            row = [psA[:, tt, :].rearrange("p (h n) -> p h n", n=P) for tt in range(NT)]
            nm = bc(t.neg_mask[:, :], 1, 4)
            v.tensor_tensor(ml_d[:, :, 0:P], row[0], nm, ALU.add)
            v.tensor_copy(ml_d[:, :, P:2 * P], row[0])
            v.tensor_tensor(ml_d[:, :, 2 * P:], row[1], nm, ALU.add).then_inc(abc_used, 1)
            for g in range(2):
                mb_softmax_in(g)
                mb_normalise(g)
                copy_out(g, 1, mb_o, mb_e)
            dve.wait_ge(mb_pt, 2)
            dve.wait_ge(mb_exp, 16)
            ch.after(v.tensor_copy(ta[:, :, :], ml_d))
            row_max(True).then_inc(d_ready, 1)
            v.tensor_tensor(flo[:, :, :], mxb[:, :, :], Fc[:, :, :].rearrange("p t h -> p h t"),
                            ALU.add).then_inc(fl_in, 1)

            def merge(b):
                for half in range(2):
                    n = 2 * b + half
                    i = len(chunks) + n
                    dve.wait_ge(proj_done, i + 1)
                    ps = psP[:, 2 * (i % 2):2 * (i % 2) + 2, :].rearrange("p b (c n) -> p (b c) n", n=SEQ)
                    o = NC + b * NK + 4 * half
                    gb, g0 = gates[:, o:o + 4, :], gates[:, NC + 4 * half:NC + 4 * half + 4, :]
                    ins = v.tensor_tensor(gb, ps, gb, ALU.mult)
                    if b:
                        ch.after(ins)
                        ins = v.tensor_tensor(g0, g0, gb, ALU.add)
                    ins.then_inc(merged, 1)
                    dve.wait_ge(merged, n + 1)

            dve.wait_ge(sig, 1)
            merge(0)
            dve.wait_ge(ml_s, 1)
            dve.wait_ge(w_ready, 8)
            ch.after(v.scalar_tensor_tensor(out=ta[:, :, :], in0=psA[:, :, 0:384], scalar=float(ML_HD) ** -0.5,
                                            in1=ta[:, :, :], op0=ALU.mult, op1=ALU.mult))
            v.tensor_reduce(den[:, :, 0], ta[:, :, 0:P], AX.X, ALU.add)
            ch.after(v.tensor_reduce(den[:, :, 1], ta[:, :, P:384], AX.X, ALU.add))
            ch.after(v.tensor_scalar(dneg[:, :, :], den[:, :, :], -1.0, None, ALU.mult))
            ch.after(v.tensor_tensor(den[:, :, :], den[:, :, :], dneg[:, :, :], ALU.max))
            dve.wait_ge(fl_ready, 1)
            ch.after(v.tensor_tensor(den[:, :, :], den[:, :, :], flo[:, :, :], ALU.max))
            ch.after(v.reciprocal(den[:, :, :], den[:, :, :]))
            scale_rows(den, ml_p)
            merge(1)
            dve.wait_ge(ml_o, 1)
            v.tensor_tensor(brT[:, 2, :, :], psA[:, :, 0:256], gates[:, 0:NC, :], ALU.mult).then_inc(ml_e, 1)
            merge(2)
            for n in range(2):
                i = len(chunks) + 6 + n
                dve.wait_ge(out_done, n + 1)
                xh = t.x[:, :, n * CHUNK:(n + 1) * CHUNK]
                v.tensor_tensor(xh, psP[:, 2 * (i % 2):2 * (i % 2) + 2, :], xh, ALU.add).then_inc(x_added, 1)
            dve.wait_ge(x_added, 2)
    ph.end()
    mem.close()


def tensors(nc, ctx):
    class T:
        pass
    t = T()

    def sb(name, shape, dt=F32):
        return ctx.enter_context(nc.sbuf_tensor(name, shape, dt))
    t.x = sb("x_res", [P, NT, D])
    t.ring = sb("weight_ring", [P, RING, NK * CHUNK])
    t.ident, t.trineg, t.tri, t.tri_strict = (sb(n, [P, P]) for n in ("ident", "trineg", "tri", "tri_strict"))
    t.neg_mask, t.ones, t.negones = (sb(n, [P, P]) for n in ("neg_mask", "ones", "negones"))
    t.eps, t.junk = sb("eps", [P, 1]), sb("junk", [P, 1])
    t.fold, t.index, t.index_i = sb("fold", [P, 2 * SLOTS]), sb("index", [P, NE]), sb("index_i", [P, NE], I32)
    t.pos_i, t.pos, t.freq = sb("pos_i", [P, NT], I32), sb("pos", [P, NT]), sb("freq", [P, ROT])
    t.ang, t.turn, t.sin, t.cos = (sb(n, [P, NT, ROT]) for n in ("ang", "turn", "sin", "cos"))
    t.ps_a = ctx.enter_context(nc.psum_tensor("ps_a", [P, 4, 512], F32))
    t.ps_b = ctx.enter_context(nc.psum_tensor("ps_b", [P, 4, 512], F32))
    t.ps_x = t.ps_b[:, 1, :]
    return t



def route(nc, t, d, l, m, prefetch):
    ph = Phase(nc, "route")
    mem = ExitStack()
    S = ph.sem

    def sb(name, shape, dt=F32):
        return mem.enter_context(nc.sbuf_tensor(name, shape, dt))

    NR = NG + NE
    gain, xn, xnT = sb("gain2", [P, D]), sb("xn2", [P, NT, D]), sb("xn2T", [P, NK, SEQ])
    wr, br, lg = sb("w_router", [P, NK, NR]), sb("b_router", [P, NR]), sb("logits", [P, NT, NR])
    ms, rs = sb("mean_sq2", [P, NT]), sb("rstd2", [P, NT])
    gmax, gsum, kmin, m1, m2, w1, w2, er = (sb(n, [P, NT]) for n in (
        "group_max", "group_sum", "key_min", "first_max", "second_max", "first_w", "second_w", "max_ratio"))
    gexp, ohg, keyg = (sb(n, [P, NT, NG]) for n in ("group_exp", "group_pick", "group_key"))
    em, key, oh1, oh2, A = (sb(n, [P, NT, NE]) for n in (
        "group_logits", "expert_key", "first_pick", "second_pick", "assigned"))
    nmax, cmp = sb("most_tokens", [P, 1]), sb("over", [P, MAX_ROUNDS - 1])

    smalls, sq_done, rstd_ready, xn_ready, hi_done, xnT_ps, xnT_ready = (S(n) for n in (
        "small_loads", "sum_sq_done", "rstd_ready", "xn_ready", "xn_high_done", "xT_done", "xnT_ready"))
    logits_done, gexp_in, gexp_done, er_in, er_done, picked, counted, dch, ach = (S(n) for n in (
        "logits_done", "group_exp_in", "group_exp_done", "ratio_in", "ratio_done", "picked", "counted",
        "dve_chain", "act_chain"))

    with nc.Block() as block:
        @block.sync
        def _(sp):
            L = bass.ds(l, 1)
            for src, dst in [
                    (d.norm2_g[L].partition_broadcast(P).rearrange("p l n -> p (l n)"), gain[:, :]),
                    (d.w_rg[L].rearrange("l (p k) n -> p (l k) n", p=P), wr[:, :, 0:NG]),
                    (d.w_re[L].rearrange("l (p k) n -> p (l k) n", p=P), wr[:, :, NG:]),
                    (d.b_rg[L].partition_broadcast(P).rearrange("p l n -> p (l n)"), br[:, 0:NG]),
                    (d.b_re[L].partition_broadcast(P).rearrange("p l n -> p (l n)"), br[:, NG:])]:
                sp.dma_start(dst, src).then_inc(smalls, 16)
            prefetch(sp)

        @block.scalar
        def _(act):
            ch = Chain(act, ach)
            A_ = nc.scalar.activation
            for tt in range(NT):
                A_(xn[:, tt, :], t.x[:, tt, :], ACT.Square, accum_out=ms[:, tt:tt + 1]).then_inc(sq_done, 1)
            act.wait_ge(sq_done, NT)
            ch.after(A_(rs[:, :], ms[:, :], ACT.Ln, bias=t.eps[:, :], scale=1.0 / D))
            A_(rs[:, :], rs[:, :], ACT.Exp, scale=-0.5).then_inc(rstd_ready, 1)
            for b in range(4):
                act.wait_ge(xnT_ps, b + 1)
                A_(xnT[:, 2 * b:2 * b + 2, :], t.ps_a[:, b, :].rearrange("p (k n) -> p k n", k=2),
                   ACT.Copy).then_inc(xnT_ready, 1)
            for tt in range(NT):
                act.wait_ge(xn_ready, tt + 1)
                A_(m.xn_hi[:, tt, :], xn[:, tt, :], ACT.Copy).then_inc(hi_done, 1)
            act.wait_ge(gexp_in, 1)
            A_(gexp[:, :, :], gexp[:, :, :], ACT.Exp).then_inc(gexp_done, 1)
            act.wait_ge(er_in, 1)
            A_(er[:, :], er[:, :], ACT.Exp).then_inc(er_done, 1)

        @block.tensor
        def _(pe):
            mm = nc.tensor.matmul
            pe.wait_ge(xn_ready, NT)
            for b in range(4):
                for k in (2 * b, 2 * b + 1):
                    for tt in range(NT):
                        o = (k % 2) * SEQ + tt * P
                        last = nc.tensor.transpose(t.ps_a[:, b, o:o + P], xn[:, tt, k::NK], t.ident[:, :])
                last.then_inc(xnT_ps, 1)
            pe.wait_ge(smalls, 16 * 5)
            pe.wait_ge(xnT_ready, 4)
            for tt in range(NT):
                for k in range(NK):
                    last = mm(t.ps_b[:, tt, 0:NR], xnT[:, k, tt * P:(tt + 1) * P], wr[:, k, :],
                              start=k == 0, stop=k == NK - 1)
            last.then_inc(logits_done, 1)
            pe.wait_ge(picked, 1)
            o = t.ps_b[:, 2, :]
            mm(o[:, 0:NE], t.tri_strict[:, :], A[:, 0, :], start=True, stop=True, skip_group_check=True)
            mm(o[:, NE:2 * NE], t.tri_strict[:, :], A[:, 1, :], start=False, stop=True, skip_group_check=True)
            mm(o[:, NE:2 * NE], t.ones[:, :], A[:, 0, :], start=False, stop=True, skip_group_check=True)
            mm(o[:, 2 * NE:3 * NE], t.ones[:, :], A[:, 0, :], start=False, stop=True, skip_group_check=True)
            mm(o[:, 2 * NE:3 * NE], t.ones[:, :], A[:, 1, :], start=False, stop=True,
               skip_group_check=True).then_inc(counted, 1)

        @block.vector
        def _(dve):
            ch = Chain(dve, dch)
            v = nc.vector
            dve.wait_ge(rstd_ready, 1)
            dve.wait_ge(smalls, 16 * 5)
            for tt in range(NT):
                v.scalar_tensor_tensor(out=xn[:, tt, :], in0=t.x[:, tt, :], scalar=rs[:, tt:tt + 1], in1=gain[:, :],
                                       op0=ALU.mult, op1=ALU.mult).then_inc(xn_ready, 1)
            for tt in range(NT):
                dve.wait_ge(hi_done, tt + 1)
                ch.after(v.tensor_tensor(m.xn_lo[:, tt, :], xn[:, tt, :], m.xn_hi[:, tt, :].bitcast(F32),
                                         ALU.subtract))
            dve.wait_ge(logits_done, 1)
            ch.after(v.tensor_tensor(lg[:, :, :], t.ps_b[:, 0:NT, 0:NR], bc(br[:, :], 1, NT), ALU.add))

            def first_max(vals, mx, k, out, n):
                ch.after(v.tensor_reduce(mx[:, :], vals, AX.X, ALU.max))
                ch.after(v.tensor_tensor(k[:, :, :], vals, bc(mx[:, :], 2, n), ALU.is_equal))
                ch.after(v.scalar_tensor_tensor(out=k[:, :, :], in0=k[:, :, :], scalar=-64.0,
                                                in1=bc(t.index[:, 0:n], 1, NT), op0=ALU.mult, op1=ALU.add))
                ch.after(v.tensor_reduce(kmin[:, :], k[:, :, :], AX.X, ALU.min))
                ch.after(v.tensor_tensor(out[:, :, :], k[:, :, :], bc(kmin[:, :], 2, n), ALU.is_equal))

            groups = lg[:, :, 0:NG]
            first_max(groups, gmax, keyg, ohg, NG)
            v.tensor_tensor(gexp[:, :, :], groups, bc(gmax[:, :], 2, NG), ALU.subtract).then_inc(gexp_in, 1)
            ch.after(v.tensor_scalar(keyg[:, :, :], ohg[:, :, :], -NEG, NEG, ALU.mult, ALU.add))
            for tt in range(NT):
                last = v.tensor_tensor(em[:, tt, :].rearrange("p (g e) -> p g e", g=NG),
                                       lg[:, tt, NG:].rearrange("p (g e) -> p g e", g=NG),
                                       bc(keyg[:, tt, :], 2, EPG), ALU.add)
                ch.after(last)
            first_max(em[:, :, :], m1, key, oh1, NE)
            ch.after(v.scalar_tensor_tensor(out=em[:, :, :], in0=oh1[:, :, :], scalar=NEG, in1=em[:, :, :],
                                            op0=ALU.mult, op1=ALU.add))
            first_max(em[:, :, :], m2, key, oh2, NE)
            v.tensor_tensor(er[:, :], m2[:, :], m1[:, :], ALU.subtract).then_inc(er_in, 1)
            v.tensor_tensor(A[:, :, :], oh1[:, :, :], oh2[:, :, :], ALU.add).then_inc(picked, 1)
            dve.wait_ge(gexp_done, 1)
            ch.after(v.tensor_reduce(gsum[:, :], gexp[:, :, :], AX.X, ALU.add))
            dve.wait_ge(er_done, 1)
            ch.after(v.tensor_scalar(w1[:, :], er[:, :], 1.0, None, ALU.add))
            ch.after(v.tensor_tensor(w1[:, :], w1[:, :], gsum[:, :], ALU.mult))
            ch.after(v.reciprocal(w1[:, :], w1[:, :]))
            ch.after(v.tensor_tensor(w2[:, :], w1[:, :], er[:, :], ALU.mult))
            v.tensor_tensor(oh1[:, :, :], oh1[:, :, :], bc(w1[:, :], 2, NE), ALU.mult)
            ch.after(v.tensor_tensor(oh2[:, :, :], oh2[:, :, :], bc(w2[:, :], 2, NE), ALU.mult))
            ch.after(v.tensor_tensor(m.comb[:, :, :], oh1[:, :, :], oh2[:, :, :], ALU.add))
            dve.wait_ge(counted, 1)
            ch.after(v.scalar_tensor_tensor(out=m.place[:, :, :],
                                            in0=t.ps_b[:, 2, 0:2 * NE].rearrange("p (t e) -> p t e", t=NT), scalar=1.0,
                                            in1=A[:, :, :], op0=ALU.add, op1=ALU.mult))
            ch.after(v.tensor_scalar(m.place[:, :, :], m.place[:, :, :], -1.0, None, ALU.add))
            ch.after(v.tensor_reduce(nmax[:, :], t.ps_b[:, 2, 2 * NE:3 * NE], AX.X, ALU.max))
            for i in range(MAX_ROUNDS - 1):
                last = v.tensor_scalar(cmp[:, i:i + 1], nmax[:, :], float(SLOTS * (i + 1)), None, ALU.is_gt)
            ch.after(last)
            ch.after(v.tensor_reduce(nmax[:, :], cmp[:, :], AX.X, ALU.add))
            ch.after(v.tensor_scalar(m.rounds[:, :], nmax[0:1, :], 1.0, None, ALU.add))
    ph.end()
    mem.close()



class Gather:

    STEPS = [("rows", k) for k in range(NK)] + [("weights", 0)] + [("select", q) for q in range(2)]

    def __init__(self, nc, t, m, S):
        self.nc, self.t, self.m = nc, t, m
        self.given, self.taken = S("bank_given"), S("bank_taken")
        self.sel_ready, self.selw_ready, self.read = S("select_ready"), S("weighted_ready"), S("select_read")

    def dve_select(self, dve, n, batch, chain):
        nc, m, v = self.nc, self.m, self.nc.vector
        ex = slice(batch * BATCH, (batch + 1) * BATCH)
        if n:
            dve.wait_ge(self.read, n)
        for tt in range(NT):
            v.tensor_tensor(m.sel[:, tt].rearrange("p (e d) s -> p e d s", d=2),
                            bc(bc(self.t.index[:, 0:SLOTS], 1, 2), 1, BATCH),
                            bc(bc(m.place[:, tt, ex], 2, 2), 3, SLOTS), ALU.is_equal).then_inc(self.sel_ready, 1)
        dve.wait_ge(self.sel_ready, NT * (n + 1))
        for tt in range(NT):
            v.tensor_tensor(m.selw[:, tt], m.sel[:, tt, 0::2, :].bitcast(F32), bc(m.comb[:, tt, ex], 2, SLOTS),
                            ALU.mult).then_inc(self.selw_ready, 1)
        chain.after(v.tensor_scalar(m.place[:, :, ex], m.place[:, :, ex], -float(SLOTS), None, ALU.add))

    def pe_step(self, pe, n, i, buf, uses):
        nc, t, m = self.nc, self.t, self.m
        mm = nc.tensor.matmul
        kind, k = self.STEPS[i]
        if uses:
            pe.wait_ge(self.taken, uses)
        if kind == "rows":
            pe.wait_ge(self.sel_ready, NT * (n + 1))
            for part, xn in enumerate((m.xn_hi, m.xn_lo)):
                for tt in range(NT):
                    last = mm(t.ps_x[:, part * 256:(part + 1) * 256], xn[:, tt, k::NK], m.sel[:, tt, 0::2, :],
                              start=tt == 0, stop=tt == NT - 1)
        elif kind == "weights":
            pe.wait_ge(self.selw_ready, NT * (n + 1))
            for tt in range(NT):
                last = mm(t.ps_x[:, 0:256], t.ones[:, :], m.selw[:, tt].rearrange("p e s -> p (e s)"),
                          start=tt == 0, stop=tt == NT - 1)
        else:
            for j in range(2):
                for tt in range(NT):
                    o = j * SEQ + tt * P
                    e = 4 * (2 * k + j)
                    last = nc.tensor.transpose(t.ps_x[:, o:o + P], m.sel[:, tt, e:e + 4, :].rearrange(
                        "p e s -> p (e s)").bitcast(F32), t.ident[:, :])
        last.then_inc(self.given, 1)
        if i == len(self.STEPS) - 1:
            pe.wait_ge(self.given, uses + 1)
            pe.sem_inc(self.read, 1)

    def act_step(self, act, i, buf, uses):
        t, m = self.t, self.m
        A = self.nc.scalar.activation
        kind, k = self.STEPS[i]
        act.wait_ge(self.given, uses + 1)
        if kind == "rows":
            dst = m.XT[buf][:, k].rearrange("p (q b s) -> p q b s", b=3, s=2 * SLOTS)
            for part in range(2):
                last = A(dst[:, :, 0::2, part * SLOTS:(part + 1) * SLOTS],
                         t.ps_x[:, part * 256:(part + 1) * 256].rearrange("p (q b s) -> p q b s", b=2, s=SLOTS),
                         ACT.Copy)
        elif kind == "weights":
            last = A(m.cw[buf][:, :], t.ps_x[:, 0:256], ACT.Copy)
        else:
            last = A(m.selT[buf][:, 2 * k:2 * k + 2, :], t.ps_x[:, :].rearrange("p (q n) -> p q n", n=SEQ), ACT.Copy)
        last.then_inc(self.taken, 1)


def moe(nc, t, d, l):
    mem = ExitStack()

    class M:
        pass
    m = M()

    def sb(name, shape, dt=F32):
        return mem.enter_context(nc.sbuf_tensor(name, shape, dt))

    m.xn_hi, m.xn_lo = sb("xn_hi", [P, NT, D], F32R), sb("xn_lo", [P, NT, D], F32R)
    m.comb, m.place = sb("combine", [P, NT, NE]), sb("place", [P, NT, NE])
    m.rounds = sb("rounds", [1, 1], I32)
    m.XT = [sb(f"XT{i}", [P, NK, BATCH // 2 * 6 * SLOTS], F32R) for i in range(2)]
    m.sel, m.selw = sb("select", [P, NT, 2 * BATCH, SLOTS], F32R), sb("select_weighted", [P, NT, BATCH, SLOTS])
    m.selT = [sb(f"selectT{i}", [P, BATCH // 2, SEQ], F32R) for i in range(2)]
    m.cw = [sb(f"slot_weight{i}", [P, BATCH * SLOTS]) for i in range(2)]
    m.h, m.act1, m.u = sb("h", [P, 2 * FE]), sb("silu_h1", [P, 2, 2 * SLOTS]), sb("h3_weighted", [P, 2, 2 * SLOTS])
    m.hidf = [sb(f"hid_whole{i}", [P, 6 * SLOTS]) for i in range(2)]
    m.hid = [sb(f"hid_parts{i}", [P, 6 * SLOTS], F32R) for i in range(2)]
    m.yhi, m.ylo = sb("y_hi", [P, D], F32R), sb("y_lo", [P, D], F32R)
    pre = [mem.enter_context(nc.semaphore(f"units_ahead{i}")) for i in range(URING)]

    order, parts, steps = [], [], []

    def use_unit(kind, e):
        n = len(order)
        order.append((kind, e))
        for h in range(UNIT // PART) if kind != "C" else (1,):
            steps.append(("part", len(parts)))
            parts.append((n, kind, e, h))

    bank, gathers = 0, 0

    def use_bank(p):
        nonlocal bank, gathers
        n = p // (BATCH // 2)
        i = gathers - n * len(Gather.STEPS)
        if p < PAIRS and i < len(Gather.STEPS):
            steps.append(("gather", (n, i, bank)))
            bank += 1
            gathers += 1

    for p in range(PAIRS + 2):
        if p < PAIRS:
            for e in (2 * p, 2 * p + 1):
                use_unit("A", e)
                use_unit("B", e)
                if e % 2:
                    steps.append(("h", p))
                use_bank(p)
        if p >= 2:
            steps.append(("scatter", p - 2))
        if p < PAIRS:
            steps.append(("hT", (p, bank)))
            bank += 1
        if 1 <= p <= PAIRS:
            use_unit("C", 2 * p - 2)
            use_bank(p)
            use_unit("C", 2 * p - 1)
            steps.append(("y", p - 1))
        elif p == 0:
            use_bank(p)
    m.order, m.parts, m.steps = order, parts, steps

    def load(sp, n, sem):
        kind, e = order[n]
        dst = t.ring[:, :, :].rearrange("p a b -> p (a b)")[:, (n % URING) * UNIT:(n % URING + 1) * UNIT]
        L, X = bass.ds(l, 1), slice(e, e + 1)
        if kind == "C":
            src = d.w2[L, X].rearrange("l e (p j) n -> p (l e j) n", p=P)
            dst = dst.rearrange("p (j n) -> p j n", j=2)
            for j in range(2):
                sp.dma_start(dst[:, j, :], src[:, j, :]).then_inc(sem, 16)
        else:
            k0 = 0 if kind == "A" else 4
            dst = dst.rearrange("p (k n) -> p k n", k=4)
            for j, w in enumerate((d.w1, d.w3)):
                src = w[L, X].rearrange("l e (p k) n -> p (l e k) n", p=P)
                sp.dma_start(dst[:, :, j * FE:(j + 1) * FE], src[:, k0:k0 + 4, :]).then_inc(sem, 16)

    def prefetch(sp):
        for n in range(URING):
            load(sp, n, pre[n])

    route(nc, t, d, l, m, prefetch)

    ph = Phase(nc, "first")
    g = Gather(nc, t, m, ph.sem)
    zeroed, dch = ph.sem("zeroed"), ph.sem("dve_chain")
    with nc.Block() as block:
        @block.gpsimd
        def _(pool):
            for buf in m.XT:
                for k in range(NK):
                    nc.gpsimd.memset(buf[:, k].rearrange("p (q b s) -> p q b s", b=3, s=2 * SLOTS)[:, :, 1, :]
                                     .bitcast(F32), 0.0).then_inc(zeroed, 1)
            for buf in m.hid + m.hidf:
                nc.gpsimd.memset(buf[:, :].bitcast(F32), 0.0).then_inc(zeroed, 1)
            pool.wait_ge(zeroed, 2 * NK + 4)

        @block.vector
        def _(dve):
            g.dve_select(dve, 0, 0, Chain(dve, dch))

        @block.tensor
        def _(pe):
            for i in range(len(g.STEPS)):
                g.pe_step(pe, 0, i, 0, i)

        @block.scalar
        def _(act):
            for i in range(len(g.STEPS)):
                g.act_step(act, i, 0, i)
            act.wait_ge(g.taken, len(g.STEPS))
    ph.end()

    m.hi, m.lo = sb("w_hi", [P, SPLITS, PART], F32R), sb("w_lo", [P, SPLITS, PART], F32R)
    rounds = nc.values_load(m.rounds[0:1, 0:1], min_val=1, max_val=MAX_ROUNDS)
    with nc.Fori(0, rounds) as r:
        experts(nc, t, m, r, rounds, pre, load)
    for s in pre:
        nc.sync.sem_clear(s)
    nc.all_engine_barrier()
    mem.close()


def experts(nc, t, m, r, rounds, pre, load):
    ph = Phase(nc, "exp")
    S = ph.sem
    g = Gather(nc, t, m, S)
    later = [S(f"units_in{i}") for i in range(URING)]
    hi_ready, lo_ready, part_used = S("high_ready"), S("low_ready"), S("part_used")
    h_done, h_copied, ht_done, silu_done, hid_ready = (S(n) for n in (
        "h_done", "h_copied", "hT_done", "silu_done", "hid_ready"))
    y_done, yhi_done, ylo_done, s_done, x_added, dch = (S(n) for n in (
        "y_done", "y_high_done", "y_low_done", "scattered", "x_added", "dve_chain"))
    acc, ps_h, ps_x, ps_y = t.ps_a, t.ps_b[:, 0, :], t.ps_x, t.ps_b[:, 2:4, :]
    raw = t.ring[:, :, :].rearrange("p a b -> p (a b)").rearrange("p (u n) -> p u n", n=UNIT)
    order, parts, steps, hi, lo = m.order, m.parts, m.steps, m.hi, m.lo
    HALF = BATCH // 2
    last_part = {n: i for i, (n, _, _, _) in enumerate(parts)}

    def arrived(eng, n):
        if n < URING:
            eng.wait_ge(pre[n], 32)
        else:
            eng.wait_ge(later[n % URING], 32 * (n // URING))

    def raw_part(i):
        n, _, _, h = parts[i]
        return raw[:, n % URING, h * PART:(h + 1) * PART]

    with nc.Block() as block:
        @block.sync
        def _(sp):
            def slot_free(n):
                sp.wait_ge(lo_ready, last_part[n] + 1)
                if order[n][0] == "C":
                    sp.wait_ge(part_used, last_part[n] + 1)
            for n in range(URING, len(order)):
                slot_free(n - URING)
                load(sp, n, later[n % URING])
            with sp.If(r + 1 < rounds):
                for n in range(URING):
                    slot_free(len(order) - URING + n)
                    sp.sem_clear(pre[n])
                    load(sp, n, pre[n])

        @block.tensor
        def _(pe):
            mm = nc.tensor.matmul

            def use_part(i):
                _, kind, e, h = parts[i]
                p, j, buf = e // 2, e % 2, i % SPLITS
                o = 2 * j * SLOTS
                if (kind, j, h) == ("A", 0, 0) and p:
                    pe.wait_ge(h_copied, p)
                if kind == "C" and j == 0:
                    pe.wait_ge(hid_ready, p + 1)
                    if p:
                        pe.wait_ge(ylo_done, p)
                pe.wait_ge(hi_ready, i + 1)
                pe.wait_ge(lo_ready, i + 1)
                if kind == "C":
                    hidf, hid = m.hidf[p % 2][:, o:o + P], m.hid[p % 2][:, o:o + P]
                    for n2 in range(2):
                        c = n2 * 512
                        mm(ps_y[:, n2, :], hidf, raw[:, parts[i][0] % URING, c:c + 512], start=j == 0, stop=False)
                        mm(ps_y[:, n2, :], hid, hi[:, buf, c:c + 512], start=False, stop=False)
                        last = mm(ps_y[:, n2, :], hid, lo[:, buf, c:c + 512], start=False, stop=j == 1)
                else:
                    for k in range(2):
                        row = 4 * (kind == "B") + 2 * h + k
                        xT = m.XT[p // HALF % 2][:, row, 6 * (p % HALF) * SLOTS + o:][:, 0:P]
                        mm(ps_h, xT, hi[:, buf, k * 512:(k + 1) * 512], start=j == 0 and row == 0, stop=False)
                        last = mm(ps_h, xT, lo[:, buf, k * 512:(k + 1) * 512], start=False,
                                  stop=j == 1 and row == NK - 1)
                last.then_inc(part_used, 1)
                return i + 1

            for what, arg in steps:
                if what == "part":
                    used = use_part(arg)
                elif what in ("h", "y"):
                    pe.wait_ge(part_used, used)
                    pe.sem_inc(h_done if what == "h" else y_done, 1)
                elif what == "gather":
                    n, i, uses = arg
                    g.pe_step(pe, n, i, (n + 1) % 2, uses)
                elif what == "scatter":
                    p = arg
                    pe.wait_ge(yhi_done, p + 1)
                    pe.wait_ge(ylo_done, p + 1)
                    for tt in range(NT):
                        for n2 in range(2):
                            for y in (m.yhi, m.ylo):
                                last = mm(acc[:, 2 * tt + n2, :], m.selT[p // HALF % 2][:, p % HALF, tt * P:(tt + 1) * P],
                                          y[:, n2 * 512:(n2 + 1) * 512], start=p == 0 and y is m.yhi,
                                          stop=p == PAIRS - 1 and y is m.ylo)
                    last.then_inc(s_done, 1)
                elif what == "hT":
                    p, uses = arg
                    pe.wait_ge(h_copied, p + 1)
                    if uses:
                        pe.wait_ge(g.taken, uses)
                    for w in range(2):
                        for j in range(2):
                            o = (2 * w + j) * 2 * SLOTS
                            last = mm(ps_x[:, o:o + 2 * SLOTS], m.h[:, w * FE + j:(w + 1) * FE:2], t.fold[:, :],
                                      start=True, stop=True)
                    last.then_inc(g.given, 1)
                    pe.wait_ge(g.given, uses + 1)
                    pe.sem_inc(ht_done, 1)

        @block.scalar
        def _(act):
            A = nc.scalar.activation

            def split_high(i):
                if i >= len(parts):
                    return
                arrived(act, parts[i][0])
                if i >= SPLITS:
                    act.wait_ge(part_used, i - SPLITS + 1)
                A(hi[:, i % SPLITS, :], raw_part(i), ACT.Copy).then_inc(hi_ready, 1)

            for i in range(SPLITS):
                split_high(i)
            for what, arg in steps:
                if what == "part":
                    split_high(arg + SPLITS)
                elif what == "gather":
                    n, i, uses = arg
                    g.act_step(act, i, (n + 1) % 2, uses)
                elif what == "h":
                    act.wait_ge(h_done, arg + 1)
                    if arg:
                        act.wait_ge(ht_done, arg)
                    A(m.h[:, :], ps_h, ACT.Copy).then_inc(h_copied, 1)
                elif what == "hT":
                    p, _ = arg
                    act.wait_ge(ht_done, p + 1)
                    if p:
                        act.wait_ge(hid_ready, p)
                    A(m.act1[:, :, :], ps_x[:, 0:4 * SLOTS].rearrange("p (j s) -> p j s", j=2),
                      ACT.Silu).then_inc(silu_done, 1)
                elif what == "y":
                    act.wait_ge(y_done, arg + 1)
                    if arg:
                        act.wait_ge(s_done, arg)
                    A(m.yhi[:, :], ps_y.rearrange("p b n -> p (b n)"), ACT.Copy).then_inc(yhi_done, 1)

        @block.vector
        def _(dve):
            ch = Chain(dve, dch)
            v = nc.vector

            def split_low(i):
                if i >= len(parts):
                    return
                arrived(dve, parts[i][0])
                dve.wait_ge(hi_ready, i + 1)
                v.tensor_tensor(lo[:, i % SPLITS, :], raw_part(i), hi[:, i % SPLITS, :].bitcast(F32),
                                ALU.subtract).then_inc(lo_ready, 1)

            def blocks(buf):
                return buf[:, :].rearrange("p (b s) -> p b s", b=3)[:, 0::2, :]

            for i in range(SPLITS):
                split_low(i)
                if i == 1:
                    g.dve_select(dve, 0, 1, ch)
            for what, arg in steps:
                if what == "part":
                    split_low(arg + SPLITS)
                elif what == "gather" and arg[1] == len(g.STEPS) - 1 and arg[0] < BATCHES - 1:
                    g.dve_select(dve, arg[0] + 1, (arg[0] + 2) % BATCHES, ch)
                elif what == "hT":
                    p, _ = arg
                    dve.wait_ge(silu_done, p + 1)
                    cw = m.cw[p // HALF % 2][:, (p % HALF) * 2 * SLOTS:][:, 0:2 * SLOTS]
                    ch.after(v.tensor_tensor(m.u[:, :, :], ps_x[:, 4 * SLOTS:8 * SLOTS].rearrange(
                        "p (j s) -> p j s", j=2), bc(cw, 1, 2), ALU.mult))
                    v.sem_inc(g.taken, 1)
                    if p >= 2:
                        dve.wait_ge(y_done, p - 1)
                    hidf, hid = blocks(m.hidf[p % 2]), blocks(m.hid[p % 2])
                    two = "p (b s) -> p b s"
                    v.tensor_tensor(hidf[:, :, 0:SLOTS], m.u[:, 0, :].rearrange(two, b=2),
                                    m.act1[:, 0, :].rearrange(two, b=2), ALU.mult)
                    ch.after(v.tensor_tensor(m.u[:, 1, :], m.u[:, 1, :], m.act1[:, 1, :], ALU.mult))
                    ch.after(v.tensor_copy(hid[:, :, 0:SLOTS], m.u[:, 1, :].rearrange(two, b=2)))
                    v.tensor_tensor(hid[:, :, SLOTS:], m.u[:, 1, :].rearrange(two, b=2),
                                    hid[:, :, 0:SLOTS].bitcast(F32), ALU.subtract).then_inc(hid_ready, 1)
                elif what == "y":
                    dve.wait_ge(yhi_done, arg + 1)
                    v.tensor_tensor(m.ylo[:, :], ps_y.rearrange("p b n -> p (b n)"), m.yhi[:, :].bitcast(F32),
                                    ALU.subtract).then_inc(ylo_done, 1)
            dve.wait_ge(s_done, PAIRS)
            v.tensor_tensor(t.x[:, :, :].rearrange("p t n -> p (t n)"), acc[:, :, :].rearrange("p b n -> p (b n)"),
                            t.x[:, :, :].rearrange("p t n -> p (t n)"), ALU.add).then_inc(x_added, 1)
            dve.wait_ge(x_added, 1)
    ph.end()


def build_program(nc, d):
    with ExitStack() as ctx:
        t = tensors(nc, ctx)
        setup_constants(nc, t, d)
        with nc.Fori(0, DEPTH) as l:
            mixer(nc, t, d, l)
            if True:
                moe(nc, t, d, l)
        ph = Phase(nc, "store")
        stored = ph.sem("stored")
        with nc.Block() as block:
            @block.sync
            def _(sp):
                sp.dma_start(d.out[0].rearrange("(t p) n -> p t n", p=P), t.x[:, :, :]).then_inc(stored, 16)
                sp.wait_ge(stored, 16)
        ph.end()


_INS = ["x", "positions", "norm1_g", "w_in", "qn_g", "kn_g", "conv_w", "ml_gate_b", "w_branch", "w_out",
        "norm2_g", "w_rg", "b_rg", "w_re", "b_re", "w1", "w3", "w2"]


def kernel(**inputs):
    import numpy as _np
    import concourse.bacc as _bacc
    from concourse import mybir as _mybir
    from concourse.bass_utils import run_bass_kernel_spmd as _run

    nc = _bacc.Bacc("TRN2", target_bir_lowering=False, num_devices=1, dynamic_dma_scratch_size=2048)
    arrays = {}

    class Dram:
        pass
    d = Dram()
    for name in _INS:
        a = _np.ascontiguousarray(inputs[name])
        arrays[f"in_{name}_dram"] = a
        d.__dict__[name] = nc.dram_tensor(f"in_{name}_dram", a.shape, _mybir.dt.from_np(a.dtype),
                                          kind="ExternalInput").ap()
    d.out = nc.dram_tensor("out_0_dram", (1, SEQ, D), _mybir.dt.float32, kind="ExternalOutput").ap()
    build_program(nc, d)
    r = _run(nc, [arrays], core_ids=[0])
    return r.results[0]["out_0_dram"]
```

```python
from contextlib import ExitStack

import numpy as np
import concourse.bass as bass
from concourse import mybir

ALU = mybir.AluOpType
ACT = mybir.ActivationFunctionType
AX = mybir.AxisListType
F32 = mybir.dt.float32
F32R = mybir.dt.float32r
I32 = mybir.dt.int32

P = 128
SEQ, D = 256, 1024
DEPTH = 2
NT = SEQ // P
NK = D // P
W = D // 2
NC = W // P
HD = 64
HEADS = W // HD
ML_HEADS = 4
ML_HD = W // ML_HEADS
ROT = HD // 8
THETA = 500000.0
EPS = 1e-6
NEG = -1e30
NG, NE, FE = 4, 32, D // 4
EPG = NE // NG
CHUNK = 512
RING = 2
MIX_SPLITS = 5
COL_IF = 10 * W
COL_GATE = COL_IF + 2 * ML_HEADS

SLOTS = 32
MAX_ROUNDS = SEQ // SLOTS
BATCH = 8
BATCHES = NE // BATCH
PAIRS = NE // 2
UNIT = 2048
URING = 8
PART = UNIT // 2
SPLITS = 6


def bc(ap, axis, count):
    shape = list(ap.shape)
    shape.insert(axis, count)
    return ap.unsqueeze(axis).broadcast_to(shape)


class Chain:

    def __init__(self, eng, sem):
        self.eng, self.sem, self.n = eng, sem, 0

    def after(self, ins):
        self.n += 1
        ins.then_inc(self.sem, 1)
        self.eng.wait_ge(self.sem, self.n)


class Phase:

    def __init__(self, nc, tag):
        self.nc, self.tag, self.sems, self.ctx = nc, tag, [], ExitStack()

    def sem(self, name):
        s = self.ctx.enter_context(self.nc.semaphore(f"{self.tag}_{name}"))
        self.sems.append(s)
        return s

    def end(self):
        nc = self.nc
        engines = (nc.sync, nc.scalar, nc.vector, nc.gpsimd, nc.tensor)
        for i, s in enumerate(self.sems):
            engines[i % len(engines)].sem_clear(s)
        self.nc.all_engine_barrier()
        self.ctx.close()


def setup_constants(nc, t, d):
    ph = Phase(nc, "setup")
    loaded, raw, made, chain = ph.sem("x_loaded"), ph.sem("filled"), ph.sem("masks_made"), ph.sem("dve_chain")
    slot_ints, trig_ready, ang_ready = ph.sem("slot_ints"), ph.sem("trig_ready"), ph.sem("angles_ready")
    pos_in = ph.sem("positions_loaded")
    with nc.Block() as block:
        @block.sync
        def _(sp):
            sp.dma_start(t.x[:, :, :], d.x[0].rearrange("(t p) n -> p t n", p=P)).then_inc(loaded, 16)
            sp.dma_start(t.pos_i[:, :], d.positions[0].rearrange("(t p) -> p t", p=P), allow_slow_non_contiguous=True).then_inc(pos_in, 16)
            sp.wait_ge(loaded, 16)

        @block.gpsimd
        def _(pool):
            fills = [(t.ident, 0.0), (t.trineg, -1.0), (t.tri, 1.0), (t.tri_strict, 1.0), (t.neg_mask, 0.0),
                     (t.ones, 1.0), (t.negones, -1.0), (t.eps, EPS)]
            for buf, v in fills:
                nc.gpsimd.memset(buf[:, :], v).then_inc(raw, 1)
            nc.gpsimd.iota(t.index_i[:, :], pattern=[[1, NE]], base=0, channel_multiplier=0).then_inc(slot_ints, 1)
            pool.wait_ge(raw, len(fills))
            for buf, cmp, row, part, fill in [
                    (t.ident, ALU.not_equal, -1, 1, 1.0),
                    (t.trineg, ALU.is_ge, -1, 1, 0.0),
                    (t.tri, ALU.is_ge, 1, -1, 0.0),
                    (t.tri_strict, ALU.is_gt, 1, -1, 0.0),
                    (t.neg_mask, ALU.is_ge, -1, 1, NEG)]:
                nc.gpsimd.affine_select(out=buf[:, :], in_=buf[:, :], compare_op=cmp, fill=fill, base=0,
                                        pattern=[[row, P]], channel_multiplier=part).then_inc(made, 1)

        @block.vector
        def _(dve):
            ch = Chain(dve, chain)
            v = nc.vector
            dve.wait_ge(slot_ints, 1)
            v.tensor_copy(t.index[:, :], t.index_i[:, :])
            dve.wait_ge(made, 5)
            halves = t.ident[:, :].rearrange("p (e d s) -> p e d s", e=2, s=SLOTS)
            v.tensor_tensor(t.fold[:, :].rearrange("p (e s) -> p e s", e=2), halves[:, :, 0, :], halves[:, :, 1, :],
                            ALU.add)
            for i in range(ROT):
                f = float(np.power(np.float32(THETA), np.float32(-i) / np.float32(ROT)))
                v.memset(t.freq[:, i:i + 1], f)
            dve.wait_ge(pos_in, 16)
            ch.after(v.tensor_copy(t.pos[:, :], t.pos_i[:, :]))
            ch.after(v.tensor_tensor(t.ang[:, :, :], bc(t.pos[:, :], 2, ROT), bc(t.freq[:, :], 1, NT), ALU.mult))
            two_pi = 2.0 * np.pi
            c1 = 6.28125
            c2 = float(np.float32(np.round((two_pi - c1) * 2.0 ** 20) / 2.0 ** 20))
            c3 = float(np.float32(two_pi - c1 - c2))
            big = float(1.5 * 2 ** 23)
            ch.after(v.tensor_scalar(t.turn[:, :, :], t.ang[:, :, :], 1.0 / two_pi, big, ALU.mult, ALU.add))
            ch.after(v.tensor_scalar(t.turn[:, :, :], t.turn[:, :, :], -big, None, ALU.add))
            for c in (c1, c2, c3):
                ch.after(v.scalar_tensor_tensor(out=t.ang[:, :, :], in0=t.turn[:, :, :], scalar=-c,
                                                in1=t.ang[:, :, :], op0=ALU.mult, op1=ALU.add))
            ch.after(v.tensor_scalar(t.turn[:, :, :], t.ang[:, :, :], np.pi / 2, -two_pi, ALU.is_gt, ALU.mult))
            ch.after(v.scalar_tensor_tensor(out=t.turn[:, :, :], in0=t.ang[:, :, :], scalar=np.pi / 2,
                                            in1=t.turn[:, :, :], op0=ALU.add, op1=ALU.add))
            lim = 3.1415925
            for buf in (t.ang, t.turn):
                v.tensor_scalar(buf[:, :, :], buf[:, :, :], lim, -lim, ALU.min, ALU.max).then_inc(ang_ready, 1)
            dve.wait_ge(ang_ready, 2)

        @block.scalar
        def _(act):
            act.wait_ge(ang_ready, 2)
            nc.scalar.activation(t.sin[:, :, :], t.ang[:, :, :], ACT.Sin).then_inc(trig_ready, 1)
            nc.scalar.activation(t.cos[:, :, :], t.turn[:, :, :], ACT.Sin).then_inc(trig_ready, 1)
            act.wait_ge(trig_ready, 2)
    ph.end()



def mixer(nc, t, d, l):
    ph = Phase(nc, "mix")
    mem = ExitStack()
    S = ph.sem

    def sb(name, shape, dt=F32):
        return mem.enter_context(nc.sbuf_tensor(name, shape, dt))

    xs = sb("mix_scaled_x", [P, NT, D])
    aT = [sb(f"xnT_{n}", [P, NK, SEQ], F32R) for n in ("high", "low")]
    brT = [sb(f"branchT_{n}", [P, 3, NC, SEQ], F32R) for n in ("high", "low")]
    whi, wlo = (sb(f"w_{n}", [P, MIX_SPLITS, 2 * CHUNK], F32R) for n in ("high", "low"))
    sbq, sbk, sbv = sb("sb_qT", [P, NC, SEQ]), sb("sb_kT", [P, NC, SEQ]), sb("sb_v", [P, NT, W])
    mbqk = sb("mb_qk", [P, 2, NT, W])
    pre = sb("ml_pre_mb_qkT", [P, 2 * NC * (SEQ + 3)])
    mlpre = pre[:, :].rearrange("p (c n) -> p c n", n=SEQ + 3)
    mbqkT = pre[:, 0:2 * NC * SEQ].rearrange("p (q c n) -> p q c n", q=2, c=NC)
    mbv, mlv = (b[:, :, :].rearrange("p c n -> p (c n)").rearrange("p (t n) -> p t n", t=NT)
                for b in (sbk, sbq))
    mlqk = sb("ml_qk", [P, 2 * NC, SEQ])
    gates = sb("gates", [P, NC + 3 * NK, SEQ])
    xnT = gates[:, 0:NK, :]
    ta, tb, tw = sb("attn_a", [P, 4, 384]), sb("attn_b", [P, 4, 384]), sb("attn_w", [P, 4, 384])
    gain, convw, convr = sb("gain1", [P, NK]), sb("conv_w", [P, 4 * 2 * NC]), sb("conv_rows", [4 * 2 * NC, P])
    qkg, mlb, wif = sb("qk_gain", [P, 2, HD]), sb("ml_bias", [P, 2 * ML_HEADS]), sb("w_if", [P, NK, 2 * ML_HEADS])
    ms, rs = sb("mean_sq", [P, NT]), sb("rstd", [P, NT])
    hss, hrs = sb("head_sq", [P, 2, NT * HEADS]), sb("head_rstd", [P, 2, NT * HEADS])
    r4 = sb("rot_tmp", [P, 4, NT, HEADS, ROT])
    mxb, nmx, sums, rsum = (sb(n, [P, 4, 2]) for n in ("row_max", "neg_max", "row_sum", "inv_sum"))
    iff, lf, lft, Fc, av = (sb(n, [P, NT, ML_HEADS * k]) for n, k in
                            (("if_pre", 2), ("log_f", 1), ("log_f_tmp", 1), ("F_cum", 1), ("a_row", 1)))
    flo, den, dneg = (sb(n, [P, 4, 2]) for n in ("floor", "den", "den_neg"))
    ring = sb("weight_ring", [P, RING, NK * CHUNK])

    smalls, gain_in, xn_split = S("small_loads"), S("gain_in"), S("xn_split")
    xs_ready, xT_done, xnT_ready = S("xs_ready"), S("xT_done"), S("xnT_ready")
    slot_in = [S(f"weights_in{i}") for i in range(RING)]
    hi_ready, lo_ready, part_used = S("high_ready"), S("low_ready"), S("part_used")
    if_done, proj_copied, out_hi, xhi, merged_hi, merged_lo = (S(n) for n in (
        "if_done", "proj_copied", "branch_high", "xn_high", "merged_high", "merged_low"))
    sq_done, rstd_ready = S("sum_sq_done"), S("rstd_ready")
    cw_t, cw_ready = S("convw_transposed"), S("convw_ready")
    conv_done, silu_done, pads = S("conv_done"), S("silu_done"), S("pads_zeroed")
    sb_z, sb_ln, sb_sp, sb_spm, sb_c, sb_w, sb_wm, sb_o, sb_e = (S(n) for n in (
        "sb_scores", "sb_log1p", "sb_softplus", "sb_softplus_masked", "sb_exponent", "sb_w",
        "sb_w_masked", "sb_out", "sb_out_copied"))
    mb_sq, mb_ss, mb_rs, mb_rot, mb_t, mb_tc = (S(n) for n in (
        "mb_squares", "mb_sums", "mb_rstd", "mb_rotated", "mb_transposed", "mb_T_copied"))
    mb_s, mb_m, mb_exp, mb_p, mb_pt, mb_w, mb_o, mb_e = (S(n) for n in (
        "mb_scores", "mb_max", "mb_exp", "mb_probs", "mb_probsT", "mb_probsT_copied", "mb_out", "mb_out_copied"))
    if_b, if_sp, lf_r, f_done, f_ready, abc, abc_used, d_ready, w_ready, fl_in, fl_ready = (S(n) for n in (
        "if_biased", "if_softplus", "log_f_ready", "F_done", "a_diag_ready", "a_rows", "a_rows_used", "d_ready",
        "w_ready", "floor_in", "floor_ready"))
    ml_s, ml_p, ml_pt, ml_w, ml_o, ml_e, sig = (S(n) for n in (
        "ml_scores", "ml_probs", "ml_probsT", "ml_probsT_copied", "ml_out", "ml_out_ready", "gates_ready"))
    merged, x_added, ml_prod = S("merged"), S("x_added"), S("ml_product")
    dch, ach = S("dve_chain"), S("act_chain")

    psP, psA = t.ps_a, t.ps_b

    chunks = [("sbq", 0), ("sbk", W), ("sbv", 2 * W), ("if", COL_IF), ("mlq", 6 * W), ("mlk", 7 * W),
              ("mbq", 3 * W), ("mbk", 4 * W), ("mlv", 8 * W), ("mbv", 5 * W), ("mlo", 9 * W)]
    chunks += [(f"g{i}", COL_GATE + i * CHUNK) for i in range(3 * D // CHUNK)]
    index = {name: i for i, (name, _) in enumerate(chunks)}
    big = [(n, c) for n, c in chunks if n != "if"]
    stream = [("in", c) for _, c in big] + [("branch", b) for b in range(3)] + [("out", n) for n in range(2)]
    place = {n: i for i, (n, _) in enumerate(big)}
    first_branch, first_out = len(big), len(big) + 3
    token_major = {"sbv", "mlv", "mbv", "mbq", "mbk", "if"}
    w_in_l = d.w_in[bass.ds(l, 1)].rearrange("l (p k) n -> p (l k) n", p=P)
    w_br_l = d.w_branch[bass.ds(l, 1)].rearrange("l b (c p) n -> p (l b) c n", p=P)
    w_out_l = d.w_out[bass.ds(l, 1)].rearrange("l (j p) n -> p (l j) n", p=P)

    def slot_view(i, kind="in"):
        v = ring[:, i % RING, :]
        return v.rearrange("p (k n) -> p k n", k=NC if kind == "branch" else NK)

    PARTS = 4

    def raw_part(i):
        c, q = i // PARTS, i % PARTS
        kind = stream[c][0]
        v = slot_view(c, kind)
        if kind == "branch":
            return v[:, 2 * (q % 2):2 * (q % 2) + 2, (q // 2) * CHUNK:(q // 2 + 1) * CHUNK]
        return v[:, 2 * q:2 * q + 2, :]

    def part_buf(w, i):
        return w[:, i % MIX_SPLITS, :].rearrange("p (k n) -> p k n", k=2)

    def parts_done(name):
        return PARTS * (place[name] + 1)

    SMALLS = 8
    with nc.Block() as block:
        @block.sync
        def _(sp):
            sp.dma_start(gain[:, :], d.norm1_g[bass.ds(l, 1)].rearrange("l (p k) -> p (l k)", k=NK)).then_inc(
                gain_in, 16)
            for i, (kind, c) in enumerate(stream):
                if i == 1:
                    for src, dst in [
                            (d.qn_g[bass.ds(l, 1)].partition_broadcast(P).rearrange("p l n -> p (l n)"), qkg[:, 0, :]),
                            (d.kn_g[bass.ds(l, 1)].partition_broadcast(P).rearrange("p l n -> p (l n)"), qkg[:, 1, :]),
                            (d.ml_gate_b[bass.ds(l, 1)].partition_broadcast(P).rearrange("p l n -> p (l n)"),
                             mlb[:, :]),
                            (w_in_l[:, :, COL_IF:COL_IF + 2 * ML_HEADS], wif[:, :, :])]:
                        sp.dma_start(dst, src).then_inc(smalls, 16)
                    for j in range(4):
                        sp.dma_start(convr[8 * j:8 * j + 8, :], d.conv_w[bass.ds(l, 1), j, :].rearrange(
                            "l (c p) -> (l c) p", p=P)).then_inc(smalls, 16)
                if i >= RING:
                    sp.wait_ge(lo_ready, PARTS * (i - RING + 1))
                src = {"in": lambda: w_in_l[:, :, c:c + CHUNK], "branch": lambda: w_br_l[:, c],
                       "out": lambda: w_out_l[:, :, c * CHUNK:(c + 1) * CHUNK]}[kind]()
                sp.dma_start(slot_view(i, kind), src).then_inc(slot_in[i % RING], 16)

        @block.gpsimd
        def _(pool):
            nc.gpsimd.memset(mlpre[:, :, 0:3], 0.0).then_inc(pads, 1)
            for g in range(2):
                diag = [b[:, :, :].rearrange("p h (b q) -> p h b q", q=P)[:, :, 0:3:2, :] for b in (tb, tw)]
                for buf, before, after in ((diag[0], sb_sp, sb_spm), (diag[1], sb_w, sb_wm)):
                    pool.wait_ge(before, g + 1)
                    for half in range(2):
                        nc.gpsimd.affine_select(out=buf[:, :, half, :], in_=buf[:, :, half, :], compare_op=ALU.is_gt,
                                                fill=0.0, base=0, pattern=[[0, 4], [1, P]],
                                                channel_multiplier=-1).then_inc(after, 1)

        @block.tensor
        def _(pe):
            mm, tr = nc.tensor.matmul, nc.tensor.transpose

            pe.wait_ge(xs_ready, 1)
            for b in range(4):
                for k in (2 * b, 2 * b + 1):
                    for tt in range(NT):
                        o = (k % 2) * SEQ + tt * P
                        last = tr(psA[:, b, o:o + P], xs[:, tt, k::NK], t.ident[:, :])
                last.then_inc(xT_done, 1)

            def part(i):
                pe.wait_ge(hi_ready, i + 1)
                pe.wait_ge(lo_ready, i + 1)
                return part_buf(whi, i), part_buf(wlo, i)

            def by_token(i, pair, xT, q):
                hi, lo = part(i)
                for k in range(2):
                    row = 2 * q + k
                    for tt in range(NT):
                        xh, xl = (x[:, row, tt * P:(tt + 1) * P] for x in xT)
                        mm(pair[:, tt, :], xh, hi[:, k, :], start=row == 0, stop=False)
                        mm(pair[:, tt, :], xh, lo[:, k, :], start=False, stop=False)
                        last = mm(pair[:, tt, :], xl, hi[:, k, :], start=False, stop=row == NK - 1)
                last.then_inc(part_used, 1)

            def by_feature(i, pair, xT, q, rows):
                hi, lo = part(i)
                for k in range(2):
                    row = 2 * q + k
                    for s in range(4):
                        dst = pair[:, s // 2, (s % 2) * SEQ:(s % 2 + 1) * SEQ]
                        wh, wl = (w[:, k, s * P:(s + 1) * P] for w in (hi, lo))
                        xh, xl = (x[:, row, :] for x in xT)
                        mm(dst, wh, xh, start=row == 0 and s % 2 == 0, stop=False, skip_group_check=True)
                        mm(dst, wh, xl, start=False, stop=False, skip_group_check=True)
                        last = mm(dst, wl, xh, start=False, stop=row == rows - 1, skip_group_check=True)
                last.then_inc(part_used, 1)

            def project(name):
                i = index[name]
                pair = psP[:, 2 * (i % 2):2 * (i % 2) + 2, :]
                if i >= 2:
                    pe.wait_ge(proj_copied, i - 1)
                if name == "if":
                    for tt in range(NT):
                        for k in range(NK):
                            last = mm(pair[:, tt, 0:2 * ML_HEADS], xnT[:, k, tt * P:(tt + 1) * P], wif[:, k, :],
                                      start=k == 0, stop=k == NK - 1)
                    last.then_inc(if_done, 1)
                    return
                for q in range(PARTS):
                    if i == 0:
                        pe.wait_ge(xn_split, q + 1)
                    if name in token_major:
                        by_token(PARTS * place[name] + q, pair, aT, q)
                    else:
                        by_feature(PARTS * place[name] + q, pair, aT, q, NK)

            def head(h):
                return 64 * (h % 2), h // 2

            def sb_scores(g):
                pe.wait_ge(proj_copied, index["sbk"] + 1)
                if g == 0:
                    pe.wait_ge(cw_ready, 1)
                else:
                    pe.wait_ge(sb_e, g)
                for hh in range(4):
                    o, c = head(4 * g + hh)
                    mm(psA[:, hh, 0:256], sbk[o:o + HD, c, 0:P], sbq[o:o + HD, c, :], start=True, stop=True)
                    last = mm(psA[:, hh, 256:384], sbk[o:o + HD, c, P:], sbq[o:o + HD, c, P:], start=False, stop=True,
                              skip_group_check=True)
                last.then_inc(sb_z, 1)

            def sb_cumsum(g):
                pe.wait_ge(sb_spm, 2 * (g + 1))
                for hh in range(4):
                    mm(psA[:, hh, 0:256], t.trineg[:, :], tb[:, hh, 0:256], start=False, stop=True,
                       skip_group_check=True)
                    mm(psA[:, hh, P:256], t.negones[:, :], tb[:, hh, 256:384], start=False, stop=True,
                       skip_group_check=True)
                    last = mm(psA[:, hh, 256:384], t.trineg[:, :], tb[:, hh, 256:384], start=False, stop=True,
                              skip_group_check=True)
                last.then_inc(sb_c, 1)

            def weigh_values(g, v, done):
                for hh in range(4):
                    h = 4 * g + hh
                    o, _ = head(h)
                    dst = psA[o:o + HD, hh - hh % 2, :]
                    mm(dst[:, 0:256], v[:, 0, h * HD:(h + 1) * HD], tw[:, hh, 0:256], start=True, stop=True,
                       skip_group_check=True)
                    last = mm(dst[:, P:256], v[:, 1, h * HD:(h + 1) * HD], tw[:, hh, 256:384], start=False, stop=True,
                              skip_group_check=True)
                last.then_inc(done, 1)

            def sb_out(g):
                pe.wait_ge(sb_wm, 2 * (g + 1))
                pe.wait_ge(proj_copied, index["sbv"] + 1)
                weigh_values(g, sbv, sb_o)

            def mb_transposes():
                pe.wait_ge(mb_rot, 2)
                pe.wait_ge(abc_used, 1)
                for q in range(2):
                    for c in range(NC):
                        for tt in range(NT):
                            o = (c % 2) * SEQ + tt * P
                            last = tr(psA[:, 2 * q + c // 2, o:o + P], mbqk[:, q, tt, c * P:(c + 1) * P], t.ident[:, :])
                last.then_inc(mb_t, 1)

            def mb_scores(g):
                pe.wait_ge(mb_tc, 2)
                if g:
                    pe.wait_ge(mb_e, g)
                for hh in range(4):
                    o, c = head(4 * g + hh)
                    q, k = mbqkT[o:o + HD, 0, c, :], mbqkT[o:o + HD, 1, c, :]
                    mm(psA[:, hh, 0:P], q[:, 0:P], k[:, 0:P], start=True, stop=True)
                    last = mm(psA[:, hh, P:384], q[:, P:], k, start=True, stop=True)
                last.then_inc(mb_s, 1)

            def probs_T(ready, count, done):
                pe.wait_ge(ready, count)
                for hh in range(4):
                    for b in range(3):
                        last = tr(psA[:, hh, b * P:(b + 1) * P], ta[:, hh, b * P:(b + 1) * P], t.ident[:, :])
                last.then_inc(done, 1)

            def mb_out(g):
                pe.wait_ge(mb_w, g + 1)
                pe.wait_ge(proj_copied, index["mbv"] + 1)
                weigh_values(g, mbv, mb_o)

            def ml_cumsum():
                pe.wait_ge(lf_r, 1)
                pe.wait_ge(sb_e, 2)
                mm(psA[:, 0, 0:4], t.tri[:, :], lf[:, 0, :], start=True, stop=True, skip_group_check=True)
                mm(psA[:, 0, 4:8], t.tri[:, :], lf[:, 1, :], start=False, stop=True, skip_group_check=True)
                mm(psA[:, 0, 4:8], t.ones[:, :], lf[:, 0, :], start=False, stop=True,
                   skip_group_check=True).then_inc(f_done, 1)

            def ml_rows():
                pe.wait_ge(f_ready, 1)
                for tt in range(NT):
                    dg = mbqkT[:, 0, :, :].rearrange("p c n -> p (c n)")[:, tt * 512:(tt + 1) * 512]
                    last = mm(psA[:, tt, :], t.ones[:, :], dg, start=True, stop=True)
                last.then_inc(abc, 1)

            def ml_scores():
                pe.wait_ge(silu_done, 2)
                pe.wait_ge(mb_e, 2)
                for c in range(NC):
                    mm(psA[:, c, 0:P], mlqk[:, c, 0:P], mlqk[:, NC + c, 0:P], start=True, stop=True)
                    last = mm(psA[:, c, P:384], mlqk[:, c, P:], mlqk[:, NC + c, :], start=True, stop=True)
                last.then_inc(ml_s, 1)

            def ml_out():
                pe.wait_ge(ml_w, 1)
                pe.wait_ge(proj_copied, index["mlv"] + 1)
                for c in range(NC):
                    mm(psA[:, c, 0:256], mlv[:, 0, c * P:(c + 1) * P], tw[:, c, 0:256], start=True, stop=False,
                       skip_group_check=True)
                    last = mm(psA[:, c, P:256], mlv[:, 1, c * P:(c + 1) * P], tw[:, c, 256:384], start=False,
                              stop=True, skip_group_check=True)
                last.then_inc(ml_o, 1)

            npj = [len(chunks)]

            def take_pair():
                n = npj[0]
                npj[0] += 1
                if n - 2 < len(chunks):
                    pe.wait_ge(proj_copied, n - 1)
                else:
                    k = n - 2 - len(chunks)
                    if k < 6:
                        pe.wait_ge(merged, k + 1)
                    else:
                        pe.wait_ge(x_added, k - 6 + 1)
                return psP[:, 2 * (n % 2):2 * (n % 2) + 2, :]

            def branch(b, halves=(0, 1)):
                pe.wait_ge(*((sb_e, 2), (mb_e, 2), (ml_e, 1))[b])
                for half in halves:
                    pair = take_pair()
                    for q in range(2):
                        by_feature(PARTS * (first_branch + b) + 2 * half + q, pair, [x[:, b] for x in brT], q, NC)

            def out_proj(n):
                pair = take_pair()
                for q in range(PARTS):
                    if n == 0:
                        pe.wait_ge(merged_lo, q // 2 + 1)
                    by_token(PARTS * (first_out + n) + q, pair, aT, q)

            project("sbq"); project("sbk"); project("sbv")
            pe.wait_ge(smalls, 16 * SMALLS)
            tr(psA[:, 0, 0:32], convr[:, :], t.ident[0:32, 0:32]).then_inc(cw_t, 1)
            project("if")
            sb_scores(0); project("mlq"); sb_cumsum(0); project("mlk"); sb_out(0); project("mbq")
            sb_scores(1); project("mbk"); sb_cumsum(1); project("mlv"); sb_out(1); project("mbv")
            ml_cumsum(); project("mlo"); ml_rows(); project("g0"); mb_transposes(); project("g1")
            mb_scores(0); project("g2"); probs_T(mb_p, 1, mb_pt); project("g3"); mb_out(0)
            mb_scores(1); project("g4"); probs_T(mb_p, 2, mb_pt); project("g5"); mb_out(1)
            branch(0, [0]); ml_scores(); branch(0, [1]); probs_T(ml_p, 1, ml_pt); branch(1, [0]); ml_out()
            branch(1, [1]); branch(2)
            out_proj(0); out_proj(1)

        @block.scalar
        def _(act):
            ch = Chain(act, ach)
            A = nc.scalar.activation

            for tt in range(NT):
                A(xs[:, tt, :], t.x[:, tt, :], ACT.Square, accum_out=ms[:, tt:tt + 1]).then_inc(sq_done, 1)
            act.wait_ge(sq_done, NT)
            ch.after(A(rs[:, :], ms[:, :], ACT.Ln, bias=t.eps[:, :], scale=1.0 / D))
            A(rs[:, :], rs[:, :], ACT.Exp, scale=-0.5).then_inc(rstd_ready, 1)

            def split(count):
                for _ in range(count):
                    i = splits[0]
                    splits[0] += 1
                    if i >= PARTS * len(stream):
                        return
                    act.wait_ge(slot_in[i // PARTS % RING], 16 * (i // PARTS // RING + 1))
                    if i >= MIX_SPLITS:
                        act.wait_ge(part_used, i - MIX_SPLITS + 1)
                    A(part_buf(whi, i), raw_part(i), ACT.Copy).then_inc(hi_ready, 1)

            splits = [0]
            split(2)
            for b in range(4):
                act.wait_ge(xnT_ready, b + 1)
                A(aT[0][:, 2 * b:2 * b + 2, :], xnT[:, 2 * b:2 * b + 2, :], ACT.Copy).then_inc(xhi, 1)
            split(MIX_SPLITS - 2)

            def out_high(b, g, ready):
                act.wait_ge(ready, g + 1)
                A(brT[0][:, b, 2 * g:2 * g + 2, :], psA[:, 0:3:2, 0:256], ACT.Copy).then_inc(out_hi, 1)

            dest = {"sbq": (sbq, 1.0 / 8), "sbk": (sbk, 1.0), "sbv": (sbv, 1.0), "mbv": (mbv, 1.0), "mlv": (mlv, 1.0)}

            def copy(name):
                i = index[name]
                if name == "if":
                    act.wait_ge(if_done, 1)
                else:
                    act.wait_ge(part_used, parts_done(name))
                src = psP[:, 2 * (i % 2):2 * (i % 2) + 2, :]
                scale = 1.0
                if name == "if":
                    src, dst = src[:, :, 0:2 * ML_HEADS], iff[:, :, :]
                elif name in dest:
                    buf, scale = dest[name]
                    dst = buf[:, :, :]
                    src = src.rearrange("p b (c n) -> p (b c) n", n=dst.shape[2])
                elif name in ("mbq", "mbk"):
                    dst = mbqk[:, int(name == "mbk"), :, :]
                elif name in ("mlq", "mlk"):
                    o = NC * int(name == "mlk")
                    dst = mlpre[:, o:o + NC, 3:]
                    src = src.rearrange("p b (c n) -> p (b c) n", n=SEQ)
                else:
                    o = 0 if name == "mlo" else NC + 4 * int(name[1:])
                    dst = gates[:, o:o + 4, :]
                    src = src.rearrange("p b (c n) -> p (b c) n", n=SEQ)
                A(dst, src, ACT.Copy, scale=scale).then_inc(proj_copied, 1)

            def sb_softplus(g):
                act.wait_ge(sb_z, g + 1)
                ch.after(A(ta[:, :, :], psA[:, :, 0:384], ACT.Abs))
                ch.after(A(ta[:, :, :], ta[:, :, :], ACT.Exp, scale=-1.0))
                A(ta[:, :, :], ta[:, :, :], ACT.Ln, bias=1.0).then_inc(sb_ln, 1)

            def sb_exp(g):
                act.wait_ge(sb_c, g + 1)
                if g:
                    act.wait_ge(sb_o, g)
                A(tw[:, :, :], psA[:, :, 0:384], ACT.Exp).then_inc(sb_w, 1)

            def mb_squares(q):
                act.wait_ge(proj_copied, index["mbk" if q else "mbq"] + 1)
                if q == 0:
                    act.wait_ge(xT_done, 4)
                A(xs[:, q, :], mbqk[:, q, :, :].rearrange("p t n -> p (t n)"), ACT.Square).then_inc(mb_sq, 1)

            def mb_rstd():
                act.wait_ge(mb_ss, 2)
                ch.after(A(hrs[:, :, :], hss[:, :, :], ACT.Ln, bias=t.eps[:, :], scale=1.0 / HD))
                A(hrs[:, :, :], hrs[:, :, :], ACT.Exp, scale=-0.5).then_inc(mb_rs, 1)

            def mb_copyT():
                act.wait_ge(mb_t, 1)
                for q, s in ((0, 1.0 / 8), (1, 1.0)):
                    A(mbqkT[:, q, :, :], psA[:, 2 * q:2 * q + 2, :].rearrange("p b (c n) -> p (b c) n", n=SEQ),
                      ACT.Copy, scale=s).then_inc(mb_tc, 1)

            def rows_exp(ready, count, sink, done):
                act.wait_ge(ready, count)
                for hh in range(4):
                    for r, (a, b) in enumerate(((0, P), (P, 384))):
                        acc = {"accum_out": sums[:, hh, r:r + 1]} if sink else {}
                        A(ta[:, hh, a:b], ta[:, hh, a:b], ACT.Exp, bias=nmx[:, hh, r:r + 1], **acc).then_inc(done, 1)

            def copy_w(src_done, count, done):
                act.wait_ge(src_done, count)
                A(tw[:, :, :], psA[:, :, 0:384], ACT.Copy).then_inc(done, 1)

            def if_softplus():
                act.wait_ge(if_b, 1)
                ch.after(A(lft[:, :, :], iff[:, :, 4:8], ACT.Abs))
                ch.after(A(lft[:, :, :], lft[:, :, :], ACT.Exp, scale=-1.0))
                A(lft[:, :, :], lft[:, :, :], ACT.Ln, bias=1.0).then_inc(if_sp, 1)

            def sigmoid(a, b, copied):
                act.wait_ge(proj_copied, index[copied] + 1)
                A(gates[:, a:b, :], gates[:, a:b, :], ACT.Sigmoid).then_inc(sig, 1)

            for name in ("sbq", "sbk", "sbv"):
                split(4); copy(name)
            act.wait_ge(cw_t, 1)
            A(convw[:, :], psA[:, 0, 0:32], ACT.Copy).then_inc(cw_ready, 1)
            copy("if"); sb_softplus(0); split(4); copy("mlq")
            sb_exp(0); split(4); copy("mlk")
            out_high(0, 0, sb_o); if_softplus(); split(4); copy("mbq")
            sb_softplus(1); split(4); copy("mbk"); mb_squares(0); mb_squares(1)
            sb_exp(1); split(2); mb_rstd(); split(2); copy("mlv")
            out_high(0, 1, sb_o); split(4); copy("mbv")
            for q in range(2):
                act.wait_ge(conv_done, q + 1)
                o = q * NC
                A(mlqk[:, o:o + NC, :], mlqk[:, o:o + NC, :], ACT.Silu).then_inc(silu_done, 1)
            split(4); copy("mlo")
            split(4); copy("g0")
            mb_copyT(); split(4); copy("g1")
            split(1); rows_exp(mb_m, 1, True, mb_exp); split(3); copy("g2")
            copy_w(mb_pt, 1, mb_w); split(4); copy("g3")
            out_high(1, 0, mb_o); split(1); rows_exp(mb_m, 2, True, mb_exp); split(3); copy("g4")
            copy_w(mb_pt, 2, mb_w); split(1); sigmoid(0, NC + NK, "g1"); split(3); copy("g5")
            out_high(1, 1, mb_o)
            act.wait_ge(fl_in, 1)
            A(flo[:, :, :], flo[:, :, :], ACT.Exp, scale=-1.0).then_inc(fl_ready, 1)
            rows_exp(d_ready, 1, False, w_ready)
            split(2)
            sigmoid(NC + NK, NC + 2 * NK, "g3"); split(2)
            split(1); copy_w(ml_pt, 1, ml_w); split(1)
            act.wait_ge(ml_prod, 1)
            A(brT[0][:, 2], tb[:, :, 0:256], ACT.Copy).then_inc(out_hi, 1)
            split(2); sigmoid(NC + 2 * NK, NC + 3 * NK, "g5")
            for half in range(2):
                split(2)
                act.wait_ge(merged, 5 + half)
                A(aT[0][:, 4 * half:4 * half + 4, :], gates[:, NC + 4 * half:NC + 4 * half + 4, :],
                  ACT.Copy).then_inc(merged_hi, 1)
            split(8)

        @block.vector
        def _(dve):
            ch = Chain(dve, dch)
            v = nc.vector
            dve.wait_ge(rstd_ready, 1)
            dve.wait_ge(sq_done, NT)
            for tt in range(NT):
                last = v.tensor_scalar(xs[:, tt, :], t.x[:, tt, :], rs[:, tt:tt + 1], None, ALU.mult)
                ch.after(last)
            v.tensor_copy(t.junk[:, 0:1], rs[:, 0:1]).then_inc(xs_ready, 1)
            splits = [0]

            def split(count):
                for _ in range(count):
                    i = splits[0]
                    splits[0] += 1
                    if i >= PARTS * len(stream):
                        return
                    dve.wait_ge(hi_ready, i + 1)
                    v.tensor_tensor(part_buf(wlo, i), raw_part(i), part_buf(whi, i).bitcast(F32),
                                    ALU.subtract).then_inc(lo_ready, 1)

            dve.wait_ge(gain_in, 16)
            split(2)
            for b in range(5):
                if b:
                    dve.wait_ge(xhi, b)
                    o = slice(2 * b - 2, 2 * b)
                    v.tensor_tensor(aT[1][:, o, :], xnT[:, o, :], aT[0][:, o, :].bitcast(F32),
                                    ALU.subtract).then_inc(xn_split, 1)
                if b == 4:
                    break
                dve.wait_ge(xT_done, b + 1)
                v.tensor_tensor(xnT[:, 2 * b:2 * b + 2, :], psA[:, b, :].rearrange("p (k n) -> p k n", k=2),
                                bc(gain[:, 2 * b:2 * b + 2], 2, SEQ), ALU.mult).then_inc(xnT_ready, 1)
            split(MIX_SPLITS - 2)

            def sb_softplus(g):
                dve.wait_ge(sb_ln, g + 1)
                if g:
                    dve.wait_ge(sb_c, g)
                v.scalar_tensor_tensor(out=tb[:, :, :], in0=psA[:, :, 0:384], scalar=0.0, in1=ta[:, :, :],
                                       op0=ALU.max, op1=ALU.add).then_inc(sb_sp, 1)

            def out_low(b, g, done):
                dve.wait_ge(out_hi, 2 * b + g + 1)
                o = slice(2 * g, 2 * g + 2)
                v.tensor_tensor(brT[1][:, b, o, :], psA[:, 0:3:2, 0:256], brT[0][:, b, o, :].bitcast(F32),
                                ALU.subtract).then_inc(done, 1)

            def conv(q):
                dve.wait_ge(proj_copied, index["mlk" if q else "mlq"] + 1)
                dve.wait_ge(cw_ready, 1)
                dve.wait_ge(pads, 1)
                for j in range(4):
                    for c in range(q * NC, q * NC + NC):
                        w = convw[:, 8 * j + c:8 * j + c + 1]
                        src = mlpre[:, c, j:j + SEQ]
                        if j == 0:
                            last = v.tensor_scalar(mlqk[:, c, :], src, w, None, ALU.mult)
                        else:
                            last = v.scalar_tensor_tensor(out=mlqk[:, c, :], in0=src, scalar=w, in1=mlqk[:, c, :],
                                                          op0=ALU.mult, op1=ALU.add)
                    if j < 3:
                        ch.after(last)
                last.then_inc(conv_done, 1)

            def mb_norm(q):
                x = mbqk[:, q, :, :].rearrange("p t (h n) -> p (t h) n", n=HD)
                ch.after(v.tensor_tensor(x, x, bc(hrs[:, q, :], 2, HD), ALU.mult))
                ch.after(v.tensor_tensor(x, x, bc(qkg[:, q, :], 1, NT * HEADS), ALU.mult))
                x = mbqk[:, q, :, :].rearrange("p t (h n) -> p t h n", n=HD)
                x1, x2 = x[:, :, :, 0:ROT], x[:, :, :, ROT:2 * ROT]
                cos, sin = bc(t.cos[:, :, :], 2, HEADS), bc(t.sin[:, :, :], 2, HEADS)
                v.tensor_tensor(r4[:, 0], x1, cos, ALU.mult)
                v.tensor_tensor(r4[:, 1], x2, sin, ALU.mult)
                v.tensor_tensor(r4[:, 2], x1, sin, ALU.mult)
                ch.after(v.tensor_tensor(r4[:, 3], x2, cos, ALU.mult))
                v.tensor_tensor(x1, r4[:, 0], r4[:, 1], ALU.subtract)
                ch.after(v.tensor_tensor(x2, r4[:, 2], r4[:, 3], ALU.add))
                v.tensor_copy(t.junk[:, 0:1], rs[:, 0:1]).then_inc(mb_rot, 1)

            def row_max(floor):
                ch.after(v.tensor_reduce(mxb[:, :, 0], ta[:, :, 0:P], AX.X, ALU.max))
                ch.after(v.tensor_reduce(mxb[:, :, 1], ta[:, :, P:384], AX.X, ALU.max))
                if floor:
                    ch.after(v.tensor_scalar(mxb[:, :, :], mxb[:, :, :], 0.0, None, ALU.max))
                return v.tensor_scalar(nmx[:, :, :], mxb[:, :, :], -1.0, None, ALU.mult)

            def mb_softmax_in(g):
                dve.wait_ge(mb_s, g + 1)
                if g:
                    dve.wait_ge(mb_pt, g)
                nm = bc(t.neg_mask[:, :], 1, 4)
                v.tensor_tensor(ta[:, :, 0:P], psA[:, :, 0:P], nm, ALU.add)
                v.tensor_copy(ta[:, :, P:2 * P], psA[:, :, P:2 * P])
                ch.after(v.tensor_tensor(ta[:, :, 2 * P:], psA[:, :, 2 * P:384], nm, ALU.add))
                row_max(False).then_inc(mb_m, 1)

            def scale_rows(r, done):
                v.tensor_tensor(ta[:, :, 0:P], ta[:, :, 0:P], bc(r[:, :, 0], 2, P), ALU.mult)
                ch.after(v.tensor_tensor(ta[:, :, P:], ta[:, :, P:], bc(r[:, :, 1], 2, 2 * P), ALU.mult))
                v.tensor_copy(t.junk[:, 0:1], rs[:, 0:1]).then_inc(done, 1)

            def mb_normalise(g):
                dve.wait_ge(mb_exp, 8 * (g + 1))
                ch.after(v.reciprocal(rsum[:, :, :], sums[:, :, :]))
                scale_rows(rsum, mb_p)

            def if_bias():
                dve.wait_ge(proj_copied, index["if"] + 1)
                v.tensor_tensor(iff[:, :, :], iff[:, :, :], bc(mlb[:, :], 1, NT), ALU.add).then_inc(if_b, 1)

            def log_f():
                dve.wait_ge(if_sp, 1)
                v.scalar_tensor_tensor(out=lf[:, :, :], in0=iff[:, :, 4:8], scalar=0.0, in1=lft[:, :, :],
                                       op0=ALU.min, op1=ALU.subtract).then_inc(lf_r, 1)

            def a_diag():
                dve.wait_ge(f_done, 1)
                ch.after(v.tensor_copy(Fc[:, :, :], psA[:, 0, 0:8].rearrange("p (t h) -> p t h", t=NT)))
                ch.after(v.tensor_tensor(av[:, :, :], iff[:, :, 0:4], Fc[:, :, :], ALU.subtract))
                dst = mbqkT[:, 0, :, :].rearrange("p c (a n) -> p (c a) n", n=P)
                v.tensor_tensor(dst, bc(t.ident[:, :], 1, NT * ML_HEADS),
                                bc(av[:, :, :].rearrange("p t h -> p (t h)"), 2, P), ALU.mult).then_inc(f_ready, 1)

            def a_rows():
                dve.wait_ge(abc, 1)
                row = [psA[:, tt, :].rearrange("p (h n) -> p h n", n=P) for tt in range(NT)]
                nm = bc(t.neg_mask[:, :], 1, 4)
                v.tensor_tensor(ml_d[:, :, 0:P], row[0], nm, ALU.add)
                v.tensor_copy(ml_d[:, :, P:2 * P], row[0])
                v.tensor_tensor(ml_d[:, :, 2 * P:], row[1], nm, ALU.add).then_inc(abc_used, 1)

            ml_d = xs[:, :, :].rearrange("p t n -> p (t n)")[:, 0:1536].rearrange("p (h n) -> p h n", n=384)

            split(12)
            if_bias(); sb_softplus(0); split(4)
            split(1); conv(0); log_f(); split(3)
            out_low(0, 0, sb_e); split(4)
            sb_softplus(1); split(1); conv(1); split(3)
            for q in range(2):
                dve.wait_ge(mb_sq, q + 1)
                v.tensor_reduce(hss[:, q, :], xs[:, q, :].rearrange("p (h n) -> p h n", n=HD), AX.X,
                                ALU.add).then_inc(mb_ss, 1)
            split(4)
            out_low(0, 1, sb_e); split(1)
            dve.wait_ge(mb_rs, 1)
            mb_norm(0); split(3)
            a_diag(); split(1); mb_norm(1); split(3)
            a_rows(); split(4)
            split(4)
            for g in range(2):
                if g:
                    out_low(1, 0, mb_e)
                mb_softmax_in(g); split(1); mb_normalise(g); split(3)
                split(4) if g == 0 else None
            dve.wait_ge(mb_pt, 2)
            dve.wait_ge(mb_exp, 16)
            ch.after(v.tensor_copy(ta[:, :, :], ml_d))
            row_max(True).then_inc(d_ready, 1)
            v.tensor_tensor(flo[:, :, :], mxb[:, :, :], Fc[:, :, :].rearrange("p t h -> p h t"),
                            ALU.add).then_inc(fl_in, 1)
            split(4)
            out_low(1, 1, mb_e)

            def merge(b, half):
                n = 2 * b + half
                i = len(chunks) + n
                dve.wait_ge(sig, b + 1)
                dve.wait_ge(part_used, PARTS * (first_branch + b) + 2 * (half + 1))
                ps = psP[:, 2 * (i % 2):2 * (i % 2) + 2, :].rearrange("p b (c n) -> p (b c) n", n=SEQ)
                o = NC + b * NK + 4 * half
                gb, g0 = gates[:, o:o + 4, :], gates[:, NC + 4 * half:NC + 4 * half + 4, :]
                ins = v.tensor_tensor(gb, ps, gb, ALU.mult)
                if b:
                    ch.after(ins)
                    ins = v.tensor_tensor(g0, g0, gb, ALU.add)
                ins.then_inc(merged, 1)
                dve.wait_ge(merged, n + 1)

            merge(0, 0)
            dve.wait_ge(ml_s, 1)
            dve.wait_ge(w_ready, 8)
            ch.after(v.scalar_tensor_tensor(out=ta[:, :, :], in0=psA[:, :, 0:384], scalar=float(ML_HD) ** -0.5,
                                            in1=ta[:, :, :], op0=ALU.mult, op1=ALU.mult))
            v.tensor_reduce(den[:, :, 0], ta[:, :, 0:P], AX.X, ALU.add)
            ch.after(v.tensor_reduce(den[:, :, 1], ta[:, :, P:384], AX.X, ALU.add))
            ch.after(v.tensor_scalar(dneg[:, :, :], den[:, :, :], -1.0, None, ALU.mult))
            ch.after(v.tensor_tensor(den[:, :, :], den[:, :, :], dneg[:, :, :], ALU.max))
            dve.wait_ge(fl_ready, 1)
            ch.after(v.tensor_tensor(den[:, :, :], den[:, :, :], flo[:, :, :], ALU.max))
            ch.after(v.reciprocal(den[:, :, :], den[:, :, :]))
            scale_rows(den, ml_p)
            split(4); merge(0, 1)
            split(1); merge(1, 0); split(1)
            dve.wait_ge(ml_o, 1)
            v.tensor_tensor(tb[:, :, 0:256], psA[:, :, 0:256], gates[:, 0:NC, :], ALU.mult).then_inc(ml_prod, 1)
            dve.wait_ge(out_hi, 5)
            v.tensor_tensor(brT[1][:, 2], tb[:, :, 0:256], brT[0][:, 2].bitcast(F32), ALU.subtract).then_inc(ml_e, 1)
            split(2); merge(1, 1)
            for half in range(2):
                split(1); merge(2, half); split(1)
                dve.wait_ge(merged_hi, half + 1)
                o = slice(4 * half, 4 * half + 4)
                v.tensor_tensor(aT[1][:, o, :], gates[:, NC + 4 * half:NC + 4 * half + 4, :],
                                aT[0][:, o, :].bitcast(F32), ALU.subtract).then_inc(merged_lo, 1)
            split(8)
            for n in range(2):
                i = len(chunks) + 6 + n
                dve.wait_ge(part_used, PARTS * (first_out + n + 1))
                xh = t.x[:, :, n * CHUNK:(n + 1) * CHUNK]
                v.tensor_tensor(xh, psP[:, 2 * (i % 2):2 * (i % 2) + 2, :], xh, ALU.add).then_inc(x_added, 1)
            dve.wait_ge(x_added, 2)
    ph.end()
    mem.close()


def tensors(nc, ctx):
    class T:
        pass
    t = T()

    def sb(name, shape, dt=F32):
        return ctx.enter_context(nc.sbuf_tensor(name, shape, dt))
    t.x = sb("x_res", [P, NT, D])
    t.ident, t.trineg, t.tri, t.tri_strict = (sb(n, [P, P]) for n in ("ident", "trineg", "tri", "tri_strict"))
    t.neg_mask, t.ones, t.negones = (sb(n, [P, P]) for n in ("neg_mask", "ones", "negones"))
    t.eps, t.junk = sb("eps", [P, 1]), sb("junk", [P, 1])
    t.fold, t.index, t.index_i = sb("fold", [P, 2 * SLOTS]), sb("index", [P, NE]), sb("index_i", [P, NE], I32)
    t.pos_i, t.pos, t.freq = sb("pos_i", [P, NT], I32), sb("pos", [P, NT]), sb("freq", [P, ROT])
    t.ang, t.turn, t.sin, t.cos = (sb(n, [P, NT, ROT]) for n in ("ang", "turn", "sin", "cos"))
    t.ps_a = ctx.enter_context(nc.psum_tensor("ps_a", [P, 4, 512], F32))
    t.ps_b = ctx.enter_context(nc.psum_tensor("ps_b", [P, 4, 512], F32))
    t.ps_x = t.ps_b[:, 1, :]
    return t



def route(nc, t, d, l, m, prefetch):
    ph = Phase(nc, "route")
    mem = ExitStack()
    S = ph.sem

    def sb(name, shape, dt=F32):
        return mem.enter_context(nc.sbuf_tensor(name, shape, dt))

    NR = NG + NE
    gain, xn, xnT = sb("gain2", [P, D]), sb("xn2", [P, NT, D]), sb("xn2T", [P, NK, SEQ])
    wr, br, lg = sb("w_router", [P, NK, NR]), sb("b_router", [P, NR]), sb("logits", [P, NT, NR])
    ms, rs = sb("mean_sq2", [P, NT]), sb("rstd2", [P, NT])
    gmax, gsum, kmin, m1, m2, w1, w2, er = (sb(n, [P, NT]) for n in (
        "group_max", "group_sum", "key_min", "first_max", "second_max", "first_w", "second_w", "max_ratio"))
    gexp, ohg, keyg = (sb(n, [P, NT, NG]) for n in ("group_exp", "group_pick", "group_key"))
    em, key, oh1, oh2, A = (sb(n, [P, NT, NE]) for n in (
        "group_logits", "expert_key", "first_pick", "second_pick", "assigned"))
    nmax, cmp = sb("most_tokens", [P, 1]), sb("over", [P, MAX_ROUNDS - 1])

    smalls, sq_done, rstd_ready, xn_ready, hi_done, xnT_ps, xnT_ready = (S(n) for n in (
        "small_loads", "sum_sq_done", "rstd_ready", "xn_ready", "xn_high_done", "xT_done", "xnT_ready"))
    logits_done, gexp_in, gexp_done, er_in, er_done, picked, counted, dch, ach = (S(n) for n in (
        "logits_done", "group_exp_in", "group_exp_done", "ratio_in", "ratio_done", "picked", "counted",
        "dve_chain", "act_chain"))

    with nc.Block() as block:
        @block.sync
        def _(sp):
            L = bass.ds(l, 1)
            for src, dst in [
                    (d.norm2_g[L].partition_broadcast(P).rearrange("p l n -> p (l n)"), gain[:, :]),
                    (d.w_rg[L].rearrange("l (p k) n -> p (l k) n", p=P), wr[:, :, 0:NG]),
                    (d.w_re[L].rearrange("l (p k) n -> p (l k) n", p=P), wr[:, :, NG:]),
                    (d.b_rg[L].partition_broadcast(P).rearrange("p l n -> p (l n)"), br[:, 0:NG]),
                    (d.b_re[L].partition_broadcast(P).rearrange("p l n -> p (l n)"), br[:, NG:])]:
                sp.dma_start(dst, src).then_inc(smalls, 16)
            prefetch(sp)

        @block.scalar
        def _(act):
            ch = Chain(act, ach)
            A_ = nc.scalar.activation
            for tt in range(NT):
                A_(xn[:, tt, :], t.x[:, tt, :], ACT.Square, accum_out=ms[:, tt:tt + 1]).then_inc(sq_done, 1)
            act.wait_ge(sq_done, NT)
            ch.after(A_(rs[:, :], ms[:, :], ACT.Ln, bias=t.eps[:, :], scale=1.0 / D))
            A_(rs[:, :], rs[:, :], ACT.Exp, scale=-0.5).then_inc(rstd_ready, 1)
            for b in range(4):
                act.wait_ge(xnT_ps, b + 1)
                A_(xnT[:, 2 * b:2 * b + 2, :], t.ps_a[:, b, :].rearrange("p (k n) -> p k n", k=2),
                   ACT.Copy).then_inc(xnT_ready, 1)
            for tt in range(NT):
                act.wait_ge(xn_ready, tt + 1)
                A_(m.xn_hi[:, tt, :], xn[:, tt, :], ACT.Copy).then_inc(hi_done, 1)
            act.wait_ge(gexp_in, 1)
            A_(gexp[:, :, :], gexp[:, :, :], ACT.Exp).then_inc(gexp_done, 1)
            act.wait_ge(er_in, 1)
            A_(er[:, :], er[:, :], ACT.Exp).then_inc(er_done, 1)

        @block.tensor
        def _(pe):
            mm = nc.tensor.matmul
            pe.wait_ge(xn_ready, NT)
            for b in range(4):
                for k in (2 * b, 2 * b + 1):
                    for tt in range(NT):
                        o = (k % 2) * SEQ + tt * P
                        last = nc.tensor.transpose(t.ps_a[:, b, o:o + P], xn[:, tt, k::NK], t.ident[:, :])
                last.then_inc(xnT_ps, 1)
            pe.wait_ge(smalls, 16 * 5)
            pe.wait_ge(xnT_ready, 4)
            for tt in range(NT):
                for k in range(NK):
                    last = mm(t.ps_b[:, tt, 0:NR], xnT[:, k, tt * P:(tt + 1) * P], wr[:, k, :],
                              start=k == 0, stop=k == NK - 1)
            last.then_inc(logits_done, 1)
            pe.wait_ge(picked, 1)
            o = t.ps_b[:, 2, :]
            mm(o[:, 0:NE], t.tri_strict[:, :], A[:, 0, :], start=True, stop=True, skip_group_check=True)
            mm(o[:, NE:2 * NE], t.tri_strict[:, :], A[:, 1, :], start=False, stop=True, skip_group_check=True)
            mm(o[:, NE:2 * NE], t.ones[:, :], A[:, 0, :], start=False, stop=True, skip_group_check=True)
            mm(o[:, 2 * NE:3 * NE], t.ones[:, :], A[:, 0, :], start=False, stop=True, skip_group_check=True)
            mm(o[:, 2 * NE:3 * NE], t.ones[:, :], A[:, 1, :], start=False, stop=True,
               skip_group_check=True).then_inc(counted, 1)

        @block.vector
        def _(dve):
            ch = Chain(dve, dch)
            v = nc.vector
            dve.wait_ge(rstd_ready, 1)
            dve.wait_ge(smalls, 16 * 5)
            for tt in range(NT):
                v.scalar_tensor_tensor(out=xn[:, tt, :], in0=t.x[:, tt, :], scalar=rs[:, tt:tt + 1], in1=gain[:, :],
                                       op0=ALU.mult, op1=ALU.mult).then_inc(xn_ready, 1)
            for tt in range(NT):
                dve.wait_ge(hi_done, tt + 1)
                ch.after(v.tensor_tensor(m.xn_lo[:, tt, :], xn[:, tt, :], m.xn_hi[:, tt, :].bitcast(F32),
                                         ALU.subtract))
            dve.wait_ge(logits_done, 1)
            ch.after(v.tensor_tensor(lg[:, :, :], t.ps_b[:, 0:NT, 0:NR], bc(br[:, :], 1, NT), ALU.add))

            def first_max(vals, mx, k, out, n):
                ch.after(v.tensor_reduce(mx[:, :], vals, AX.X, ALU.max))
                ch.after(v.tensor_tensor(k[:, :, :], vals, bc(mx[:, :], 2, n), ALU.is_equal))
                ch.after(v.scalar_tensor_tensor(out=k[:, :, :], in0=k[:, :, :], scalar=-64.0,
                                                in1=bc(t.index[:, 0:n], 1, NT), op0=ALU.mult, op1=ALU.add))
                ch.after(v.tensor_reduce(kmin[:, :], k[:, :, :], AX.X, ALU.min))
                ch.after(v.tensor_tensor(out[:, :, :], k[:, :, :], bc(kmin[:, :], 2, n), ALU.is_equal))

            groups = lg[:, :, 0:NG]
            first_max(groups, gmax, keyg, ohg, NG)
            v.tensor_tensor(gexp[:, :, :], groups, bc(gmax[:, :], 2, NG), ALU.subtract).then_inc(gexp_in, 1)
            ch.after(v.tensor_scalar(keyg[:, :, :], ohg[:, :, :], -NEG, NEG, ALU.mult, ALU.add))
            for tt in range(NT):
                last = v.tensor_tensor(em[:, tt, :].rearrange("p (g e) -> p g e", g=NG),
                                       lg[:, tt, NG:].rearrange("p (g e) -> p g e", g=NG),
                                       bc(keyg[:, tt, :], 2, EPG), ALU.add)
                ch.after(last)
            first_max(em[:, :, :], m1, key, oh1, NE)
            ch.after(v.scalar_tensor_tensor(out=em[:, :, :], in0=oh1[:, :, :], scalar=NEG, in1=em[:, :, :],
                                            op0=ALU.mult, op1=ALU.add))
            first_max(em[:, :, :], m2, key, oh2, NE)
            v.tensor_tensor(er[:, :], m2[:, :], m1[:, :], ALU.subtract).then_inc(er_in, 1)
            v.tensor_tensor(A[:, :, :], oh1[:, :, :], oh2[:, :, :], ALU.add).then_inc(picked, 1)
            dve.wait_ge(gexp_done, 1)
            ch.after(v.tensor_reduce(gsum[:, :], gexp[:, :, :], AX.X, ALU.add))
            dve.wait_ge(er_done, 1)
            ch.after(v.tensor_scalar(w1[:, :], er[:, :], 1.0, None, ALU.add))
            ch.after(v.tensor_tensor(w1[:, :], w1[:, :], gsum[:, :], ALU.mult))
            ch.after(v.reciprocal(w1[:, :], w1[:, :]))
            ch.after(v.tensor_tensor(w2[:, :], w1[:, :], er[:, :], ALU.mult))
            v.tensor_tensor(oh1[:, :, :], oh1[:, :, :], bc(w1[:, :], 2, NE), ALU.mult)
            ch.after(v.tensor_tensor(oh2[:, :, :], oh2[:, :, :], bc(w2[:, :], 2, NE), ALU.mult))
            ch.after(v.tensor_tensor(m.comb[:, :, :], oh1[:, :, :], oh2[:, :, :], ALU.add))
            dve.wait_ge(counted, 1)
            ch.after(v.scalar_tensor_tensor(out=m.place[:, :, :],
                                            in0=t.ps_b[:, 2, 0:2 * NE].rearrange("p (t e) -> p t e", t=NT), scalar=1.0,
                                            in1=A[:, :, :], op0=ALU.add, op1=ALU.mult))
            ch.after(v.tensor_scalar(m.place[:, :, :], m.place[:, :, :], -1.0, None, ALU.add))
            ch.after(v.tensor_reduce(nmax[:, :], t.ps_b[:, 2, 2 * NE:3 * NE], AX.X, ALU.max))
            for i in range(MAX_ROUNDS - 1):
                last = v.tensor_scalar(cmp[:, i:i + 1], nmax[:, :], float(SLOTS * (i + 1)), None, ALU.is_gt)
            ch.after(last)
            ch.after(v.tensor_reduce(nmax[:, :], cmp[:, :], AX.X, ALU.add))
            ch.after(v.tensor_scalar(m.rounds[:, :], nmax[0:1, :], 1.0, None, ALU.add))
    ph.end()
    mem.close()



class Gather:

    STEPS = [("rows", k) for k in range(NK)] + [("weights", 0)] + [("select", q) for q in range(2)]

    def __init__(self, nc, t, m, S, banks):
        self.nc, self.t, self.m, self.banks = nc, t, m, banks
        self.given, self.taken = S("bank_given"), S("bank_taken")
        self.sel_ready, self.selw_ready, self.read = S("select_ready"), S("weighted_ready"), S("select_read")

    def dve_select(self, dve, n, batch, chain):
        nc, m, v = self.nc, self.m, self.nc.vector
        ex = slice(batch * BATCH, (batch + 1) * BATCH)
        if n:
            dve.wait_ge(self.read, n)
        for tt in range(NT):
            v.tensor_tensor(m.sel[:, tt].rearrange("p (e d) s -> p e d s", d=2),
                            bc(bc(self.t.index[:, 0:SLOTS], 1, 2), 1, BATCH),
                            bc(bc(m.place[:, tt, ex], 2, 2), 3, SLOTS), ALU.is_equal).then_inc(self.sel_ready, 1)
        dve.wait_ge(self.sel_ready, NT * (n + 1))
        for tt in range(NT):
            v.tensor_tensor(m.selw[:, tt], m.sel[:, tt, 0::2, :].bitcast(F32), bc(m.comb[:, tt, ex], 2, SLOTS),
                            ALU.mult).then_inc(self.selw_ready, 1)
        chain.after(v.tensor_scalar(m.place[:, :, ex], m.place[:, :, ex], -float(SLOTS), None, ALU.add))

    def pe_step(self, pe, n, i, buf, uses):
        bank = self.banks[uses % len(self.banks)]
        nc, t, m = self.nc, self.t, self.m
        mm = nc.tensor.matmul
        kind, k = self.STEPS[i]
        if uses >= len(self.banks):
            pe.wait_ge(self.taken, uses - len(self.banks) + 1)
        if kind == "rows":
            pe.wait_ge(self.sel_ready, NT * (n + 1))
            for part, xn in enumerate((m.xn_hi, m.xn_lo)):
                for tt in range(NT):
                    last = mm(bank[:, part * 256:(part + 1) * 256], xn[:, tt, k::NK], m.sel[:, tt, 0::2, :],
                              start=tt == 0, stop=tt == NT - 1)
        elif kind == "weights":
            pe.wait_ge(self.selw_ready, NT * (n + 1))
            for tt in range(NT):
                last = mm(bank[:, 0:256], t.ones[:, :], m.selw[:, tt].rearrange("p e s -> p (e s)"),
                          start=tt == 0, stop=tt == NT - 1)
        else:
            for j in range(2):
                for tt in range(NT):
                    o = j * SEQ + tt * P
                    e = 4 * (2 * k + j)
                    last = nc.tensor.transpose(bank[:, o:o + P], m.sel[:, tt, e:e + 4, :].rearrange(
                        "p e s -> p (e s)").bitcast(F32), t.ident[:, :])
        last.then_inc(self.given, 1)
        if i == len(self.STEPS) - 1:
            pe.wait_ge(self.given, uses + 1)
            pe.sem_inc(self.read, 1)

    def act_step(self, act, i, buf, uses):
        t, m, bank = self.t, self.m, self.banks[uses % len(self.banks)]
        A = self.nc.scalar.activation
        kind, k = self.STEPS[i]
        act.wait_ge(self.given, uses + 1)
        if kind == "rows":
            dst = m.XT[buf][:, k].rearrange("p (q b s) -> p q b s", b=3, s=2 * SLOTS)
            for part in range(2):
                last = A(dst[:, :, 0::2, part * SLOTS:(part + 1) * SLOTS],
                         bank[:, part * 256:(part + 1) * 256].rearrange("p (q b s) -> p q b s", b=2, s=SLOTS),
                         ACT.Copy)
        elif kind == "weights":
            last = A(m.cw[buf][:, :], bank[:, 0:256], ACT.Copy)
        else:
            last = A(m.selT[buf][:, 2 * k:2 * k + 2, :], bank[:, :].rearrange("p (q n) -> p q n", n=SEQ), ACT.Copy)
        last.then_inc(self.taken, 1)


def moe(nc, t, d, l):
    mem = ExitStack()

    class M:
        pass
    m = M()

    def sb(name, shape, dt=F32):
        return mem.enter_context(nc.sbuf_tensor(name, shape, dt))

    m.xn_hi, m.xn_lo = sb("xn_hi", [P, NT, D], F32R), sb("xn_lo", [P, NT, D], F32R)
    m.comb, m.place = sb("combine", [P, NT, NE]), sb("place", [P, NT, NE])
    m.rounds = sb("rounds", [1, 1], I32)
    m.XT = [sb(f"XT{i}", [P, NK, BATCH // 2 * 6 * SLOTS], F32R) for i in range(2)]
    m.sel, m.selw = sb("select", [P, NT, 2 * BATCH, SLOTS], F32R), sb("select_weighted", [P, NT, BATCH, SLOTS])
    m.selT = [sb(f"selectT{i}", [P, BATCH // 2, SEQ], F32R) for i in range(2)]
    m.cw = [sb(f"slot_weight{i}", [P, BATCH * SLOTS]) for i in range(2)]
    m.h, m.act1, m.u = sb("h", [P, 2 * FE]), sb("silu_h1", [P, 2, 2 * SLOTS]), sb("h3_weighted", [P, 2, 2 * SLOTS])
    m.hidf = [sb(f"hid_whole{i}", [P, 6 * SLOTS]) for i in range(2)]
    m.hid = [sb(f"hid_parts{i}", [P, 6 * SLOTS], F32R) for i in range(2)]
    m.yhi, m.ylo = sb("y_hi", [P, D], F32R), sb("y_lo", [P, D], F32R)
    t.ring = sb("units_ring", [P, 4, URING * UNIT // 4])
    pre = [mem.enter_context(nc.semaphore(f"units_ahead{i}")) for i in range(URING)]

    order, parts, steps = [], [], []

    def use_unit(kind, e):
        n = len(order)
        order.append((kind, e))
        for h in range(UNIT // PART) if kind != "C" else (1,):
            steps.append(("part", len(parts)))
            parts.append((n, kind, e, h))

    bank, gathers = 0, 0

    def use_bank(p):
        nonlocal bank, gathers
        n = p // (BATCH // 2)
        i = gathers - n * len(Gather.STEPS)
        if p < PAIRS and i < len(Gather.STEPS):
            steps.append(("gather", (n, i, bank)))
            bank += 1
            gathers += 1

    for p in range(PAIRS + 2):
        if p < PAIRS:
            for e in (2 * p, 2 * p + 1):
                use_unit("A", e)
                use_unit("B", e)
                if e % 2:
                    steps.append(("h", p))
                use_bank(p)
        if p >= 2:
            steps.append(("scatter", p - 2))
        if p < PAIRS:
            steps.append(("hT", (p, bank)))
            bank += 1
        if 1 <= p <= PAIRS:
            use_unit("C", 2 * p - 2)
            use_bank(p)
            use_unit("C", 2 * p - 1)
            steps.append(("y", p - 1))
        elif p == 0:
            use_bank(p)
    m.order, m.parts, m.steps = order, parts, steps

    def load(sp, n, sem):
        kind, e = order[n]
        dst = t.ring[:, :, :].rearrange("p a b -> p (a b)")[:, (n % URING) * UNIT:(n % URING + 1) * UNIT]
        L, X = bass.ds(l, 1), slice(e, e + 1)
        if kind == "C":
            src = d.w2[L, X].rearrange("l e (p j) n -> p (l e j) n", p=P)
            dst = dst.rearrange("p (j n) -> p j n", j=2)
            for j in range(2):
                sp.dma_start(dst[:, j, :], src[:, j, :]).then_inc(sem, 16)
        else:
            k0 = 0 if kind == "A" else 4
            dst = dst.rearrange("p (k n) -> p k n", k=4)
            for j, w in enumerate((d.w1, d.w3)):
                src = w[L, X].rearrange("l e (p k) n -> p (l e k) n", p=P)
                sp.dma_start(dst[:, :, j * FE:(j + 1) * FE], src[:, k0:k0 + 4, :]).then_inc(sem, 16)

    def prefetch(sp):
        for n in range(URING):
            load(sp, n, pre[n])

    route(nc, t, d, l, m, prefetch)

    m.hi, m.lo = sb("w_hi", [P, SPLITS, PART], F32R), sb("w_lo", [P, SPLITS, PART], F32R)
    units = t.ring[:, :, :].rearrange("p a b -> p (a b)").rearrange("p (u n) -> p u n", n=UNIT)

    def raw_part(i):
        n, _, _, h = parts[i]
        return units[:, n % URING, h * PART:(h + 1) * PART]
    m.raw_unit = lambda n: units[:, n % URING, :]

    def high(i):
        return nc.scalar.activation(m.hi[:, i % SPLITS, :], raw_part(i), ACT.Copy)

    def low(i):
        return nc.vector.tensor_tensor(m.lo[:, i % SPLITS, :], raw_part(i), m.hi[:, i % SPLITS, :].bitcast(F32),
                                       ALU.subtract)
    m.high, m.low = high, low
    ph = Phase(nc, "first")
    g = Gather(nc, t, m, ph.sem, [t.ps_a[:, i, :] for i in range(4)])
    zeroed, dch, hi_ready, lo_ready = (ph.sem(n) for n in ("zeroed", "dve_chain", "high_ready", "low_ready"))
    with nc.Block() as block:
        @block.gpsimd
        def _(pool):
            for buf in m.XT:
                for k in range(NK):
                    nc.gpsimd.memset(buf[:, k].rearrange("p (q b s) -> p q b s", b=3, s=2 * SLOTS)[:, :, 1, :]
                                     .bitcast(F32), 0.0).then_inc(zeroed, 1)
            for buf in m.hid + m.hidf:
                nc.gpsimd.memset(buf[:, :].bitcast(F32), 0.0).then_inc(zeroed, 1)
            pool.wait_ge(zeroed, 2 * NK + 4)

        @block.vector
        def _(dve):
            g.dve_select(dve, 0, 0, Chain(dve, dch))
            for i in range(SPLITS):
                dve.wait_ge(hi_ready, i + 1)
                m.low(i).then_inc(lo_ready, 1)
            dve.wait_ge(lo_ready, SPLITS)

        @block.tensor
        def _(pe):
            for i in range(len(g.STEPS)):
                g.pe_step(pe, 0, i, 0, i)

        @block.scalar
        def _(act):
            for i in range(len(g.STEPS)):
                g.act_step(act, i, 0, i)
                if i < SPLITS:
                    act.wait_ge(pre[parts[i][0]], 32)
                    m.high(i).then_inc(hi_ready, 1)
            act.wait_ge(g.taken, len(g.STEPS))
    ph.end()

    rounds = nc.values_load(m.rounds[0:1, 0:1], min_val=1, max_val=MAX_ROUNDS)
    with nc.Fori(0, rounds) as r:
        experts(nc, t, m, r, rounds, pre, load)
    for s in pre:
        nc.sync.sem_clear(s)
    nc.all_engine_barrier()
    mem.close()


def experts(nc, t, m, r, rounds, pre, load):
    ph = Phase(nc, "exp")
    S = ph.sem
    g = Gather(nc, t, m, S, [t.ps_x])
    later = [S(f"units_in{i}") for i in range(URING)]
    hi_ready, lo_ready, part_used = S("high_ready"), S("low_ready"), S("part_used")
    h_done, h_copied, ht_done, silu_done, hid_ready = (S(n) for n in (
        "h_done", "h_copied", "hT_done", "silu_done", "hid_ready"))
    y_done, yhi_done, ylo_done, s_done, x_added, dch = (S(n) for n in (
        "y_done", "y_high_done", "y_low_done", "scattered", "x_added", "dve_chain"))
    ahead_in, ahead_hi, ahead_lo = S("ahead_units_in"), S("ahead_high"), S("ahead_low")
    acc, ps_h, ps_x, ps_y = t.ps_a, t.ps_b[:, 0, :], t.ps_x, t.ps_b[:, 2:4, :]
    order, parts, steps, hi, lo = m.order, m.parts, m.steps, m.hi, m.lo
    HALF = BATCH // 2
    last_part = {n: i for i, (n, _, _, _) in enumerate(parts)}

    def arrived(eng, n):
        if n < URING:
            eng.wait_ge(pre[n], 32)
        else:
            eng.wait_ge(later[n % URING], 32 * (n // URING))

    def split_done(eng, sem, i):
        if i >= SPLITS:
            eng.wait_ge(sem, i - SPLITS + 1)

    with nc.Block() as block:
        @block.sync
        def _(sp):
            def slot_free(n):
                split_done(sp, lo_ready, last_part[n])
                if order[n][0] == "C":
                    sp.wait_ge(part_used, last_part[n] + 1)
            for n in range(URING, len(order)):
                slot_free(n - URING)
                load(sp, n, later[n % URING])
            with sp.If(r + 1 < rounds):
                for n in range(URING):
                    slot_free(len(order) - URING + n)
                    sp.sem_clear(pre[n])
                    load(sp, n, pre[n])
                for n in range(parts[SPLITS - 1][0] + 1):
                    sp.wait_ge(pre[n], 32)
                sp.sem_inc(ahead_in, 1)

        @block.tensor
        def _(pe):
            mm = nc.tensor.matmul

            def use_part(i):
                _, kind, e, h = parts[i]
                p, j, buf = e // 2, e % 2, i % SPLITS
                o = 2 * j * SLOTS
                if (kind, j, h) == ("A", 0, 0) and p:
                    pe.wait_ge(h_copied, p)
                if kind == "C" and j == 0:
                    pe.wait_ge(hid_ready, p + 1)
                    if p:
                        pe.wait_ge(ylo_done, p)
                split_done(pe, hi_ready, i)
                split_done(pe, lo_ready, i)
                if kind == "C":
                    hidf, hid = m.hidf[p % 2][:, o:o + P], m.hid[p % 2][:, o:o + P]
                    for n2 in range(2):
                        c = n2 * 512
                        mm(ps_y[:, n2, :], hidf, m.raw_unit(parts[i][0])[:, c:c + 512], start=j == 0, stop=False)
                        mm(ps_y[:, n2, :], hid, hi[:, buf, c:c + 512], start=False, stop=False)
                        last = mm(ps_y[:, n2, :], hid, lo[:, buf, c:c + 512], start=False, stop=j == 1)
                else:
                    for k in range(2):
                        row = 4 * (kind == "B") + 2 * h + k
                        xT = m.XT[p // HALF % 2][:, row, 6 * (p % HALF) * SLOTS + o:][:, 0:P]
                        mm(ps_h, xT, hi[:, buf, k * 512:(k + 1) * 512], start=j == 0 and row == 0, stop=False)
                        last = mm(ps_h, xT, lo[:, buf, k * 512:(k + 1) * 512], start=False,
                                  stop=j == 1 and row == NK - 1)
                last.then_inc(part_used, 1)
                return i + 1

            for what, arg in steps:
                if what == "part":
                    used = use_part(arg)
                elif what in ("h", "y"):
                    pe.wait_ge(part_used, used)
                    pe.sem_inc(h_done if what == "h" else y_done, 1)
                elif what == "gather":
                    n, i, uses = arg
                    g.pe_step(pe, n, i, (n + 1) % 2, uses)
                elif what == "scatter":
                    p = arg
                    pe.wait_ge(yhi_done, p + 1)
                    pe.wait_ge(ylo_done, p + 1)
                    for tt in range(NT):
                        for n2 in range(2):
                            for y in (m.yhi, m.ylo):
                                last = mm(acc[:, 2 * tt + n2, :], m.selT[p // HALF % 2][:, p % HALF, tt * P:(tt + 1) * P],
                                          y[:, n2 * 512:(n2 + 1) * 512], start=p == 0 and y is m.yhi,
                                          stop=p == PAIRS - 1 and y is m.ylo)
                    last.then_inc(s_done, 1)
                elif what == "hT":
                    p, uses = arg
                    pe.wait_ge(h_copied, p + 1)
                    if uses:
                        pe.wait_ge(g.taken, uses)
                    for w in range(2):
                        for j in range(2):
                            o = (2 * w + j) * 2 * SLOTS
                            last = mm(ps_x[:, o:o + 2 * SLOTS], m.h[:, w * FE + j:(w + 1) * FE:2], t.fold[:, :],
                                      start=True, stop=True)
                    last.then_inc(g.given, 1)
                    pe.wait_ge(g.given, uses + 1)
                    pe.sem_inc(ht_done, 1)

        @block.scalar
        def _(act):
            A = nc.scalar.activation

            def split_high(i):
                if i >= len(parts):
                    return
                arrived(act, parts[i][0])
                act.wait_ge(part_used, i - SPLITS + 1)
                m.high(i).then_inc(hi_ready, 1)

            for what, arg in steps:
                if what == "part":
                    split_high(arg + SPLITS)
                elif what == "gather":
                    n, i, uses = arg
                    g.act_step(act, i, (n + 1) % 2, uses)
                elif what == "h":
                    act.wait_ge(h_done, arg + 1)
                    if arg:
                        act.wait_ge(ht_done, arg)
                    A(m.h[:, :], ps_h, ACT.Copy).then_inc(h_copied, 1)
                elif what == "hT":
                    p, _ = arg
                    act.wait_ge(ht_done, p + 1)
                    if p:
                        act.wait_ge(hid_ready, p)
                    A(m.act1[:, :, :], ps_x[:, 0:4 * SLOTS].rearrange("p (j s) -> p j s", j=2),
                      ACT.Silu).then_inc(silu_done, 1)
                elif what == "y":
                    act.wait_ge(y_done, arg + 1)
                    if arg:
                        act.wait_ge(s_done, arg)
                    A(m.yhi[:, :], ps_y.rearrange("p b n -> p (b n)"), ACT.Copy).then_inc(yhi_done, 1)
            with act.If(r + 1 < rounds):
                act.wait_ge(part_used, len(parts))
                act.wait_ge(ahead_in, 1)
                for i in range(SPLITS):
                    m.high(i).then_inc(ahead_hi, 1)

        @block.vector
        def _(dve):
            ch = Chain(dve, dch)
            v = nc.vector

            def split_low(i):
                if i >= len(parts):
                    return
                arrived(dve, parts[i][0])
                split_done(dve, hi_ready, i)
                m.low(i).then_inc(lo_ready, 1)

            def blocks(buf):
                return buf[:, :].rearrange("p (b s) -> p b s", b=3)[:, 0::2, :]

            g.dve_select(dve, 0, 1, ch)
            for what, arg in steps:
                if what == "part":
                    split_low(arg + SPLITS)
                elif what == "gather" and arg[1] == len(g.STEPS) - 1 and arg[0] < BATCHES - 1:
                    g.dve_select(dve, arg[0] + 1, (arg[0] + 2) % BATCHES, ch)
                elif what == "hT":
                    p, _ = arg
                    dve.wait_ge(silu_done, p + 1)
                    cw = m.cw[p // HALF % 2][:, (p % HALF) * 2 * SLOTS:][:, 0:2 * SLOTS]
                    ch.after(v.tensor_tensor(m.u[:, :, :], ps_x[:, 4 * SLOTS:8 * SLOTS].rearrange(
                        "p (j s) -> p j s", j=2), bc(cw, 1, 2), ALU.mult))
                    v.sem_inc(g.taken, 1)
                    if p >= 2:
                        dve.wait_ge(y_done, p - 1)
                    hidf, hid = blocks(m.hidf[p % 2]), blocks(m.hid[p % 2])
                    two = "p (b s) -> p b s"
                    v.tensor_tensor(hidf[:, :, 0:SLOTS], m.u[:, 0, :].rearrange(two, b=2),
                                    m.act1[:, 0, :].rearrange(two, b=2), ALU.mult)
                    ch.after(v.tensor_tensor(m.u[:, 1, :], m.u[:, 1, :], m.act1[:, 1, :], ALU.mult))
                    ch.after(v.tensor_copy(hid[:, :, 0:SLOTS], m.u[:, 1, :].rearrange(two, b=2)))
                    v.tensor_tensor(hid[:, :, SLOTS:], m.u[:, 1, :].rearrange(two, b=2),
                                    hid[:, :, 0:SLOTS].bitcast(F32), ALU.subtract).then_inc(hid_ready, 1)
                elif what == "y":
                    dve.wait_ge(yhi_done, arg + 1)
                    v.tensor_tensor(m.ylo[:, :], ps_y.rearrange("p b n -> p (b n)"), m.yhi[:, :].bitcast(F32),
                                    ALU.subtract).then_inc(ylo_done, 1)
            dve.wait_ge(s_done, PAIRS)
            v.tensor_tensor(t.x[:, :, :].rearrange("p t n -> p (t n)"), acc[:, :, :].rearrange("p b n -> p (b n)"),
                            t.x[:, :, :].rearrange("p t n -> p (t n)"), ALU.add).then_inc(x_added, 1)
            with dve.If(r + 1 < rounds):
                for i in range(SPLITS):
                    dve.wait_ge(ahead_hi, i + 1)
                    m.low(i).then_inc(ahead_lo, 1)
                dve.wait_ge(ahead_lo, SPLITS)
            dve.wait_ge(x_added, 1)
    ph.end()


def build_program(nc, d):
    with ExitStack() as ctx:
        t = tensors(nc, ctx)
        setup_constants(nc, t, d)
        with nc.Fori(0, DEPTH) as l:
            mixer(nc, t, d, l)
            if True:
                moe(nc, t, d, l)
        ph = Phase(nc, "store")
        stored = ph.sem("stored")
        with nc.Block() as block:
            @block.sync
            def _(sp):
                sp.dma_start(d.out[0].rearrange("(t p) n -> p t n", p=P), t.x[:, :, :]).then_inc(stored, 16)
                sp.wait_ge(stored, 16)
        ph.end()


_INS = ["x", "positions", "norm1_g", "w_in", "qn_g", "kn_g", "conv_w", "ml_gate_b", "w_branch", "w_out",
        "norm2_g", "w_rg", "b_rg", "w_re", "b_re", "w1", "w3", "w2"]


def kernel(**inputs):
    import numpy as _np
    import concourse.bacc as _bacc
    from concourse import mybir as _mybir
    from concourse.bass_utils import run_bass_kernel_spmd as _run

    nc = _bacc.Bacc("TRN2", target_bir_lowering=False, num_devices=1, dynamic_dma_scratch_size=2048)
    arrays = {}

    class Dram:
        pass
    d = Dram()
    for name in _INS:
        a = _np.ascontiguousarray(inputs[name])
        arrays[f"in_{name}_dram"] = a
        d.__dict__[name] = nc.dram_tensor(f"in_{name}_dram", a.shape, _mybir.dt.from_np(a.dtype),
                                          kind="ExternalInput").ap()
    d.out = nc.dram_tensor("out_0_dram", (1, SEQ, D), _mybir.dt.float32, kind="ExternalOutput").ap()
    build_program(nc, d)
    r = _run(nc, [arrays], core_ids=[0])
    return r.results[0]["out_0_dram"]
```
